# Optimizing a Trainium2 kernel written in Bass

```python
import jax, jax.numpy as jnp
from jax import lax
import numpy as np
import jax
import jax.numpy as jnp

D_MODEL = 1024
BATCH = 1
SEQ = 256
DEPTH = 2

MLA_HEADS = 8
QK_NOPE = 64
QK_ROPE = 32
V_HEAD = 64
Q_LORA = 256
KV_LORA = 256
ROPE_THETA = 10000.0
ATTN_BLOCK = 128
SC_GROUPS = 8
SC_WIDTH = 512
SC_K = 3
CF_GROUPS = 8
CF_WIDTH = 512
CF_K = 31
GM_GROUPS = 4
GM_WIDTH = 512
GM_CHUNK = 128
N_BRANCH = 4
FFN_HIDDEN = -(-8 * D_MODEL // (3 * 256)) * 256
N_IN = Q_LORA + KV_LORA + QK_ROPE + 3 * SC_WIDTH + 2 * CF_WIDTH + 2 * GM_WIDTH + N_BRANCH * D_MODEL
EPS = 1e-6


def rms_norm(x, g):
    x32 = x.astype(jnp.float32)
    y = x32 * lax.rsqrt(jnp.mean(x32 * x32, axis=-1, keepdims=True) + EPS)
    return (y * g.astype(jnp.float32)).astype(x.dtype)

def layer_norm(x, g, b):
    x32 = x.astype(jnp.float32)
    mu = jnp.mean(x32, axis=-1, keepdims=True)
    xc = x32 - mu
    var = jnp.mean(xc * xc, axis=-1, keepdims=True)
    y = xc * lax.rsqrt(var + EPS) * g.astype(jnp.float32) + b.astype(jnp.float32)
    return y.astype(x.dtype)

def apply_rope(t, cos, sin):
    cos = cos.astype(t.dtype)
    sin = sin.astype(t.dtype)
    t1, t2 = jnp.split(t, 2, axis=-1)
    return jnp.concatenate([t1 * cos - t2 * sin, t2 * cos + t1 * sin], axis=-1)

def split_points():
    sizes = [Q_LORA, KV_LORA, QK_ROPE, SC_WIDTH, SC_WIDTH, SC_WIDTH,
             CF_WIDTH, CF_WIDTH, GM_WIDTH, GM_WIDTH]
    pts, acc = [], 0
    for s in sizes:
        acc += s
        pts.append(acc)
    return pts

def mla_branch(c_q, c_kv, k_rope, cos, sin, q_norm, w_uq, kv_norm, w_ukv):
    B, S, _ = c_q.shape
    q = (rms_norm(c_q, q_norm) @ w_uq).reshape(B, S, MLA_HEADS, QK_NOPE + QK_ROPE)
    q_nope = q[..., :QK_NOPE]
    q_rope = apply_rope(q[..., QK_NOPE:], cos[:, :, None, :], sin[:, :, None, :])
    kv = (rms_norm(c_kv, kv_norm) @ w_ukv).reshape(B, S, MLA_HEADS, QK_NOPE + V_HEAD)
    k_nope = kv[..., :QK_NOPE]
    v = kv[..., QK_NOPE:]
    k_rope = apply_rope(k_rope, cos, sin)
    scale = (QK_NOPE + QK_ROPE) ** -0.5
    nb = S // ATTN_BLOCK

    def blocks(t):
        return jnp.moveaxis(t.reshape(B, nb, ATTN_BLOCK, *t.shape[2:]), 1, 0)

    def attend(qs):
        qn, qr = qs
        s = (jnp.einsum('bqhd,bkhd->bhqk', qn, k_nope)
             + jnp.einsum('bqhr,bkr->bhqk', qr, k_rope))
        p = jax.nn.softmax(s.astype(jnp.float32) * scale, axis=-1).astype(v.dtype)
        return jnp.einsum('bhqk,bkhd->bqhd', p, v)

    o = lax.map(attend, (blocks(q_nope), blocks(q_rope)))
    return jnp.moveaxis(o, 0, 1).reshape(B, S, MLA_HEADS * V_HEAD)

def short_conv_branch(b_gate, c_gate, x_in, w):
    S = x_in.shape[1]
    z = c_gate * x_in
    pad = SC_K // 2
    zp = jnp.pad(z, ((0, 0), (pad, pad), (0, 0)))
    w = w.astype(z.dtype)
    y = zp[:, 0:S] * w[0]
    for k in range(1, SC_K):
        y = y + zp[:, k:k + S] * w[k]
    return b_gate * y

def conformer_branch(a, gate, conv_w, conv_b, ln_g, ln_b):
    z = a * jax.nn.sigmoid(gate)
    y = lax.conv_general_dilated(
        z, conv_w[:, None, :].astype(z.dtype), window_strides=(1,),
        padding=[(CF_K // 2, CF_K // 2)], dimension_numbers=('NWC', 'WIO', 'NWC'),
        feature_group_count=CF_WIDTH) + conv_b
    return jax.nn.silu(layer_norm(y, ln_g, ln_b))

def gmlp_branch(u, v, ln_g, ln_b, ws, bs):
    B, S, _ = u.shape
    nc = S // GM_CHUNK
    v = layer_norm(v, ln_g, ln_b).reshape(B, nc, GM_CHUNK, GM_GROUPS, GM_WIDTH // GM_GROUPS)
    mixed = jnp.einsum('gts,bnsgc->bntgc', ws, v) + bs.T[None, None, :, :, None]
    return u * mixed.reshape(B, S, GM_WIDTH)

def first_inputs(seed: int = 0) -> dict:
    key = jax.random.key(seed)
    ks = iter(jax.random.split(key, 40))

    def nrm(shape, scale):
        return jax.random.normal(next(ks), shape, jnp.float32) * scale

    def gain(shape):
        return 1.0 + nrm(shape, 0.05)

    L, D = DEPTH, D_MODEL
    x = jax.random.normal(next(ks), (BATCH, SEQ, D), jnp.float32)
    offs = jax.random.randint(next(ks), (BATCH, 1), 0, SEQ, dtype=jnp.int32)
    positions = jnp.arange(SEQ, dtype=jnp.int32)[None, :] + offs
    return {
        "x": x,
        "positions": positions,
        "norm_mix_pre": gain((L, D)),
        "w_in": nrm((L, D, N_IN), D ** -0.5),
        "mla_q_norm": gain((L, Q_LORA)),
        "w_uq": nrm((L, Q_LORA, MLA_HEADS * (QK_NOPE + QK_ROPE)), Q_LORA ** -0.5),
        "mla_kv_norm": gain((L, KV_LORA)),
        "w_ukv": nrm((L, KV_LORA, MLA_HEADS * (QK_NOPE + V_HEAD)), KV_LORA ** -0.5),
        "w_o_mla": nrm((L, MLA_HEADS * V_HEAD, D), (MLA_HEADS * V_HEAD) ** -0.5),
        "sc_conv_w": nrm((L, SC_K, SC_WIDTH), SC_K ** -0.5),
        "w_o_sc": nrm((L, SC_WIDTH, D), SC_WIDTH ** -0.5),
        "cf_conv_w": nrm((L, CF_K, CF_WIDTH), CF_K ** -0.5),
        "cf_conv_b": nrm((L, CF_WIDTH), 0.02),
        "cf_ln_g": gain((L, CF_WIDTH)),
        "cf_ln_b": nrm((L, CF_WIDTH), 0.02),
        "w_o_cf": nrm((L, CF_WIDTH, D), CF_WIDTH ** -0.5),
        "gm_ln_g": gain((L, GM_WIDTH)),
        "gm_ln_b": nrm((L, GM_WIDTH), 0.02),
        "gm_ws": nrm((L, GM_GROUPS, GM_CHUNK, GM_CHUNK), GM_CHUNK ** -0.5),
        "gm_bs": 1.0 + nrm((L, GM_GROUPS, GM_CHUNK), 0.02),
        "w_o_gm": nrm((L, GM_WIDTH, D), GM_WIDTH ** -0.5),
        "gate_b": nrm((L, N_BRANCH, D), 0.02),
        "w_out": nrm((L, D, D), D ** -0.5),
        "norm_mix_post": gain((L, D)),
        "norm_ffn_pre": gain((L, D)),
        "w_ffn_in": nrm((L, D, 2 * FFN_HIDDEN), D ** -0.5),
        "w_ffn_out": nrm((L, FFN_HIDDEN, D), FFN_HIDDEN ** -0.5),
        "norm_ffn_post": gain((L, D)),
    }

def first_block(x, positions, norm_mix_pre, w_in, mla_q_norm, w_uq, mla_kv_norm, w_ukv, w_o_mla,
              sc_conv_w, w_o_sc, cf_conv_w, cf_conv_b, cf_ln_g, cf_ln_b, w_o_cf,
              gm_ln_g, gm_ln_b, gm_ws, gm_bs, w_o_gm, gate_b, w_out, norm_mix_post,
              norm_ffn_pre, w_ffn_in, w_ffn_out, norm_ffn_post):
    B, S, D = x.shape
    inv_freq = ROPE_THETA ** (-jnp.arange(0, QK_ROPE, 2, dtype=jnp.float32) / QK_ROPE)
    ang = positions.astype(jnp.float32)[..., None] * inv_freq
    cos, sin = jnp.cos(ang), jnp.sin(ang)
    pts = split_points()

    for l in range(DEPTH):
        h = rms_norm(x, norm_mix_pre[l])
        proj = h @ w_in[l]
        (c_q, c_kv, k_rope, sc_b, sc_c, sc_x, cf_a, cf_g, gm_u, gm_v, gate_logits) = \
            jnp.split(proj, pts, axis=-1)

        y_a = mla_branch(c_q, c_kv, k_rope, cos, sin, mla_q_norm[l], w_uq[l],
                         mla_kv_norm[l], w_ukv[l]) @ w_o_mla[l]
        y_b = short_conv_branch(sc_b, sc_c, sc_x, sc_conv_w[l]) @ w_o_sc[l]
        y_c = conformer_branch(cf_a, cf_g, cf_conv_w[l], cf_conv_b[l],
                               cf_ln_g[l], cf_ln_b[l]) @ w_o_cf[l]
        y_d = gmlp_branch(jax.nn.gelu(gm_u), jax.nn.gelu(gm_v), gm_ln_g[l], gm_ln_b[l],
                          gm_ws[l], gm_bs[l]) @ w_o_gm[l]

        g = jax.nn.sigmoid(gate_logits.reshape(B, S, N_BRANCH, D) + gate_b[l])
        merged = g[:, :, 0] * y_a + g[:, :, 1] * y_b + g[:, :, 2] * y_c + g[:, :, 3] * y_d
        x = x + rms_norm(merged @ w_out[l], norm_mix_post[l])

        h2 = rms_norm(x, norm_ffn_pre[l])
        gu = h2 @ w_ffn_in[l]
        f_g, f_u = jnp.split(gu, 2, axis=-1)
        f = (jax.nn.silu(f_g) * f_u) @ w_ffn_out[l]
        x = x + rms_norm(f, norm_ffn_post[l])
    return x


CHUNK = 64
N_MEM = 256
NORM_EPS = 1e-6
NEG_INF = -1e30

RWKV_HEADS = 8
RWKV_HEAD_DIM = 64
RWKV_DIM = RWKV_HEADS * RWKV_HEAD_DIM
RWKV_DECAY_RANK = 64
RWKV_A_RANK = 64
RWKV_V_RANK = 32
RWKV_GATE_RANK = 128
RWKV_LNX_EPS = 1e-5 * RWKV_HEAD_DIM
RWKV_SIZES = (RWKV_DIM, RWKV_DIM, RWKV_DIM, RWKV_DECAY_RANK, RWKV_A_RANK, RWKV_GATE_RANK)
RWKV_COLS = sum(RWKV_SIZES)

DSA_HEADS = 8
DSA_HEAD_DIM = 64
DSA_DIM = DSA_HEADS * DSA_HEAD_DIM
IDX_HEADS = 8
IDX_DIM = 64
DSA_TOPK_MAX = 256
Q_BLOCK = 128
DSA_SIZES = (DSA_DIM, DSA_HEAD_DIM, DSA_HEAD_DIM, IDX_HEADS * IDX_DIM, IDX_DIM, IDX_HEADS)
DSA_COLS = sum(DSA_SIZES)

IN_SIZES = (RWKV_COLS, DSA_COLS, D_MODEL, D_MODEL)
N_IN_2 = sum(IN_SIZES)

MEM_HEADS = 4
MEM_HEAD_DIM = 128
MEM_DIM = MEM_HEADS * MEM_HEAD_DIM

FFN_DIM = 2816
N_EXPERTS = 8
TOP_K = 2
EXPERT_DIM = 1408
N_DENSE = (DEPTH + 1) // 2
N_MOE = DEPTH // 2


def split_cols(t, sizes):
    return jnp.split(t, np.cumsum(sizes)[:-1].tolist(), axis=-1)

def rms_norm_2(x, g):
    x32 = x.astype(jnp.float32)
    y = x32 * lax.rsqrt(jnp.mean(x32 * x32, axis=-1, keepdims=True) + NORM_EPS)
    return (y * g.astype(jnp.float32)).astype(x.dtype)

def rope_tables(positions, dim):
    inv_freq = 1.0 / (ROPE_THETA ** (jnp.arange(0, dim, 2, dtype=jnp.float32) / dim))
    ang = positions.astype(jnp.float32)[..., None] * inv_freq
    return jnp.cos(ang), jnp.sin(ang)

def apply_rope_2(x, cos, sin):
    shape = cos.shape[:2] + (1,) * (x.ndim - 3) + cos.shape[2:]
    c, s = cos.reshape(shape), sin.reshape(shape)
    x1, x2 = jnp.split(x.astype(jnp.float32), 2, axis=-1)
    return jnp.concatenate([x1 * c - x2 * s, x2 * c + x1 * s], axis=-1).astype(x.dtype)

def token_shift(t):
    return jnp.pad(t[:, :-1], ((0, 0), (1, 0), (0, 0)))

def rwkv7_scan(r, w, k, v, a, b):
    bsz, _, h, n = r.shape
    xs = tuple(jnp.moveaxis(t, 1, 0) for t in (r, w, k, v, a, b))

    def step(state, inp):
        r_t, w_t, k_t, v_t, a_t, b_t = inp
        sa = jnp.einsum('bhvk,bhk->bhv', state, a_t)
        state = (state * w_t[:, :, None, :] + sa[..., None] * b_t[:, :, None, :]
                 + v_t[..., None] * k_t[:, :, None, :])
        return state, jnp.einsum('bhvk,bhk->bhv', state, r_t)

    _, ys = lax.scan(step, jnp.zeros((bsz, h, n, n), jnp.float32), xs)
    return jnp.moveaxis(ys, 0, 1)

def rwkv7_branch(cols, v_first, mu, w0, w2, a0, a2, g2, v_mix, k_k, k_a, r_k, lnx_g, lnx_b):
    bsz, seqlen, _ = cols.shape
    cols = cols + (token_shift(cols) - cols) * mu
    r, k, v, wd, ad, gd = split_cols(cols, RWKV_SIZES)
    w_log = -jax.nn.softplus(-(w0 + jnp.tanh(wd) @ w2)) - 0.5
    a = jax.nn.sigmoid(a0 + ad @ a2)
    g = jax.nn.sigmoid(gd) @ g2
    if v_mix is None:
        v_first = v
    else:
        v0, v1, v2 = v_mix
        v = v + (v_first - v) * jax.nn.sigmoid(v0 + (v @ v1) @ v2)
    heads = lambda t: t.astype(jnp.float32).reshape(bsz, seqlen, RWKV_HEADS, RWKV_HEAD_DIM)
    kk = heads(k * k_k)
    kk = kk / jnp.maximum(jnp.sqrt(jnp.sum(kk * kk, axis=-1, keepdims=True)), 1e-12)
    k = k * (1.0 + (a - 1.0) * k_a)
    rh, kh, vh, ah = heads(r), heads(k), heads(v), heads(a)
    decay = jnp.exp(-jnp.exp(heads(w_log)))
    y = rwkv7_scan(rh, decay, kh, vh, -kk, kk * ah)
    mean = jnp.mean(y, axis=-1, keepdims=True)
    var = jnp.mean(jnp.square(y - mean), axis=-1, keepdims=True)
    y = (y - mean) * lax.rsqrt(var + RWKV_LNX_EPS)
    y = y.reshape(bsz, seqlen, RWKV_DIM) * lnx_g.astype(jnp.float32) + lnx_b.astype(jnp.float32)
    bonus = jnp.sum(rh * kh * r_k.astype(jnp.float32), axis=-1, keepdims=True) * vh
    y = y + bonus.reshape(bsz, seqlen, RWKV_DIM)
    return (y * g.astype(jnp.float32)).astype(cols.dtype), v_first

def dsa_attention(q, k, v, q_idx, k_idx, w_idx):
    length = q.shape[1]
    top_k = min(DSA_TOPK_MAX, length // 4)
    key_pos = jnp.arange(length)
    gather = jax.vmap(lambda t, i: t[i])
    k_idx32 = k_idx.astype(jnp.float32)

    def query_block(i):
        start = i * Q_BLOCK
        qb = lax.dynamic_slice_in_dim(q, start, Q_BLOCK, axis=1)
        qib = lax.dynamic_slice_in_dim(q_idx, start, Q_BLOCK, axis=1).astype(jnp.float32)
        wb = lax.dynamic_slice_in_dim(w_idx, start, Q_BLOCK, axis=1).astype(jnp.float32)
        limit = ((start + jnp.arange(Q_BLOCK)) // CHUNK + 1) * CHUNK
        admissible = key_pos[None, :] < limit[:, None]
        logits = jnp.einsum('bqhd,bsd->bqhs', qib, k_idx32) * (IDX_DIM ** -0.5)
        score = jnp.einsum('bqhs,bqh->bqs', jax.nn.relu(logits), wb) * (IDX_HEADS ** -0.5)
        score = jnp.where(admissible[None], score, NEG_INF)
        _, sel = lax.top_k(score, top_k)
        valid = sel < limit[None, :, None]
        ks, vs = gather(k, sel), gather(v, sel)
        s = jnp.einsum('bqhd,bqkd->bqhk', qb, ks).astype(jnp.float32) * (DSA_HEAD_DIM ** -0.5)
        p = jax.nn.softmax(jnp.where(valid[:, :, None, :], s, NEG_INF), axis=-1)
        return jnp.einsum('bqhk,bqkd->bqhd', p.astype(vs.dtype), vs)

    out = lax.map(query_block, jnp.arange(length // Q_BLOCK))
    return jnp.moveaxis(out, 0, 1).reshape(q.shape)

def dsa_branch(cols, cos_q, sin_q, cos_i, sin_i, q_norm, k_norm, idx_k_norm):
    bsz, seqlen, _ = cols.shape
    q, k, v, iq, ik, iw = split_cols(cols, DSA_SIZES)
    q = apply_rope_2(rms_norm_2(q.reshape(bsz, seqlen, DSA_HEADS, DSA_HEAD_DIM), q_norm), cos_q, sin_q)
    k = apply_rope_2(rms_norm_2(k, k_norm), cos_q, sin_q)
    iq = apply_rope_2(iq.reshape(bsz, seqlen, IDX_HEADS, IDX_DIM), cos_i, sin_i)
    ik = apply_rope_2(rms_norm_2(ik, idx_k_norm), cos_i, sin_i)
    return dsa_attention(q, k, v, iq, ik, iw).reshape(bsz, seqlen, DSA_DIM)

def memory_attention(h, mem_n, wq, wkv, q_norm, k_norm, wo):
    bsz, seqlen, _ = h.shape
    n_mem = mem_n.shape[1]
    q = rms_norm_2((h @ wq).reshape(bsz, seqlen, MEM_HEADS, MEM_HEAD_DIM), q_norm)
    k, v = split_cols(mem_n @ wkv, (MEM_DIM, MEM_DIM))
    k = rms_norm_2(k.reshape(bsz, n_mem, MEM_HEADS, MEM_HEAD_DIM), k_norm)
    v = v.reshape(bsz, n_mem, MEM_HEADS, MEM_HEAD_DIM)
    s = jnp.einsum('bshd,bmhd->bhsm', q, k).astype(jnp.float32) * (MEM_HEAD_DIM ** -0.5)
    p = jax.nn.softmax(s, axis=-1).astype(v.dtype)
    o = jnp.einsum('bhsm,bmhd->bshd', p, v).reshape(bsz, seqlen, MEM_DIM)
    return o @ wo

def swiglu(h, wg, wu, wd):
    return (jax.nn.silu(h @ wg) * (h @ wu)) @ wd

def moe_swiglu(h, router, bias, wg, wu, wd):
    logits = (h @ router).astype(jnp.float32) + bias.astype(jnp.float32)
    top_logit, top_idx = lax.top_k(logits, TOP_K)
    top_w = jax.nn.softmax(top_logit, axis=-1)
    gates = jnp.sum(jax.nn.one_hot(top_idx, N_EXPERTS, dtype=jnp.float32) * top_w[..., None], axis=-2)
    gates = gates.astype(h.dtype)
    out = jnp.zeros_like(h)
    for e in range(N_EXPERTS):
        out = out + gates[..., e:e + 1] * swiglu(h, wg[e], wu[e], wd[e])
    return out

def second_inputs(seed: int = 0) -> dict:
    keys = iter(jax.random.split(jax.random.key(seed), 48))
    f32 = jnp.float32

    def normal(shape, scale):
        return jax.random.normal(next(keys), shape, f32) * scale

    def gain(shape):
        return 1.0 + normal(shape, 0.02)

    x = normal((BATCH, SEQ, D_MODEL), 1.0)
    mem = normal((BATCH, N_MEM, D_MODEL), 1.0)
    offsets = jax.random.randint(next(keys), (BATCH, 1), 0, 64) * CHUNK
    positions = (offsets + jnp.arange(SEQ)[None, :]).astype(jnp.int32)
    nv = DEPTH - 1
    return {
        'x': x,
        'mem': mem,
        'positions': positions,
        'norm_mix': gain((DEPTH, D_MODEL)),
        'w_in': normal((DEPTH, D_MODEL, N_IN_2), D_MODEL ** -0.5),
        'rwkv_mu': jax.random.uniform(next(keys), (DEPTH, RWKV_COLS), f32, 0.0, 1.0),
        'rwkv_w0': jax.random.uniform(next(keys), (DEPTH, RWKV_DIM), f32, -6.0, -1.0),
        'rwkv_w2': normal((DEPTH, RWKV_DECAY_RANK, RWKV_DIM), 0.5 * RWKV_DECAY_RANK ** -0.5),
        'rwkv_a0': normal((DEPTH, RWKV_DIM), 0.1),
        'rwkv_a2': normal((DEPTH, RWKV_A_RANK, RWKV_DIM), RWKV_A_RANK ** -0.5),
        'rwkv_g2': normal((DEPTH, RWKV_GATE_RANK, RWKV_DIM), RWKV_GATE_RANK ** -0.5),
        'rwkv_v0': normal((nv, RWKV_DIM), 0.5),
        'rwkv_v1': normal((nv, RWKV_DIM, RWKV_V_RANK), RWKV_DIM ** -0.5),
        'rwkv_v2': normal((nv, RWKV_V_RANK, RWKV_DIM), RWKV_V_RANK ** -0.5),
        'rwkv_kk': 0.85 + normal((DEPTH, RWKV_DIM), 0.02),
        'rwkv_ka': gain((DEPTH, RWKV_DIM)),
        'rwkv_rk': normal((DEPTH, RWKV_HEADS, RWKV_HEAD_DIM), 0.1),
        'rwkv_lnx_g': gain((DEPTH, RWKV_DIM)),
        'rwkv_lnx_b': normal((DEPTH, RWKV_DIM), 0.02),
        'dsa_q_norm': gain((DEPTH, DSA_HEAD_DIM)),
        'dsa_k_norm': gain((DEPTH, DSA_HEAD_DIM)),
        'idx_k_norm': gain((DEPTH, IDX_DIM)),
        'w_branch_a': normal((DEPTH, RWKV_DIM, D_MODEL), RWKV_DIM ** -0.5),
        'w_branch_b': normal((DEPTH, DSA_DIM, D_MODEL), DSA_DIM ** -0.5),
        'w_out': normal((DEPTH, D_MODEL, D_MODEL), 0.5 * D_MODEL ** -0.5),
        'norm_mem': gain((DEPTH, D_MODEL)),
        'mem_tok_norm': gain((DEPTH, D_MODEL)),
        'mem_wq': normal((DEPTH, D_MODEL, MEM_DIM), D_MODEL ** -0.5),
        'mem_wkv': normal((DEPTH, D_MODEL, 2 * MEM_DIM), D_MODEL ** -0.5),
        'mem_q_norm': gain((DEPTH, MEM_HEAD_DIM)),
        'mem_k_norm': gain((DEPTH, MEM_HEAD_DIM)),
        'mem_wo': normal((DEPTH, MEM_DIM, D_MODEL), 0.5 * MEM_DIM ** -0.5),
        'norm_ffn': gain((DEPTH, D_MODEL)),
        'ffn_wg': normal((N_DENSE, D_MODEL, FFN_DIM), D_MODEL ** -0.5),
        'ffn_wu': normal((N_DENSE, D_MODEL, FFN_DIM), D_MODEL ** -0.5),
        'ffn_wd': normal((N_DENSE, FFN_DIM, D_MODEL), 0.5 * FFN_DIM ** -0.5),
        'moe_router': normal((N_MOE, D_MODEL, N_EXPERTS), D_MODEL ** -0.5),
        'moe_bias': normal((N_MOE, N_EXPERTS), 0.01),
        'moe_wg': normal((N_MOE, N_EXPERTS, D_MODEL, EXPERT_DIM), D_MODEL ** -0.5),
        'moe_wu': normal((N_MOE, N_EXPERTS, D_MODEL, EXPERT_DIM), D_MODEL ** -0.5),
        'moe_wd': normal((N_MOE, N_EXPERTS, EXPERT_DIM, D_MODEL), 0.5 * EXPERT_DIM ** -0.5),
    }

def second_block(x, mem, positions, norm_mix, w_in, rwkv_mu, rwkv_w0, rwkv_w2, rwkv_a0, rwkv_a2,
              rwkv_g2, rwkv_v0, rwkv_v1, rwkv_v2, rwkv_kk, rwkv_ka, rwkv_rk, rwkv_lnx_g, rwkv_lnx_b,
              dsa_q_norm, dsa_k_norm, idx_k_norm, w_branch_a, w_branch_b, w_out, norm_mem,
              mem_tok_norm, mem_wq, mem_wkv, mem_q_norm, mem_k_norm, mem_wo, norm_ffn, ffn_wg,
              ffn_wu, ffn_wd, moe_router, moe_bias, moe_wg, moe_wu, moe_wd):
    cos_q, sin_q = rope_tables(positions, DSA_HEAD_DIM)
    cos_i, sin_i = rope_tables(positions, IDX_DIM)
    v_first = None
    for l in range(DEPTH):
        h = rms_norm_2(x, norm_mix[l])
        cols_a, cols_b, gate_a, gate_b = split_cols(h @ w_in[l], IN_SIZES)
        v_mix = None if l == 0 else (rwkv_v0[l - 1], rwkv_v1[l - 1], rwkv_v2[l - 1])
        y_a, v_first = rwkv7_branch(cols_a, v_first, rwkv_mu[l], rwkv_w0[l], rwkv_w2[l], rwkv_a0[l],
                                    rwkv_a2[l], rwkv_g2[l], v_mix, rwkv_kk[l], rwkv_ka[l], rwkv_rk[l],
                                    rwkv_lnx_g[l], rwkv_lnx_b[l])
        y_b = dsa_branch(cols_b, cos_q, sin_q, cos_i, sin_i, dsa_q_norm[l], dsa_k_norm[l], idx_k_norm[l])
        merged = (jax.nn.sigmoid(gate_a) * (y_a @ w_branch_a[l])
                  + jax.nn.sigmoid(gate_b) * (y_b @ w_branch_b[l]))
        x = x + merged @ w_out[l]
        x = x + memory_attention(rms_norm_2(x, norm_mem[l]), rms_norm_2(mem, mem_tok_norm[l]), mem_wq[l],
                                 mem_wkv[l], mem_q_norm[l], mem_k_norm[l], mem_wo[l])
        h = rms_norm_2(x, norm_ffn[l])
        j = l // 2
        if l % 2 == 0:
            x = x + swiglu(h, ffn_wg[j], ffn_wu[j], ffn_wd[j])
        else:
            x = x + moe_swiglu(h, moe_router[j], moe_bias[j], moe_wg[j], moe_wu[j], moe_wd[j])
    return x


def setup_inputs(seed=0):
    out = dict(first_inputs(seed))
    for name, value in second_inputs(seed + 1).items():
        if name != "x":
            out[name + "_2"] = value
    return out


def reference(
    x, positions, norm_mix_pre, w_in, mla_q_norm, w_uq, mla_kv_norm, w_ukv, w_o_mla, sc_conv_w,
    w_o_sc, cf_conv_w, cf_conv_b, cf_ln_g, cf_ln_b, w_o_cf, gm_ln_g, gm_ln_b, gm_ws, gm_bs,
    w_o_gm, gate_b, w_out, norm_mix_post, norm_ffn_pre, w_ffn_in, w_ffn_out, norm_ffn_post,
    mem_2, positions_2, norm_mix_2, w_in_2, rwkv_mu_2, rwkv_w0_2, rwkv_w2_2, rwkv_a0_2,
    rwkv_a2_2, rwkv_g2_2, rwkv_v0_2, rwkv_v1_2, rwkv_v2_2, rwkv_kk_2, rwkv_ka_2, rwkv_rk_2,
    rwkv_lnx_g_2, rwkv_lnx_b_2, dsa_q_norm_2, dsa_k_norm_2, idx_k_norm_2, w_branch_a_2,
    w_branch_b_2, w_out_2, norm_mem_2, mem_tok_norm_2, mem_wq_2, mem_wkv_2, mem_q_norm_2,
    mem_k_norm_2, mem_wo_2, norm_ffn_2, ffn_wg_2, ffn_wu_2, ffn_wd_2, moe_router_2, moe_bias_2,
    moe_wg_2, moe_wu_2, moe_wd_2,
):
    x = first_block(
        x, positions, norm_mix_pre, w_in, mla_q_norm, w_uq, mla_kv_norm, w_ukv, w_o_mla,
        sc_conv_w, w_o_sc, cf_conv_w, cf_conv_b, cf_ln_g, cf_ln_b, w_o_cf, gm_ln_g, gm_ln_b,
        gm_ws, gm_bs, w_o_gm, gate_b, w_out, norm_mix_post, norm_ffn_pre, w_ffn_in, w_ffn_out,
        norm_ffn_post,
    )
    return second_block(
        x, mem_2, positions_2, norm_mix_2, w_in_2, rwkv_mu_2, rwkv_w0_2, rwkv_w2_2, rwkv_a0_2,
        rwkv_a2_2, rwkv_g2_2, rwkv_v0_2, rwkv_v1_2, rwkv_v2_2, rwkv_kk_2, rwkv_ka_2, rwkv_rk_2,
        rwkv_lnx_g_2, rwkv_lnx_b_2, dsa_q_norm_2, dsa_k_norm_2, idx_k_norm_2, w_branch_a_2,
        w_branch_b_2, w_out_2, norm_mem_2, mem_tok_norm_2, mem_wq_2, mem_wkv_2, mem_q_norm_2,
        mem_k_norm_2, mem_wo_2, norm_ffn_2, ffn_wg_2, ffn_wu_2, ffn_wd_2, moe_router_2,
        moe_bias_2, moe_wg_2, moe_wu_2, moe_wd_2,
    )


_drawn_inputs = setup_inputs


def setup_inputs(seed=0):
    import zlib

    import numpy as np

    out = dict(_drawn_inputs(seed))
    spreads = {}
    factors = {'mla_q_norm': 7.928,
     'mla_kv_norm': 5.704,
     'cf_conv_b': 2.674,
     'cf_ln_b': 4.345,
     'gm_ln_b': 3.812,
     'gm_bs': 5.0,
     'gate_b': 4.464,
     'norm_mix_2': 5.937,
     'rwkv_w2_2': 25.582,
     'rwkv_a0_2': 8.0,
     'rwkv_v0_2': 3.642,
     'rwkv_kk_2': 64.0,
     'rwkv_ka_2': 8.0,
     'rwkv_lnx_g_2': 64.0,
     'rwkv_lnx_b_2': 64.0,
     'dsa_q_norm_2': 55.007,
     'dsa_k_norm_2': 58.519,
     'idx_k_norm_2': 50.946,
     'norm_mem_2': 34.821,
     'mem_tok_norm_2': 31.7,
     'mem_q_norm_2': 33.262,
     'mem_k_norm_2': 33.202,
     'norm_ffn_2': 37.293,
     'moe_bias_2': 58.528,
     'rwkv_w0_2': 3.644}
    for name, (base, spread) in spreads.items():
        noise = np.random.default_rng([zlib.crc32(name.encode()), seed]).standard_normal(out[name].shape)
        drawn = base * np.exp(spread * noise) if base else spread * noise
        out[name] = jnp.asarray(drawn.astype(out[name].dtype))
    for name, factor in factors.items():
        out[name] = (out[name] * factor).astype(out[name].dtype)
    return out
```

```python
import numpy as np
from contextlib import ExitStack
import concourse.bass as bass
from concourse import mybir

S = 256
F32 = mybir.dt.float32
I32 = mybir.dt.int32
U32 = mybir.dt.uint32
ALU = mybir.AluOpType
ACT = mybir.ActivationFunctionType
AXX = mybir.AxisListType.X

VECS1 = [("nmp", "norm_mix_pre", 8), ("qn", "mla_q_norm", 2), ("kvn", "mla_kv_norm", 2), ("scw", "sc_conv_w", 12),
         ("cfw", "cf_conv_w", 124), ("cfb", "cf_conv_b", 4), ("clg", "cf_ln_g", 4), ("clb", "cf_ln_b", 4),
         ("gb", "gate_b", 32), ("npo", "norm_mix_post", 8), ("nfp", "norm_ffn_pre", 8), ("nfo", "norm_ffn_post", 8)]
VECS2 = [("nmix", "norm_mix_2", 8), ("mu", "rwkv_mu_2", 15), ("w0", "rwkv_w0_2", 4), ("a0", "rwkv_a0_2", 4),
         ("kk", "rwkv_kk_2", 4), ("ka", "rwkv_ka_2", 4), ("rk", "rwkv_rk_2", 4), ("lxg", "rwkv_lnx_g_2", 4),
         ("lxb", "rwkv_lnx_b_2", 4), ("dq", "dsa_q_norm_2", 1), ("dk", "dsa_k_norm_2", 1), ("di", "idx_k_norm_2", 1),
         ("nmem", "norm_mem_2", 8), ("mtok", "mem_tok_norm_2", 8), ("mq", "mem_q_norm_2", 1), ("mk", "mem_k_norm_2", 1),
         ("nffn", "norm_ffn_2", 8), ("v0", "rwkv_v0_2", 4)]
NVEC = 2 * (sum(n for _, _, n in VECS1) + sum(n for _, _, n in VECS2))
NCST = 10 * 128 + 512 + 256 + 64 + 8 + 4


def vec_offsets():
    off, at = {}, 0
    for l in range(2):
        for key, _, n in VECS1 + VECS2:
            off[key, l] = at
            at += n
    return off


def build_program(nc, ins, out):
    ctx = ExitStack()
    with ctx:
        build(nc, ctx, ins, out)


class Prog:

    def __init__(self, nc, ctx):
        self.nc, self.ctx = nc, ctx
        self.q = {e: [] for e in ("pe", "act", "dve", "pool", "sp")}
        self.n = {e: 0 for e in ("pe", "act", "dve", "pool")}
        self.sem = {e: ctx.enter_context(nc.semaphore("s_" + e)) for e in self.n}
        self.dn = {}
        self.bar = {e: [] for e in self.q}

    def put(self, eng, fn, *after):
        self.q[eng].append((self.bar[eng] + flat(after), fn, self.sem[eng], 1))
        self.bar[eng] = []
        self.n[eng] += 1
        return (eng, self.n[eng])

    def dma(self, slot, dst, src, *after, eng="sp"):
        key = "d_" + slot
        if key not in self.sem:
            self.sem[key] = self.ctx.enter_context(self.nc.semaphore(key))
            self.dn[key] = 0
        self.q[eng].append((flat(after), lambda e: e.dma_start(dst, src), self.sem[key], 16))
        self.dn[key] += 16
        return (key, self.dn[key])

    def now(self):
        return [(e, n) for e, n in self.n.items() if n]

    def barrier(self):
        for e in self.n:
            self.bar[e] = self.now()

    def replay(self, eng, e):
        seen = {}
        for after, fn, sem, inc in self.q[eng]:
            for key, val in after:
                if seen.get(key, 0) < val:
                    e.wait_ge(self.sem[key], val)
                    seen[key] = val
            fn(e).then_inc(sem, inc)


def flat(ts):
    r = []
    for t in ts:
        if t is None:
            continue
        if isinstance(t, list):
            r += flat(t)
        else:
            r.append(t)
    return r


class Ring:

    def __init__(self, bufs):
        self.bufs, self.free, self.i = bufs, [None] * len(bufs), 0

    def take(self):
        n = len(self.bufs)
        i = next((j % n for j in range(self.i, self.i + n) if self.free[j % n] != "taken"), None)
        assert i is not None, "ring overrun"
        self.i = (i + 1) % n
        tok, self.free[i] = self.free[i], "taken"
        return i, self.bufs[i], tok

    def give(self, i, *tok):
        self.free[i] = flat(tok)


def build(nc, ctx, ins, out):
    P = Prog(nc, ctx)
    VO = vec_offsets()

    def sb(name, n, dt=F32):
        return ctx.enter_context(nc.sbuf_tensor(name, [128, n], dt))

    def tt(eng, o, a, b, op, *dep):
        return P.put(eng, lambda e: e.tensor_tensor(o, a, b, op), *dep)

    def ts(eng, o, a, s1, s2, op0, op1, *dep):
        if s2 is None:
            return P.put(eng, lambda e: e.tensor_scalar(o, a, s1, None, op0), *dep)
        return P.put(eng, lambda e: e.tensor_scalar(o, a, s1, s2, op0, op1), *dep)

    def stt(eng, o, a, s, b, op0, op1, *dep):
        return P.put(eng, lambda e: e.scalar_tensor_tensor(out=o, in0=a, scalar=s, in1=b, op0=op0, op1=op1), *dep)

    def cp(eng, o, a, *dep):
        if eng == "act":
            return P.put("act", lambda e: e.activation(o, a, ACT.Copy), *dep)
        return P.put(eng, lambda e: e.tensor_copy(o, a), *dep)

    def act(o, a, f, *dep, bias=None, scale=1.0, acc=None):
        kw = {}
        if bias is not None:
            kw["bias"] = bias
        if acc is not None:
            kw["accum_out"] = acc
        return P.put("act", lambda e: e.activation(o, a, f, scale=scale, **kw), *dep)

    def mms(items, *dep):
        def fn(e):
            for o, l, r, st, sp in items:
                if r is None:
                    last = e.transpose(o, l, IDENT[0:l.shape[0], 0:l.shape[0]])
                else:
                    last = e.matmul(o, l, r, start=st, stop=sp)
            return last
        return P.put("pe", fn, *dep)

    MUL, ADD, SUB, MAX, MIN = ALU.mult, ALU.add, ALU.subtract, ALU.max, ALU.min

    SLOT, NSLOT = 2048, 7
    Wring = Ring([sb(f"wr{i}", SLOT) for i in range(NSLOT)])
    X = sb("X", 2048)
    H = sb("H", 2048)
    VEC = sb("VEC", NVEC)
    CST = sb("CST", NCST)
    SW = sb("SW", 2304)
    MISC = sb("MISC", 3072)
    GR, WS, WKR = MISC[:, 0:1536], MISC[:, 1536:2048], MISC[:, 2048:2816]
    VF = sb("VF", 1024)
    S8 = sb("S8", 32)
    ROPE = sb("ROPE", 1024)
    SC = sb("SC", 8 * 512)
    ST = sb("ST", 64)
    RS = sb("RS", 3 * 512)
    BIG = sb("BIG", 22528)
    PS = [ctx.enter_context(nc.psum_tensor(f"ps{i}", [128, 512], F32)) for i in range(8)]
    Gb = Ring(PS[0:4])
    Ab = Ring(PS[4:8])
    Scr = Ring([SC[:, i * 512:(i + 1) * 512] for i in range(8)])
    Stat = Ring([ST[:, i * 4:(i + 1) * 4] for i in range(16)])

    def cst(i, n=128):
        return CST[:, i:i + n]

    IDENT, ONES, BONES = cst(0), cst(128), cst(256)
    ROT96, ROT64 = cst(384), cst(512)
    D16, D16T, C16, C32, CST64 = cst(640), cst(768), cst(896), cst(1024), cst(1152)
    MASKT = cst(1280, 512)
    SCM = cst(1792, 256)
    ID64 = cst(2048, 64)
    IOTA8 = cst(2112, 8)
    IF1, IF2 = cst(2120, 1), cst(2121, 1)

    x3 = X[:, :].rearrange("p (t s) -> p t s", s=S)
    h3 = H[:, :].rearrange("p (t s) -> p t s", s=S)

    def vec(key, l, i=0, n=1):
        o = VO[key, l] + i
        return VEC[:, o:o + n]

    def big(off, *shape):
        n = int(np.prod(shape))
        assert off + n <= 22528, (off, shape)
        v = BIG[:, off:off + n]
        if len(shape) == 1:
            return v
        if len(shape) == 2:
            return v.rearrange("p (a b) -> p a b", b=shape[1])
        if len(shape) == 3:
            return v.rearrange("p (a b c) -> p a b c", b=shape[1], c=shape[2])
        return v.rearrange("p (a b c d) -> p a b c d", b=shape[1], c=shape[2], d=shape[3])

    def bc(ap, n):
        return ap.unsqueeze(1).broadcast_to([ap.shape[0], n, ap.shape[-1]])

    t_vec = P.dma("vec", VEC[:, :], ins["vecs"])
    t_cst = P.dma("cst", CST[:, :], ins["cst"])
    t_x = P.dma("x", X[:, :], ins["xT"])
    t_c = [t_vec, t_cst]

    def load(W, k0, k1, c0, c1):
        nk, w = k1 - k0, c1 - c0
        assert nk * w <= SLOT
        i, buf, free = Wring.take()
        v = buf[:, 0:nk * w].rearrange("p (k n) -> p k n", n=w)
        src = W[k0 * 128:k1 * 128, c0:c1].rearrange("(k p) n -> p k n", p=128)
        tok = P.dma(f"w{i}", v, src, free)
        return i, v, tok

    def gemm(jobs, kt, rhs, dep, consume, ring=None):
        ring = ring or Gb
        n = 0
        for specs, banks in jobs:
            parts = []
            for W, c0, c1 in specs:
                m = -(-kt * (c1 - c0) // SLOT)
                cut = [round(kt * i / m) for i in range(m + 1)]
                parts.append([(a, b, load(W, a, b, c0, c1)) for a, b in zip(cut, cut[1:])])
            arrived = [x[2][2] for p in parts for x in p]
            for bank in banks:
                bi, ps, free = ring.take()
                items = []
                for t, (s, col, w) in enumerate(bank):
                    for a, b, (_, v, _) in parts[s]:
                        for k in range(a, b):
                            items.append((ps[0:w, t * S:(t + 1) * S], v[:, k - a, col:col + w], rhs(k), k == 0, k == kt - 1))
                tok = mms(items, arrived, dep, free)
                ring.give(bi, consume(n, ps, tok))
                n += 1
                yield
            for p in parts:
                for _, _, (i, _, _) in p:
                    Wring.give(i, tok)

    def pairs(W, c0, n, wide=256):
        jobs = []
        for a in range(0, n, wide):
            b = min(n, a + wide)
            tiles = [(0, c, min(128, b - a - c)) for c in range(0, b - a, 128)]
            jobs.append(([(W, c0 + a, c0 + b)], [tiles[i:i + 2] for i in range(0, len(tiles), 2)]))
        return jobs

    rs_last = [None]

    def rsqrt(dst, src, scale, eps, dep, w=256, final=1.0, floor=None):
        pp = src.shape[0]
        v, t = RS[0:pp, 0:w], RS[0:pp, 512:512 + w]
        y = RS[0:pp, 1024:1024 + w]
        if floor is None:
            k = ts("dve", v, src, float(scale), float(eps), MUL, ADD, dep, rs_last[0])
        else:
            k = ts("dve", v, src, float(floor), None, MAX, None, dep, rs_last[0])
        k = ts("dve", y.bitcast(I32), v.bitcast(I32), -0.5, float(0x5f3759df), MUL, ADD, k)
        for c in (3.0, 12.0):
            k = tt("dve", t, y, y, MUL, k)
            k = tt("dve", t, t, v, MUL, k)
            k = stt("dve", y, t, c, y, SUB, MUL, k)
        k = tt("dve", t, y, y, MUL, k)
        k = tt("dve", t, t, v, MUL, k)
        k = ts("dve", t, t, float(-final / 8192.0), float(final * 0.09375), MUL, ADD, k)
        k = tt("dve", dst, t, y, MUL, k)
        rs_last[0] = k
        return k

    def sumsq(src, nt, lhsT, dep, rows=128, own=False):
        bi, ps, free = Ab.take()
        toks = []
        for t0 in range(0, nt, 2):
            m = min(2, nt - t0)
            si, sq, sfree = Scr.take()
            sqv = sq[0:rows, 0:m * S].rearrange("p (t s) -> p t s", s=S)
            a = act(sqv, src[0:rows, t0:t0 + m, :], ACT.Square, dep, sfree)
            k = mms([(ps[0:rows, 0:S], lhsT[0:rows, 0:rows], sqv[:, u, :], t0 + u == 0, t0 + u == nt - 1) for u in range(m)],
                    a, free, t_c)
            Scr.give(si, k)
        return bi, ps, k

    def rmsnorm(src, nt, gkey, l, dst, dep, fac=1.0):
        bi, ps, k = sumsq(src, nt, ONES, dep)
        si, r, sfree = Scr.take()
        k = rsqrt(r[:, 0:S], ps[:, 0:S], 1.0 / (128 * nt), 1e-6, [k, sfree])
        Ab.give(bi, k)
        toks = []
        for t in range(nt):
            toks.append(stt("dve", dst[:, t, :], src[:, t, :], vec(gkey, l, t), r[:, 0:S], MUL, MUL, k, dep, t_c))
        Scr.give(si, toks)
        return toks

    def residual_rms(m, gkey, l, dep, fac):
        bi, ps, k = sumsq(m, 8, ONES, dep)
        si, r, sfree = Scr.take()
        k = rsqrt(r[:, 0:S], ps[:, 0:S], fac * fac / 1024, 1e-6, [k, sfree], final=fac)
        Ab.give(bi, k)
        toks = []
        for t in range(8):
            a = stt("dve", m[:, t, :], m[:, t, :], vec(gkey, l, t), r[:, 0:S], MUL, MUL, k, dep)
            toks.append(tt("pool", x3[:, t, :], x3[:, t, :], m[:, t, :], ADD, a))
        Scr.give(si, toks)
        return toks

    def sigmoid_in(o, a, *dep, bias=None, eng="dve"):
        k = act(o, a, ACT.Tanh, *dep, bias=bias, scale=0.5)
        return ts(eng, o, o, 0.5, 0.5, MUL, ADD, k), k

    def attention(nh, q, kk, scale, v, dst, dv, dep, nks=(256, 256), pen=None, K=128, base=lambda h: 0, done=None):
        kept = {}
        for h in range(nh + 1):
            if h < nh:
                bi, ps, free = Ab.take()
                s3 = ps[:, :].rearrange("p (b s) -> p b s", s=S)
                t = mms([(s3[:, b, 0:nks[b]], q(h)[:, b * 128:(b + 1) * 128], kk(h)[:, 0:nks[b]], True, True) for b in range(2)],
                        dep, free)
                si, pr, sfree = Scr.take()
                p3 = pr.rearrange("p (b s) -> p b s", s=S)
                ti, st, tfree = Stat.take()
                ui, su, ufree = Stat.take()
                if pen is None:
                    m = P.put("dve", lambda e, o=st[:, 0:2], i=s3: e.reduce_max(o, i, AXX), t, tfree)
                    m = ts("dve", st[:, 2:4], st[:, 0:2], -float(scale), None, MUL, None, m)
                    ex = []
                    for b in range(2):
                        ex.append(act(p3[:, b, :], s3[:, b, :], ACT.Exp, m, sfree, ufree, bias=st[:, 2 + b:3 + b], scale=float(scale),
                                      acc=su[:, b:b + 1]))
                    Ab.give(bi, ex)
                else:
                    ms = [stt("dve", p3[:, b, 0:nks[b]], s3[:, b, 0:nks[b]], float(scale), pen(b), MUL, ADD, t, sfree, dep)
                          for b in range(2)]
                    Ab.give(bi, ms)
                    m = [P.put("dve", lambda e, o=st[:, b:b + 1], i=p3[:, b, 0:nks[b]]: e.reduce_max(o, i, AXX), ms[b], tfree)
                         for b in range(2)]
                    m = ts("dve", st[:, 2:4], st[:, 0:2], -1.0, None, MUL, None, m)
                    ex = []
                    for b in range(2):
                        ex.append(act(p3[:, b, 0:nks[b]], p3[:, b, 0:nks[b]], ACT.Exp, m, ufree, bias=st[:, 2 + b:3 + b],
                                      acc=su[:, b:b + 1]))
                rc = P.put("dve", lambda e, o=su[:, 2:4], i=su[:, 0:2]: e.reciprocal(o, i), ex)
                sc = [ts("dve", p3[:, b, 0:nks[b]], p3[:, b, 0:nks[b]], su[:, 2 + b:3 + b], None, MUL, None, rc) for b in range(2)]
                Stat.give(ti, ex)
                Stat.give(ui, sc)
                kept[h] = (si, p3, sc)
                yield
            if h > 0:
                g = h - 1
                si, p3, sc = kept.pop(g)
                bi, ps, free = Ab.take()
                tp = ps[:, :].rearrange("p (k s) -> p k s", s=S)
                todo = [(tp[:, kt, b * 128:(b + 1) * 128], p3[:, b, kt * 128:(kt + 1) * 128], None, True, True)
                        for b in range(2) for kt in range(nks[b] // 128)]
                t = mms(todo, sc, free, t_c)
                Scr.give(si, t)
                pi, pt, pfree = Scr.take()
                pt3 = pt.rearrange("p (k s) -> p k s", s=S)
                if nks[0] == 256:
                    c = [cp("act", pt, ps[:, :], t, pfree)]
                else:
                    c = [cp("act", pt3[:, 0, :], tp[:, 0, :], t, pfree), cp("act", pt3[:, 1, 128:256], tp[:, 1, 128:256], t, pfree)]
                Ab.give(bi, c)
                bi, ps, free = Ab.take()
                items = []
                if nks[0] == 256:
                    items = [(ps[0:dv, 0:S], v(g, kt), pt3[:, kt, :], kt == 0, kt == 1) for kt in range(2)]
                else:
                    items = [(ps[0:dv, 0:128], v(g, 0), pt3[:, 0, 0:128], True, True),
                             (ps[0:dv, 128:256], v(g, 0), pt3[:, 0, 128:256], True, False),
                             (ps[0:dv, 128:256], v(g, 1), pt3[:, 1, 128:256], False, True)]
                t = mms(items, c, free, dep)
                Scr.give(pi, t)
                c = cp("dve", dst(g), ps[0:dv, 0:S], t)
                Ab.give(bi, c)
                done.append(c)
                yield

    def run(g):
        for _ in g:
            pass

    def interleave(gens, weights):
        gens = [[g, w, 0.0] for g, w in zip(gens, weights)]
        while gens:
            gens.sort(key=lambda a: a[2])
            a = gens[0]
            try:
                next(a[0])
                a[2] += a[1]
            except StopIteration:
                gens.pop(0)

    TWO_PI = 2 * np.pi
    C1 = 6.28125
    C2 = float(np.float32(np.round((TWO_PI - C1) * 2**20) / 2**20))
    C3 = float(TWO_PI - C1 - C2)
    MAGIC = 12582912.0

    def rope_tables(off, pos, freq):
        si, sc, _ = Scr.take()
        pi = sc[:, 0:S].bitcast(I32)
        t = P.dma("pos%d" % off, pi, pos.partition_broadcast(128))
        ang, kx = sc[:, 256:512], RS[:, 0:S]
        a = ts("dve", ang, pi, freq, None, MUL, None, t, t_c, rs_last[0])
        for j, (shift, add) in enumerate(((0.25, np.pi / 2), (0.0, 0.0))):
            o = ROPE[:, off + j * S:off + (j + 1) * S]
            k = ts("dve", kx, ang, float(1 / TWO_PI), float(shift), MUL, ADD, a)
            k = ts("dve", kx, kx, MAGIC, None, ADD, None, k)
            k = ts("dve", kx, kx, -MAGIC, None, ADD, None, k)
            k = stt("dve", o, kx, -C1, ang, MUL, ADD, k)
            k = stt("dve", o, kx, -C2, o, MUL, ADD, k)
            k = stt("dve", o, kx, -C3, o, MUL, ADD, k)
            a = k
            k = ts("dve", o, o, float(add), None, ADD, None, k)
            k = ts("dve", o, o, 3.1415925, -3.1415925, MIN, MAX, k)
            a = k
            k2 = act(o, o, ACT.Sin, k)
        Scr.give(si, k)
        rs_last[0] = k
        return k2

    t_rope = [rope_tables(0, ins["positions"], IF1), rope_tables(512, ins["positions_2"], IF2)]
    z_wkr = P.put("pool", lambda e: e.memset(WKR[:, :], 0.0))
    wkr3 = WKR[:, :].rearrange("p (k n) -> p k n", n=96)
    xdep = [t_x]

    use_small = [None]

    def block1_mix(l):
        P.barrier()
        w_in, w_uq, w_ukv = ins["w_in"][l], ins["w_uq"][l], ins["w_ukv"][l]
        t_kr = P.dma("wkr", wkr3[:, :, 64:96], w_in[:, 512:544].rearrange("(k p) n -> p k n", p=128), z_wkr, use_small[0])
        t_gr = [P.dma("gr0", GR[:, 0:512], ins["gm_ln_g"][l].partition_broadcast(128), use_small[0]),
                P.dma("gr1", GR[:, 512:1024], ins["gm_ln_b"][l].partition_broadcast(128), use_small[0]),
                P.dma("gr2", GR[:, 1024:1536], ins["gm_bs"][l].rearrange("g t -> (g t)").partition_broadcast(128), use_small[0])]
        t_ws = P.dma("ws", WS[:, :], ins["gm_wsT"][l], use_small[0])
        G = big(0, 32, S)
        C = big(8192, 4, S)
        QT = big(9216, 8, S)
        KT = big(11264, 8, S)
        V = big(13312, 2, 512)
        O = big(14336, 4, S)
        Bc = big(15360, 4, S)
        CA = big(16384, 4, 288)
        ZS = big(17536, 4, 258)
        CY = big(18568, 4, S)
        GU = big(19592, 4, S)
        GV = big(20616, 2, 512)
        cos1, sin1 = ROPE[:, 0:S], ROPE[:, S:2 * S]

        hd = rmsnorm(x3, 8, "nmp", l, h3, xdep)
        rhs = lambda k: h3[:, k, :]
        yield
        cdone = []

        def put_c(dst, t0):
            def f(n, ps, tok):
                c = cp("act", dst[:, t0 + 2 * n:t0 + 2 * n + 2, :], ps[:, :].rearrange("p (t s) -> p t s", s=S), tok)
                cdone.append(c)
                return c
            return f
        yield from gemm(pairs(w_in, 0, 512), 8, rhs, hd, put_c(C, 0))
        cq = rmsnorm(C[:, 0:2, :], 2, "qn", l, C[:, 0:2, :], cdone)
        ck = rmsnorm(C[:, 2:4, :], 2, "kvn", l, C[:, 2:4, :], cdone)
        bi, ps, free = Gb.take()
        t = mms([(ps[0:96, 0:S], wkr3[:, k, :], h3[:, k, :], k == 0, k == 7) for k in range(8)], hd, t_kr, z_wkr, free)
        ki, kr, kfree = Scr.take()
        a = cp("act", kr[0:96, 0:S], ps[0:96, 0:S], t, kfree)
        t = mms([(ps[0:96, S:2 * S], ROT96[0:96, 0:96], kr[0:96, 0:S], True, True)], a)
        b1 = tt("dve", kr[64:96, 0:S], kr[64:96, 0:S], cos1[64:96, :], MUL, t, t_rope)
        b2 = tt("dve", kr[64:96, S:2 * S], ps[64:96, S:2 * S], sin1[64:96, :], MUL, t)
        Gb.give(bi, b2)
        kdone = [tt("dve", KT[64:96, :, :], bc(kr[64:96, 0:S], 8), bc(kr[64:96, S:2 * S], 8), ADD, b1, b2)]
        Scr.give(ki, kdone)
        yield

        zc = P.put("pool", lambda e: e.memset(CA[:, :, :], 0.0))
        zs = P.put("pool", lambda e: e.memset(ZS[:, :, :], 0.0))
        az = []

        def put_a(n, ps, tok):
            c = cp("act", CA[:, 2 * n:2 * n + 2, 15:271], ps[:, :].rearrange("p (t s) -> p t s", s=S), tok, zc)
            az.append(c)
            return c

        def put_g(n, ps, tok):
            si, s, sf = Scr.take()
            a = act(s, ps[:, :], ACT.Tanh, tok, sf, scale=0.5)
            b = ts("dve", s, s, 0.5, 0.5, MUL, ADD, a)
            c = tt("dve", CA[:, 2 * n:2 * n + 2, 15:271], CA[:, 2 * n:2 * n + 2, 15:271], s.rearrange("p (t s) -> p t s", s=S), MUL, b, az[n])
            az[n] = c
            Scr.give(si, c)
            return a
        yield from gemm(pairs(w_in, 2080, 512), 8, rhs, hd, put_a)
        yield from gemm(pairs(w_in, 2592, 512), 8, rhs, hd, put_g)

        last = {}

        def conv():
            for t in range(4):
                last[t] = ts("dve", CY[:, t, :], CA[:, t, 0:S], vec("cfw", l, t), vec("cfb", l, t), MUL, ADD, az)
            yield
            for k in range(1, 31):
                for t in range(4):
                    last[t] = stt("dve", CY[:, t, :], CA[:, t, k:k + S], vec("cfw", l, 4 * k + t), CY[:, t, :], MUL, ADD, last[t])
                yield
            toks = list(last.values())
            bi, ps, free = Ab.take()
            m = mms([(ps[:, 0:S], ONES, CY[:, t, :], t == 0, t == 3) for t in range(4)], toks, free)
            si, s, sf = Scr.take()
            mean = ts("dve", s[:, 0:S], ps[:, 0:S], 1.0 / 512, None, MUL, None, m, sf)
            Ab.give(bi, mean)
            cen = [tt("dve", CY[:, 2 * i:2 * i + 2, :], CY[:, 2 * i:2 * i + 2, :], bc(s[:, 0:S], 2), SUB, mean, toks) for i in range(2)]
            yield
            bi, ps, k = sumsq(CY, 4, ONES, cen)
            k = rsqrt(s[:, S:2 * S], ps[:, 0:S], 1.0 / 512, 1e-6, k)
            Ab.give(bi, k)
            yield
            fin = []
            for t in range(4):
                a = tt("dve", CY[:, t, :], CY[:, t, :], s[:, S:2 * S], MUL, k)
                a = ts("dve", CY[:, t, :], CY[:, t, :], vec("clg", l, t), vec("clb", l, t), MUL, ADD, a)
                ti, th, tf = Scr.take()
                b = act(th[:, 0:S], CY[:, t, :], ACT.Tanh, a, tf, scale=0.5)
                b = stt("dve", CY[:, t, :], th[:, 0:S], 1.0, CY[:, t, :], ADD, MUL, b)
                b = ts("dve", CY[:, t, :], CY[:, t, :], 0.5, None, MUL, None, b)
                Scr.give(ti, b)
                fin.append(b)
                yield
            Scr.give(si, fin)
            last["y"] = fin

        def gelu(dst, src, w, tok, free):
            si, s, sf = Scr.take()
            a = act(s[:, 0:w], src, ACT.Square, tok, sf)
            a = ts("dve", s[:, 0:w], s[:, 0:w], 0.044715, 1.0, MUL, ADD, a)
            a = tt("dve", s[:, 0:w], s[:, 0:w], src, MUL, a)
            a = act(s[:, 0:w], s[:, 0:w], ACT.Tanh, a, scale=float(np.sqrt(2 / np.pi)))
            a = stt("dve", s[:, 0:w], s[:, 0:w], 1.0, src, ADD, MUL, a)
            b = ts("pool", dst, s[:, 0:w], 0.5, None, MUL, None, a, free)
            Scr.give(si, b)
            return a, b

        def main():
            qdone, vdone = [], []
            wi, wv, wt = load(w_uq, 0, 2, 0, 768)
            for p in range(4):
                bi, ps, free = Gb.take()
                items = [(ps[0:96, u * S:(u + 1) * S], wv[:, k, (2 * p + u) * 96:(2 * p + u + 1) * 96], C[:, k, :], k == 0, k == 1)
                         for u in range(2) for k in range(2)]
                t = mms(items, cq, wt, free)
                b2i, ps2, free2 = Ab.take()
                qv = QT[0:96, 2 * p:2 * p + 2, :]
                a = cp("act", qv, ps[0:96, :].rearrange("p (t s) -> p t s", s=S), t)
                Gb.give(bi, a)
                m = mms([(ps2[0:96, :], ROT96[0:96, 0:96], qv, True, True)], a, free2)
                si, s, sf = Scr.take()
                qr = QT[64:96, 2 * p:2 * p + 2, :]
                s3 = s[64:96, :].rearrange("p (t s) -> p t s", s=S)
                b = tt("dve", qr, qr, bc(cos1[64:96, :], 2), MUL, m)
                c = tt("dve", s3, ps2[64:96, :].rearrange("p (t s) -> p t s", s=S), bc(sin1[64:96, :], 2), MUL, m, sf)
                Ab.give(b2i, c)
                d = tt("dve", qr, qr, s3, ADD, b, c)
                Scr.give(si, d)
                qdone.append(d)
                yield
            Wring.give(wi, t)
            wi, wv, wt = load(w_ukv, 0, 2, 0, 1024)
            for p in range(4):
                bi, ps, free = Gb.take()
                items = [(ps[0:64, u * S:(u + 1) * S], wv[:, k, (2 * p + u) * 128:(2 * p + u) * 128 + 64], C[:, 2 + k, :], k == 0, k == 1)
                         for u in range(2) for k in range(2)]
                t = mms(items, ck, wt, free)
                a = cp("act", KT[0:64, 2 * p:2 * p + 2, :], ps[0:64, :].rearrange("p (t s) -> p t s", s=S), t)
                Gb.give(bi, a)
                kdone.append(a)
                yield
            wvv = wv.rearrange("p k (h n) -> p k h n", n=128)
            for tb in range(2):
                bi, ps, free = Gb.take()
                t = mms([(ps[:, :], C[:, 2 + k, tb * 128:(tb + 1) * 128], wvv[:, k, :, 64:128], k == 0, k == 1) for k in range(2)], ck, wt, free)
                a = cp("act", V[:, tb, :], ps[:, :], t)
                Gb.give(bi, a)
                vdone.append(a)
            Wring.give(wi, t)
            yield
            odone = []
            o = lambda h: O[(h % 2) * 64:(h % 2) * 64 + 64, h // 2, :]
            yield from attention(8, lambda h: QT[0:96, h, :], lambda h: KT[0:96, h, :], 96 ** -0.5,
                                 lambda h, kt: V[:, kt, h * 64:(h + 1) * 64], o, 64, [qdone, kdone, vdone], done=odone)
            last["o"] = odone

        def rest():
            bd, cd = [], []

            def put_b(n, ps, tok):
                c = cp("act", Bc[:, 2 * n:2 * n + 2, :], ps[:, :].rearrange("p (t s) -> p t s", s=S), tok)
                bd.append(c)
                return c

            def put_cc(n, ps, tok):
                c = cp("act", ZS[:, 2 * n:2 * n + 2, 1:257], ps[:, :].rearrange("p (t s) -> p t s", s=S), tok, zs)
                cd.append(c)
                return c

            def put_x(n, ps, tok):
                z = ZS[:, 2 * n:2 * n + 2, 1:257]
                c = tt("dve", z, ps[:, :].rearrange("p (t s) -> p t s", s=S), z, MUL, tok, cd[n])
                cd[n] = c
                return c
            yield from gemm(pairs(w_in, 544, 512), 8, rhs, hd, put_b)
            yield from gemm(pairs(w_in, 1056, 512), 8, rhs, hd, put_cc)
            yield from gemm(pairs(w_in, 1568, 512), 8, rhs, hd, put_x)
            sd = []
            for t in range(4):
                si, s, sf = Scr.take()
                y = s[:, 0:S]
                a = ts("dve", y, ZS[:, t, 0:S], vec("scw", l, t), None, MUL, None, cd, sf)
                a = stt("dve", y, ZS[:, t, 1:257], vec("scw", l, 4 + t), y, MUL, ADD, a)
                a = stt("dve", y, ZS[:, t, 2:258], vec("scw", l, 8 + t), y, MUL, ADD, a)
                a = tt("pool", Bc[:, t, :], Bc[:, t, :], y, MUL, a, bd)
                Scr.give(si, a)
                sd.append(a)
            last["s"] = sd
            yield
            ud, vd = [], []

            def put_u(n, ps, tok):
                a, b = gelu(GU[:, 2 * n:2 * n + 2, :].rearrange("p t s -> p (t s)"), ps[:, :], 512, tok, None)
                ud.append(b)
                return a
            yield from gemm(pairs(w_in, 3104, 512), 8, rhs, hd, put_u)
            parts = [load(w_in, 0, 8, 3616 + 256 * i, 3872 + 256 * i) for i in range(2)]
            for tb in range(2):
                bi, ps, free = Gb.take()
                t = mms([(ps[:, i * S:(i + 1) * S], h3[:, k, tb * 128:(tb + 1) * 128], parts[i][1][:, k, :], k == 0, k == 7)
                         for i in range(2) for k in range(8)], hd, parts[0][2], parts[1][2], free)
                gv = GV[:, tb, :]
                a, b = gelu(gv, ps[:, :], 512, t, None)
                Gb.give(bi, a)
                ti, st, tf = Stat.take()
                t2, st2, tf2 = Stat.take()
                si, s, sf = Scr.take()
                c = P.put("dve", lambda e, o=s[:, 0:6], i=gv: e.bn_stats(o, i), b, sf)
                c = P.put("dve", lambda e, o=st[:, 0:2], i=s[:, 0:6]: e.bn_aggr(o, i), c, tf)
                Scr.give(si, c)
                c = rsqrt(st2[:, 0:1], st[:, 1:2], 1.0, 1e-6, [c, tf2], w=1)
                d = ts("dve", gv, gv, st[:, 0:1], st2[:, 0:1], SUB, MUL, c)
                d = tt("dve", gv, gv, GR[:, 0:512], MUL, d, t_gr)
                d = tt("dve", gv, gv, GR[:, 512:1024], ADD, d)
                Stat.give(ti, d)
                Stat.give(t2, d)
                vd.append(d)
                yield
            for i in range(2):
                Wring.give(parts[i][0], t)
            gd = []
            for g in range(4):
                bi, ps, free = Ab.take()
                t = mms([(ps[:, n * 128:(n + 1) * 128], GV[:, n, g * 128:(g + 1) * 128], WS[:, g * 128:(g + 1) * 128], True, True)
                         for n in range(2)], vd, t_ws, free)
                si, s, sf = Scr.take()
                a = tt("dve", s[:, 0:S].rearrange("p (n t) -> p n t", n=2), ps[:, 0:S].rearrange("p (n t) -> p n t", n=2),
                       bc(GR[:, 1024 + g * 128:1024 + (g + 1) * 128], 2), ADD, t, sf, t_gr)
                Ab.give(bi, a)
                a = tt("pool", GU[:, g, :], GU[:, g, :], s[:, 0:S], MUL, a, ud)
                Scr.give(si, a)
                gd.append(a)
            use_small[0] = [gd, t]
            last["g"] = gd
            yield

            gi, hb, gf = Scr.take()
            hbt = ts("dve", hb[:, 0:32], vec("gb", l, 0, 32), 0.5, None, MUL, None, gf, t_c)
            gates = []

            def put_gate(n, ps, tok):
                r = [act(G[:, 2 * n + u, :], ps[:, u * S:(u + 1) * S], ACT.Tanh, tok, hbt, bias=hb[:, 2 * n + u:2 * n + u + 1], scale=0.5)
                     for u in range(2)]
                gates.append(r)
                return r
            yield from gemm(pairs(w_in, 4128, 4096), 8, rhs, hd, put_gate)
            Scr.give(gi, gates)
            last["gates"] = gates

        interleave([main(), rest(), conv()], [1.0, 1.0, 1.6])

        M = big(9216, 8, S)
        mt = {}
        for b, (src, key, W) in enumerate(((Bc, "s", "w_o_sc"), (GU, "g", "w_o_gm"), (CY, "y", "w_o_cf"), (O, "o", "w_o_mla"))):
            gb = {"s": 1, "g": 3, "y": 2, "o": 0}[key]

            def put_m(n, ps, tok, b=b, gb=gb):
                mv = M[:, 2 * n:2 * n + 2, :].rearrange("p t s -> p (t s)")
                gv = G[:, 8 * gb + 2 * n:8 * gb + 2 * n + 2, :].rearrange("p t s -> p (t s)")
                if b == 0:
                    a = stt("dve", mv, gv, 1.0, ps[:, :], ADD, MUL, tok, last["gates"], last["o"])
                    mt[n] = a
                    return a
                si, s, sf = Scr.take()
                a = stt("dve", s, gv, 1.0, ps[:, :], ADD, MUL, tok, sf)
                mt[n] = tt("pool", mv, mv, s, ADD, a, mt[n])
                Scr.give(si, mt[n])
                return a
            yield from gemm(pairs(ins[W][l], 0, 1024, 512), 4, lambda k, src=src: src[:, k, :], last[key], put_m)
        Y = big(0, 8, S)
        yd = []

        def put_y(n, ps, tok):
            a = cp("act", Y[:, 2 * n:2 * n + 2, :].rearrange("p t s -> p (t s)"), ps[:, :], tok)
            yd.append(a)
            return a
        md = list(mt.values())
        yield from gemm(pairs(ins["w_out"][l], 0, 1024), 8, lambda k: M[:, k, :], md, put_y)
        xdep[:] = residual_rms(Y, "npo", l, yd, 0.5)

    def ffn_up(Wg, Wu, g0, u0, nt, F, hd, gate=None):
        jobs = []
        for a in range(0, nt, 2):
            m = min(2, nt - a)
            jobs.append(([(Wg, g0 + a * 128, g0 + (a + m) * 128), (Wu, u0 + a * 128, u0 + (a + m) * 128)],
                         [[(0, i * 128, 128), (1, i * 128, 128)] for i in range(m)]))
        fd = []

        def put_f(n, ps, tok):
            si, s, sf = Scr.take()
            t = act(s[:, 0:S], ps[:, 0:S], ACT.Tanh, tok, sf, scale=0.5)
            a = stt("dve", s[:, S:2 * S], s[:, 0:S], 1.0, ps[:, 0:S], ADD, MUL, t)
            if gate is not None:
                a = tt("pool", s[:, S:2 * S], s[:, S:2 * S], gate, MUL, a)
            b = stt("dve", F[:, n, :], ps[:, S:2 * S], 0.5, s[:, S:2 * S], MUL, MUL, a)
            Scr.give(si, b)
            fd.append(b)
            return b
        yield from gemm(jobs, 8, lambda k: h3[:, k, :], hd, put_f)
        return fd

    def block1_ffn(l):
        P.barrier()
        hd = rmsnorm(x3, 8, "nfp", l, h3, xdep)
        F = big(0, 22, S)
        fd = yield from ffn_up(ins["w_ffn_in"][l], ins["w_ffn_in"][l], 0, 2816, 22, F, hd)
        Y = big(5632, 8, S)
        yd = []

        def put_y(n, ps, tok):
            a = cp("act", Y[:, 2 * n:2 * n + 2, :].rearrange("p t s -> p (t s)"), ps[:, :], tok)
            yd.append(a)
            return a
        yield from gemm(pairs(ins["w_ffn_out"][l], 0, 1024), 22, lambda k: F[:, k, :], fd, put_y)
        xdep[:] = residual_rms(Y, "nfo", l, yd, 1.0)

    def add_x(n, ps, tok, fac=1.0):
        v = x3[:, 2 * n:2 * n + 2, :].rearrange("p t s -> p (t s)")
        a = stt("dve", v, ps[:, :], fac, v, MUL, ADD, tok)
        xnew.append(a)
        return a

    xnew = []

    vf3 = VF[:, :].rearrange("p (t s) -> p t s", s=S)
    small2 = [None]

    def block_rsqrt(dst, src, nt, lhsT, scale, eps, dep, floor=None):
        toks = []
        for t0 in range(0, nt, 2):
            m = min(2, nt - t0)
            si, sq, sf = Scr.take()
            a = act(sq[:, 0:m * S].rearrange("p (t s) -> p t s", s=S), src[:, t0:t0 + m, :], ACT.Square, dep, sf)
            bi, ps, free = Ab.take()
            k = mms([(ps[:, 0:m * S], lhsT, sq[:, 0:m * S], True, True)], a, free, t_c)
            Scr.give(si, k)
            k = rsqrt(dst[:, t0:t0 + m, :].rearrange("p t s -> p (t s)"), ps[:, 0:m * S], scale, eps, k, w=m * S, floor=floor)
            Ab.give(bi, k)
            toks.append(k)
        return toks

    def block2_mix(l):
        P.barrier()
        w_in = ins["w_in_2"][l]
        ld = [P.dma("sw0", SW[0:64, 0:512], ins["rwkv_w2_2"][l], small2[0]),
              P.dma("sw1", SW[0:64, 512:1024], ins["rwkv_a2_2"][l], small2[0]),
              P.dma("sw2", SW[:, 1024:1536], ins["rwkv_g2_2"][l], small2[0])]
        if l:
            ld += [P.dma("sw3", SW[:, 1536:1664].rearrange("p (k n) -> p k n", n=32),
                         ins["rwkv_v1_2"][l - 1].rearrange("(k p) n -> p k n", p=128), small2[0]),
                   P.dma("sw4", SW[0:32, 1664:2176], ins["rwkv_v2_2"][l - 1], small2[0])]
        hd = rmsnorm(x3, 8, "nmix", l, h3, xdep)
        rhs = lambda k: h3[:, k, :]
        yield
        CS = big(0, 15, S)
        CP = big(3840, 15, 257)
        zc = P.put("pool", lambda e: e.memset(CP[:, :, 0:1], 0.0))
        cd = []

        def put_p(n, ps, tok):
            a = cp("act", CP[:, 2 * n:2 * n + 2, 1:257], ps[:, :].rearrange("p (t s) -> p t s", s=S), tok)
            cd.append(a)
            return a
        yield from gemm(pairs(w_in, 0, 1536), 8, rhs, hd, put_p)

        def put_q(n, ps, tok):
            a = cp("act", CP[0:64, 12:14, 1:257], ps[0:64, :].rearrange("p (t s) -> p t s", s=S), tok)
            cd.append(a)
            return a

        def put_r(n, ps, tok):
            a = cp("act", CP[:, 14, 1:257], ps[:, 0:S], tok)
            cd.append(a)
            return a
        yield from gemm([([(w_in, 1536, 1664)], [[(0, 0, 64), (0, 64, 64)]])], 8, rhs, hd, put_q)
        yield from gemm(pairs(w_in, 1664, 128), 8, rhs, hd, put_r)
        md = []
        for t0, t1, pp in ((0, 12, 128), (12, 14, 64), (14, 15, 128)):
            a = tt("dve", CS[0:pp, t0:t1, :], CP[0:pp, t0:t1, 0:S], CP[0:pp, t0:t1, 1:257], SUB, cd, zc)
            for t in range(t0, t1):
                md.append(stt("dve", CS[0:pp, t, :], CS[0:pp, t, :], vec("mu", l, t)[0:pp, :], CP[0:pp, t, 1:257], MUL, ADD, a))
        yield
        r3, k3, v3 = CS[:, 0:4, :], CS[:, 4:8, :], CS[:, 8:12, :]
        B0 = 3840
        LW, CUM, AA, GG, KK, BB = (big(B0 + 1024 * i, 4, S) for i in range(6))
        AR = big(B0 + 6144, 4, 2, 2, 128)
        BT, KTl, BH, KH = (big(B0 + 8192 + 1024 * i, 4, S) for i in range(4))
        Y = big(B0 + 12288, 4, S)
        RP = big(B0 + 13312, 8, S)
        MN = big(B0 + 15360, 8, 3, 128)
        PC = big(B0 + 18432, 4, 4)
        PC0 = big(B0 + 18448, 2, 4, 4)

        si, tw, sf = Scr.take()
        a = act(tw[0:64, 0:S], CS[0:64, 12, :], ACT.Tanh, md, sf)
        g1 = act(tw[:, S:2 * S], CS[:, 14, :], ACT.Tanh, md, scale=0.5)
        g1 = ts("dve", tw[:, S:2 * S], tw[:, S:2 * S], 0.5, 0.5, MUL, ADD, g1)
        hi, hbv, hf = Scr.take()
        hb = ts("dve", hbv[:, 0:4], vec("w0", l, 0, 4), 0.5, None, MUL, None, hf, t_c)
        hb = ts("dve", hbv[:, 4:8], vec("a0", l, 0, 4), 0.5, None, MUL, None, hb)
        if l:
            hb = ts("dve", hbv[:, 8:12], vec("v0", l, 0, 4), 0.5, None, MUL, None, hb)
        hb = ts("dve", hbv[:, 12:16], vec("ka", l, 0, 4), -1.0, 1.0, MUL, ADD, hb)
        cde = float(np.exp(-0.5) / 2)
        lw, aa, gg = [], [], []
        for p in range(2):
            bi, ps, free = Ab.take()
            t = mms([(ps[:, u * S:(u + 1) * S], SW[0:64, (2 * p + u) * 128:(2 * p + u + 1) * 128], tw[0:64, 0:S], True, True) for u in range(2)], a, ld, free)
            ac = [act(LW[:, 2 * p + u, :], ps[:, u * S:(u + 1) * S], ACT.Tanh, t, hb, md, bias=hbv[:, 2 * p + u:2 * p + u + 1], scale=0.5) for u in range(2)]
            Ab.give(bi, ac)
            lw.append(ts("dve", LW[:, 2 * p:2 * p + 2, :], LW[:, 2 * p:2 * p + 2, :], -cde, -cde, MUL, ADD, ac))
            bi, ps, free = Ab.take()
            t2 = mms([(ps[:, u * S:(u + 1) * S], SW[0:64, 512 + (2 * p + u) * 128:512 + (2 * p + u + 1) * 128], CS[0:64, 13, :], True, True) for u in range(2)], md, ld, free)
            ac = [act(AA[:, 2 * p + u, :], ps[:, u * S:(u + 1) * S], ACT.Tanh, t2, hb, bias=hbv[:, 4 + 2 * p + u:5 + 2 * p + u], scale=0.5) for u in range(2)]
            Ab.give(bi, ac)
            aa.append(ts("dve", AA[:, 2 * p:2 * p + 2, :], AA[:, 2 * p:2 * p + 2, :], 0.5, 0.5, MUL, ADD, ac))
            bi, ps, free = Ab.take()
            t3 = mms([(ps[:, u * S:(u + 1) * S], SW[:, 1024 + (2 * p + u) * 128:1024 + (2 * p + u + 1) * 128], tw[:, S:2 * S], True, True) for u in range(2)], g1, ld, free)
            gg.append(cp("act", GG[:, 2 * p:2 * p + 2, :].rearrange("p t s -> p (t s)"), ps[:, :], t3, md))
            Ab.give(bi, gg[-1])
            yield
        Scr.give(si, t, t3)
        if l == 0:
            vdep = [cp("pool", vf3, v3, md)]
        else:
            bi, ps, free = Ab.take()
            t = mms([(ps[0:32, 0:S], SW[:, 1536 + 32 * k:1568 + 32 * k], v3[:, k, :], k == 0, k == 3) for k in range(4)], md, ld, free)
            si, s, sf = Scr.take()
            c = cp("act", s[0:32, 0:S], ps[0:32, 0:S], t, sf)
            Ab.give(bi, c)
            vdep = []
            df = tt("dve", vf3, vf3, v3, SUB, md)
            for p in range(2):
                bi, ps, free = Ab.take()
                t = mms([(ps[:, u * S:(u + 1) * S], SW[0:32, 1664 + (2 * p + u) * 128:1664 + (2 * p + u + 1) * 128], s[0:32, 0:S], True, True) for u in range(2)], c, ld, free)
                di, d, df2 = Scr.take()
                ac = [act(d[:, u * S:(u + 1) * S], ps[:, u * S:(u + 1) * S], ACT.Tanh, t, hb, df2, bias=hbv[:, 8 + 2 * p + u:9 + 2 * p + u], scale=0.5) for u in range(2)]
                Ab.give(bi, ac)
                x = ts("dve", d, d, 0.5, 0.5, MUL, ADD, ac)
                x = tt("dve", d, d, vf3[:, 2 * p:2 * p + 2, :].rearrange("p t s -> p (t s)"), MUL, x, df)
                vp = v3[:, 2 * p:2 * p + 2, :].rearrange("p t s -> p (t s)")
                x = tt("dve", vp, vp, d, ADD, x)
                Scr.give(di, x)
                vdep.append(x)
            Scr.give(si, t)
            yield
        kt = [ts("dve", KK[:, t, :], k3[:, t, :], vec("kk", l, t), None, MUL, None, md) for t in range(4)]
        rq = block_rsqrt(BB, KK, 4, BONES, 1.0, 0.0, kt, floor=1e-24)
        kn = tt("dve", KK[:, :, :], KK[:, :, :], BB[:, :, :], MUL, rq, kt)
        yield
        k2 = []
        for t in range(4):
            c = ts("dve", BT[:, t, :], AA[:, t, :], vec("ka", l, t), hbv[:, 12 + t:13 + t], MUL, ADD, aa, hb)
            k2.append(tt("dve", k3[:, t, :], k3[:, t, :], BT[:, t, :], MUL, c, kt))
        Scr.give(hi, k2, lw, aa)
        bb = tt("dve", BB[:, :, :], KK[:, :, :], AA[:, :, :], MUL, kn, aa)
        cu = []
        for t in range(4):
            cu.append(P.put("dve", lambda e, t=t: e.tensor_tensor_scan(CUM[:, t, :], SCM, LW[:, t, :], 0.0, MUL, ADD), lw, t_c))
        yield
        e1 = tt("dve", LW[:, :, :], CUM[:, :, :], LW[:, :, :], SUB, cu)
        e1 = act(LW[:, :, :], LW[:, :, :], ACT.Exp, e1)
        a1 = stt("dve", AR[:, :, :, 0, :], KK[:, :, :].rearrange("p t (b s) -> p t b s", s=128), -1.0,
                 LW[:, :, :].rearrange("p t (b s) -> p t b s", s=128), MUL, MUL, e1, kn)
        e2 = act(LW[:, :, :], CUM[:, :, :], ACT.Exp, a1, cu)
        a2 = tt("dve", AR[:, :, :, 1, :], r3.rearrange("p t (b s) -> p t b s", s=128), LW[:, :, :].rearrange("p t (b s) -> p t b s", s=128), MUL, e2, md)
        cl = CUM[:, :, :].rearrange("p t (c s) -> p t c s", s=64)
        pc = act(PC[:, :, :], cl[:, :, :, 63], ACT.Exp, cu, md)
        e3 = act(LW[:, :, :], CUM[:, :, :], ACT.Exp, a2, scale=-1.0)
        b1 = tt("dve", BT[:, :, :], BB[:, :, :], LW[:, :, :], MUL, e3, bb, k2)
        b2 = tt("dve", KTl[:, :, :], k3, LW[:, :, :], MUL, e3, k2)
        yield
        e4 = []
        for t in range(4):
            e4.append(tt("dve", LW[:, t, :].rearrange("p (c s) -> p c s", s=64),
                         cl[:, t, :, 63:64].broadcast_to([128, 4, 64]), cl[:, t, :, :], SUB, b1, b2))
        e4 = act(LW[:, :, :], LW[:, :, :], ACT.Exp, e4)
        b3 = tt("dve", BH[:, :, :], BB[:, :, :], LW[:, :, :], MUL, e4, bb)
        b4 = tt("dve", KH[:, :, :], k3, LW[:, :, :], MUL, e4, k2)
        bo = [stt("dve", BB[:, t, :], r3[:, t, :], vec("rk", l, t), k3[:, t, :], MUL, MUL, b1, b3) for t in range(4)]
        bon = []
        for p in range(2):
            bi, ps, free = Ab.take()
            bp = BB[:, 2 * p:2 * p + 2, :].rearrange("p t s -> p (t s)")
            t = mms([(ps[:, :], BONES, bp, True, True)], bo, free)
            bon.append(tt("dve", bp, ps[:, :], v3[:, 2 * p:2 * p + 2, :].rearrange("p t s -> p (t s)"), MUL, t, vdep))
            Ab.give(bi, bon[-1])
        pc0 = [cp("dve", PC0[0:64, e, :, :], PC[64 * e:64 * e + 64, :, :], pc) for e in range(2)]
        ready = [a1, a2, b1, b2, b3, b4, vdep, pc]
        yield
        WK = [big(B0, 1024), big(B0 + 1024, 1024)]
        WK2 = [big(B0 + 2048, 1024), big(B0 + 4096, 1024)]
        WK3 = [MISC[:, 0:1536], MISC[:, 1536:3072]]
        gfree = [ready, ready]
        yd, rd, mn = [], [], []

        def group(j, blk, z):
            dep = [ready, gfree[z]]
            LT4 = WK[z].rearrange("p (e n) -> p e n", e=2)
            LL = WK2[z][:, 0:512].rearrange("p (e a n) -> p e a n", e=2, a=2)
            TT = WK2[z][:, 512:1024].rearrange("p (e a n) -> p e a n", e=2, a=2)
            TK = WK3[z][:, 0:512].rearrange("p (a n) -> p a n", a=4)
            Lf = WK3[z][:, 512:768].rearrange("p (e n) -> p e n", e=2)
            L16 = WK3[z][:, 768:1024].rearrange("p (e n) -> p e n", e=2)
            ZZ = WK3[z][:, 1024:1280].rearrange("p (e n) -> p e n", e=2)
            XU = WK3[z][:, 1280:1536].rearrange("p (e n) -> p e n", e=2)
            cols = slice(blk * 128, (blk + 1) * 128)
            bi, ps, free = Ab.take()
            t = mms([(ps[:, 0:128], AR[:, j, blk, 0, :], None, 1, 1), (ps[:, 128:256], v3[:, j, cols], None, 1, 1),
                     (ps[:, 256:384], BH[:, j, cols], None, 1, 1), (ps[:, 384:512], KH[:, j, cols], None, 1, 1)], dep, free)
            tk = cp("act", TK.rearrange("p a n -> p (a n)"), ps[:, :], t, dep)
            Ab.give(bi, tk)
            lt = []
            for e in range(2):
                r = slice(64 * e, 64 * e + 64)
                bi, ps, free = Ab.take()
                ar = AR[r, j, blk, :, :].rearrange("p a n -> p (a n)")
                t = mms([(ps[:, 0:256], BT[r, j, cols], ar, True, True), (ps[:, 256:512], KTl[r, j, cols], ar, True, True)], dep, free)
                lt.append(tt("dve", LT4[:, e, :], ps[:, :], MASKT, MUL, t, dep))
                Ab.give(bi, lt[-1])
            yield
            lf = []
            for e in range(2):
                bi, ps, free = Ab.take()
                r = slice(64 * e, 64 * e + 64)
                t = mms([(ps[:, 0:128], AR[r, j, blk, 0, :], BT[r, j, cols], True, True)], dep, free)
                lf.append(tt("dve", Lf[:, e, :], ps[:, 0:128], CST64, MUL, t, dep))
                Ab.give(bi, lf[-1])
            d1 = tt("pool", LL[:, :, 0, :], Lf, bc(D16, 2), MUL, lf, dep)
            d2 = tt("pool", LL[:, :, 1, :], LT4[:, :, 0:128], bc(D16T, 2), MUL, lt, dep)
            i1 = tt("pool", TT[:, :, 0, :], LL[:, :, 0, :], bc(IDENT, 2), ADD, d1, dep)
            i2 = tt("pool", TT[:, :, 1, :], LL[:, :, 1, :], bc(IDENT, 2), ADD, d2, dep)
            l16 = tt("pool", L16, Lf, bc(C16, 2), MUL, lf, dep)
            l32 = tt("pool", Lf, Lf, bc(C32, 2), MUL, l16, d1)
            yield
            ll, tn = [d1, d2], [i1, i2]
            for m in range(3):
                bi, ps, free = Ab.take()
                v = ps[:, :].rearrange("p (e a n) -> p e a n", e=2, a=2)
                t = mms([x for e in range(2) for x in ((v[:, e, 0, :], LL[:, e, 1, :], LL[:, e, 0, :], True, True),
                                                      (v[:, e, 1, :], LL[:, e, 0, :], LL[:, e, 1, :], True, True))], ll, free)
                ll = cp("act", LL, v, t, tn)
                Ab.give(bi, ll)
                yield
                bi, ps, free = Ab.take()
                v = ps[:, :].rearrange("p (e a n) -> p e a n", e=2, a=2)
                t = mms([x for e in range(2) for x in ((v[:, e, 0, :], TT[:, e, 1, :], LL[:, e, 0, :], True, True),
                                                      (v[:, e, 1, :], LL[:, e, 0, :], TT[:, e, 1, :], True, True))], ll, tn, free)
                tn = tt("dve", TT, TT, v, ADD, t)
                Ab.give(bi, tn)
                yield
            for c, Lo in ((0, L16), (1, Lf)):
                bi, ps, free = Ab.take()
                t = mms([(ps[:, e * 128:(e + 1) * 128], Lo[:, e, :], TT[:, e, 1, :], True, True) for e in range(2)], tn, l16, l32, free)
                zz = cp("act", ZZ, ps[:, 0:256].rearrange("p (e n) -> p e n", e=2), t, dep, tn)
                Ab.give(bi, zz)
                bi, ps, free = Ab.take()
                v = ps[:, :].rearrange("p (e a n) -> p e a n", e=2, a=2)
                if c == 0:
                    t = mms([x for e in range(2) for x in ((v[:, e, 0, :], ZZ[:, e, :], TT[:, e, 0, :], True, True),
                                                          (v[:, e, 1, :], TT[:, e, 0, :], ZZ[:, e, :], True, True))], zz, free)
                    tn = tt("dve", TT, TT, v, ADD, t)
                else:
                    t = mms([(v[:, e, 1, :], TT[:, e, 0, :], ZZ[:, e, :], True, True) for e in range(2)], zz, free)
                    tn = tt("dve", TT[:, :, 1, :], TT[:, :, 1, :], v[:, :, 1, :], ADD, t)
                Ab.give(bi, tn)
                yield
            bi, ps, free = Ab.take()
            t = mms([(ps[:, e * 64:(e + 1) * 64], LT4[:, e, 256:384], TK[:, 1, e * 64:(e + 1) * 64], True, True) for e in range(2)], lt, tk, free)
            xc = cp("act", ZZ[:, 0, :], ps[:, 0:128], t, tn)
            Ab.give(bi, xc)
            bi, ps, free = Ab.take()
            v = ps[:, 0:256].rearrange("p (e n) -> p e n", e=2)
            t = mms([x for e in range(2) for x in ((v[:, e, 0:64], TT[:, e, 1, :], TK[:, 0, e * 64:(e + 1) * 64], True, True),
                                                  (v[:, e, 64:128], TT[:, e, 1, :], ZZ[:, 0, e * 64:(e + 1) * 64], True, True))], xc, tn, tk, free)
            xu = cp("act", XU, v, t, dep)
            Ab.give(bi, xu)
            yield
            bi, ps, free = Ab.take()
            t = mms([x for e in range(2) for x in (
                (ps[0:64, e * 128:(e + 1) * 128], XU[:, e, 0:64], LT4[:, e, 128:256], True, True),
                (ps[0:64, 256 + e * 128:384 + e * 128], XU[:, e, 64:128], LT4[:, e, 128:256], True, False),
                (ps[0:64, 256 + e * 128:384 + e * 128], TK[:, 1, e * 64:(e + 1) * 64], LT4[:, e, 384:512], False, True))], xu, free)
            o = []
            for e in range(2):
                r = slice(64 * e, 64 * e + 64)
                o.append(tt("dve", RP[0:64, 2 * j + e, cols], ps[0:64, e * 128:(e + 1) * 128], AR[r, j, blk, 1, :], ADD, t, dep))
                o.append(cp("dve", Y[r, j, cols], ps[0:64, 256 + e * 128:384 + e * 128], t, dep))
            Ab.give(bi, o)
            rd.append(o)
            mm = []
            for c in range(2):
                ch = 2 * blk + c
                if ch == 3:
                    continue
                r = slice(64 * c, 64 * c + 64)
                bi, ps, free = Ab.take()
                v = ps[0:64, 0:256].rearrange("p (e n) -> p e n", e=2)
                items = []
                for e in range(2):
                    q = slice(64 * e, 64 * e + 64)
                    items += [(v[:, e, 0:64], XU[r, e, 0:64], TK[r, 2, q], True, True),
                              (v[:, e, 64:128], TK[r, 2, q], XU[r, e, 64:128], True, False),
                              (v[:, e, 64:128], TK[r, 3, q], TK[r, 1, q], False, True)]
                t = mms(items, xu, tk, free)
                c2 = [cp("dve", MN[0:64, 2 * j:2 * j + 2, ch, 64:128], v[:, :, 64:128], t, dep)]
                for e in range(2):
                    c2.append(stt("dve", MN[0:64, 2 * j + e, ch, 0:64], ID64[0:64, :], PC0[0:64, e, j, ch:ch + 1], v[:, e, 0:64], MUL, ADD, t, pc0))
                Ab.give(bi, c2)
                mm.append(c2)
            mn.append(mm)
            gfree[z] = [o, mm, t]
            yield

        groups = [(j, b) for j in range(4) for b in range(2)]
        for i in range(0, 8, 2):
            interleave([group(*groups[i], 0), group(*groups[i + 1], 1)], [1.0, 1.0])
            yield
        SS = WK[0].rearrange("p (h n) -> p h n", n=64)
        sd = [mn, gfree[0], gfree[1]]
        for c in range(1, 3):
            bi, ps, free = Ab.take()
            prev = (lambda h: MN[0:64, h, 0, 64:128]) if c == 1 else (lambda h: SS[0:64, h, :])
            t = mms([(ps[0:64, h * 64:(h + 1) * 64], MN[0:64, h, c, 0:64], prev(h), True, True) for h in range(8)], sd, free)
            sd = [tt("dve", SS[0:64, 8 * (c - 1):8 * c, :], ps[0:64, :].rearrange("p (h n) -> p h n", n=64), MN[0:64, :, c, 64:128], ADD, t, sd)]
            Ab.give(bi, sd)
        yy = []
        for h in range(8):
            bi, ps, free = Ab.take()
            st = [MN[0:64, h, 0, 64:128], SS[0:64, h, :], SS[0:64, 8 + h, :]]
            t = mms([(ps[0:64, 64 * c:64 * c + 64], st[c], RP[0:64, h, 64 * c + 64:64 * c + 128], True, True) for c in range(3)], sd, rd, free)
            r = slice(64 * (h % 2), 64 * (h % 2) + 64)
            yy.append(tt("dve", Y[r, h // 2, 64:256], ps[0:64, 0:192], Y[r, h // 2, 64:256], ADD, t, rd))
            Ab.give(bi, yy[-1])
        yield
        cen = []
        for p in range(2):
            bi, ps, free = Ab.take()
            yp = Y[:, 2 * p:2 * p + 2, :].rearrange("p t s -> p (t s)")
            t = mms([(ps[:, :], BONES, yp, True, True)], yy, free)
            cen.append(stt("dve", yp, ps[:, :], -1.0 / 64, yp, MUL, ADD, t))
            Ab.give(bi, cen[-1])
        rq = block_rsqrt(KTl, Y, 4, BONES, 1.0 / 64, 1e-5 * 64, cen)
        a = tt("dve", Y[:, :, :], Y[:, :, :], KTl[:, :, :], MUL, rq, cen)
        fin = []
        for t in range(4):
            b = ts("dve", Y[:, t, :], Y[:, t, :], vec("lxg", l, t), vec("lxb", l, t), MUL, ADD, a)
            b = tt("dve", Y[:, t, :], Y[:, t, :], BB[:, t, :], ADD, b, bon)
            fin.append(tt("dve", Y[:, t, :], Y[:, t, :], GG[:, t, :], MUL, b, gg))
        ya = cp("pool", YA3, Y[:, :, :], fin)
        small2[0] = P.now()
        yield

        P.barrier()
        DA = big(0, 10, S)
        V2 = big(2560, 2, 64)
        IW = big(2688, 2, 8)
        RR = big(2816, 6, S)
        O = big(4352, 4, S)
        SCO = big(5376, 2, S)
        WKX = big(5888, 2, S)
        PEN = big(6400, 2, S)
        dd = []

        def put_d(t0):
            def f(n, ps, tok):
                a = cp("act", DA[:, t0 + 2 * n:t0 + 2 * n + 2, :], ps[:, :].rearrange("p (t s) -> p t s", s=S), tok)
                dd.append(a)
                return a
            return f
        yield from gemm(pairs(w_in, 1792, 512), 8, rhs, hd, put_d(0))
        for j, c0 in enumerate((2304, 2944)):
            w = 128 if j == 0 else 72
            wi, wv, wt = load(w_in, 0, 8, c0, c0 + w)
            bi, ps, free = Gb.take()
            items = [(ps[0:64, 0:S], wv[:, k, 0:64], h3[:, k, :], k == 0, k == 7) for k in range(8)]
            n = w - 64
            items += [(ps[:, S + 64 * tb:S + 64 * tb + n], h3[:, k, tb * 128:(tb + 1) * 128], wv[:, k, 64:w], k == 0, k == 7)
                      for tb in range(2) for k in range(8)]
            t = mms(items, hd, wt, free)
            Wring.give(wi, t)
            o = [cp("act", DA[0:64, 4 + j, :], ps[0:64, 0:S], t), cp("act", DA[64:128, 4 + j, :], ps[0:64, 0:S], t)]
            dst = V2 if j == 0 else IW
            o.append(cp("act", dst[:, :, :], ps[:, S:S + 128].rearrange("p (b n) -> p b n", b=2)[:, :, 0:n], t))
            Gb.give(bi, o)
            dd.append(o)
        yield from gemm(pairs(w_in, 2432, 512), 8, rhs, hd, put_d(6))
        rq = block_rsqrt(RR, DA, 6, BONES, 1.0 / 64, 1e-6, dd)
        nd = []
        for t in range(6):
            key = "dq" if t < 4 else ("dk" if t == 4 else "di")
            nd.append(stt("dve", DA[:, t, :], DA[:, t, :], vec(key, l), RR[:, t, :], MUL, MUL, rq, dd))
        cos2, sin2 = ROPE[:, 512:768], ROPE[:, 768:1024]
        rp = []
        for p in range(5):
            bi, ps, free = Ab.take()
            dv = DA[:, 2 * p:2 * p + 2, :]
            t = mms([(ps[:, :], ROT64, dv.rearrange("p t s -> p (t s)"), True, True)], nd, dd, free)
            a = tt("dve", dv, dv, bc(cos2, 2), MUL, t, t_rope)
            si, s, sf = Scr.take()
            s3 = s.rearrange("p (t s) -> p t s", s=S)
            b = tt("dve", s3, ps[:, :].rearrange("p (t s) -> p t s", s=S), bc(sin2, 2), MUL, t, sf)
            Ab.give(bi, b)
            rp.append(tt("dve", dv, dv, s3, ADD, a, b))
            Scr.give(si, rp[-1])
        yield
        GT = big(8192, 16, S)
        gates = []

        def gate_gemm():
            def put_gate(n, ps, tok):
                a = act(GT[:, 2 * n:2 * n + 2, :].rearrange("p t s -> p (t s)"), ps[:, :], ACT.Tanh, tok, scale=0.5)
                gates.append(a)
                return a
            yield from gemm(pairs(w_in, 3016, 2048), 8, rhs, hd, put_gate)

        odone = []

        def sparse():
            nks = (128, 256)
            acc = [None, None]
            for b in range(2):
                nk = nks[b]
                for p in range(4):
                    si, s, sf = Scr.take()
                    s3 = s[:, 0:2 * nk].rearrange("p (e s) -> p e s", e=2)
                    a = []
                    for e in range(2):
                        bi, ps, free = Ab.take()
                        r = slice(64 * e, 64 * e + 64)
                        t = mms([(ps[:, 0:nk], DA[r, 6 + p, b * 128:(b + 1) * 128], DA[r, 5, 0:nk], True, True)], rp, free)
                        a.append(act(s3[:, e, :], ps[:, 0:nk], ACT.Relu, t, sf, scale=0.125))
                        Ab.give(bi, a[-1])
                    for e in range(2):
                        w = IW[:, b, 2 * p + e:2 * p + e + 1]
                        if p == 0 and e == 0:
                            acc[b] = ts("dve", SCO[:, b, 0:nk], s3[:, e, :], w, None, MUL, None, a, dd)
                        else:
                            acc[b] = stt("dve", SCO[:, b, 0:nk], s3[:, e, :], w, SCO[:, b, 0:nk], MUL, ADD, a, acc[b])
                    Scr.give(si, acc[b])
                    yield
                a = ts("dve", SCO[:, b, 0:nk], SCO[:, b, 0:nk], float(8 ** -0.5), None, MUL, None, acc[b])
                m0 = 64 if b == 0 else 192
                a = P.put("dve", lambda e, b=b, m0=m0: e.memset(SCO[0:64, b, m0:m0 + 64], -1e30), a)
                for it in range(8):
                    src = SCO if it == 0 else WKX
                    xi, m8, mf = Stat8.take()
                    c = P.put("dve", lambda e, o=m8, i=src[:, b, 0:nk]: e.max(o, i), a, mf)
                    a = P.put("dve", lambda e, o=WKX[:, b, 0:nk], r=m8, i=src[:, b, 0:nk]: e.match_replace(o, r, i, -3e38), c)
                    Stat8.give(xi, a)
                    yield
                a = ts("dve", PEN[:, b, 0:nk], WKX[:, b, 0:nk], -3e38, -1e30, ALU.is_gt, MUL, a)
                a = P.put("dve", lambda e, b=b, m0=m0: e.memset(PEN[0:64, b, m0:m0 + 64], -1e30), a)
                acc[b] = a
            yield from attention(8, lambda h: DA[64 * (h % 2):64 * (h % 2) + 64, h // 2, :],
                                 lambda h: DA[64 * (h % 2):64 * (h % 2) + 64, 4, :], 0.125,
                                 lambda h, kt: V2[:, kt, :], lambda h: O[64 * (h % 2):64 * (h % 2) + 64, h // 2, :], 64,
                                 [rp, acc], nks=nks, pen=lambda b: PEN[:, b, 0:nks[b]], done=odone)
        interleave([gate_gemm(), sparse()], [1.0, 0.25])
        M = big(12288, 8, S)
        mt = {}
        for b, (src, W, dep) in enumerate(((YA3, "w_branch_a_2", ya), (O, "w_branch_b_2", odone))):
            def put_m(n, ps, tok, b=b):
                mv = M[:, 2 * n:2 * n + 2, :].rearrange("p t s -> p (t s)")
                gv = GT[:, 8 * b + 2 * n:8 * b + 2 * n + 2, :].rearrange("p t s -> p (t s)")
                if b == 0:
                    mt[n] = stt("dve", mv, gv, 1.0, ps[:, :], ADD, MUL, tok, gates)
                    return mt[n]
                si, s, sf = Scr.take()
                a = stt("dve", s, gv, 1.0, ps[:, :], ADD, MUL, tok, sf)
                mt[n] = tt("pool", mv, mv, s, ADD, a, mt[n])
                Scr.give(si, mt[n])
                return a
            yield from gemm(pairs(ins[W][l], 0, 1024, 512), 4, lambda k, src=src: src[:, k, :], dep, put_m)
        xnew.clear()
        yield from gemm(pairs(ins["w_out_2"][l], 0, 1024), 8, lambda k: M[:, k, :], list(mt.values()), lambda n, ps, tok: add_x(n, ps, tok, 0.5))
        xdep[:] = list(xnew)

    def block2_mem(l):
        P.barrier()
        MT = big(0, 8, S)
        MH = big(2048, 8, S)
        Q = big(4096, 4, S)
        K = big(5120, 4, S)
        V = big(6144, 2, 512)
        O = big(7168, 4, S)
        RR = big(8192, 4, S)
        t_m = P.dma("mem", MT[:, :, :].rearrange("p t s -> p (t s)"), ins["memT"], P.now())
        hd = rmsnorm(x3, 8, "nmem", l, h3, xdep)
        mh = rmsnorm(MT, 8, "mtok", l, MH, [t_m])
        yield
        qd, kd, vd = [], [], []

        def put_to(dst, lst):
            def f(n, ps, tok):
                a = cp("act", dst[:, 2 * n:2 * n + 2, :].rearrange("p t s -> p (t s)"), ps[:, :], tok)
                lst.append(a)
                return a
            return f
        yield from gemm(pairs(ins["mem_wkv_2"][l], 0, 512), 8, lambda k: MH[:, k, :], mh, put_to(K, kd))
        parts = [load(ins["mem_wkv_2"][l], 0, 8, 512 + 256 * i, 768 + 256 * i) for i in range(2)]
        for tb in range(2):
            bi, ps, free = Gb.take()
            t = mms([(ps[:, i * S:(i + 1) * S], MH[:, k, tb * 128:(tb + 1) * 128], parts[i][1][:, k, :], k == 0, k == 7)
                     for i in range(2) for k in range(8)], mh, parts[0][2], parts[1][2], free)
            a = cp("act", V[:, tb, :], ps[:, :], t)
            Gb.give(bi, a)
            vd.append(a)
        for i in range(2):
            Wring.give(parts[i][0], t)
        yield from gemm(pairs(ins["mem_wq_2"][l], 0, 512), 8, lambda k: h3[:, k, :], hd, put_to(Q, qd))
        nd = []
        for src, key, dep in ((K, "mk", kd), (Q, "mq", qd)):
            rq = block_rsqrt(RR, src, 4, ONES, 1.0 / 128, 1e-6, [dep, nd])
            nd.append(tt("dve", src[:, :, :], src[:, :, :], RR[:, :, :], MUL, rq, dep))
            nd.append(ts("dve", src[:, :, :], src[:, :, :], vec(key, l), None, MUL, None, nd))
        yield
        od = []
        yield from attention(4, lambda h: Q[:, h, :], lambda h: K[:, h, :], 128 ** -0.5, lambda h, kt: V[:, kt, h * 128:(h + 1) * 128],
                             lambda h: O[:, h, :], 128, [nd, vd], done=od)
        xnew.clear()
        yield from gemm(pairs(ins["mem_wo_2"][l], 0, 1024, 512), 4, lambda k: O[:, k, :], od, lambda n, ps, tok: add_x(n, ps, tok, 1.0))
        xdep[:] = list(xnew)

    def block2_ffn():
        P.barrier()
        hd = rmsnorm(x3, 8, "nffn", 0, h3, xdep)
        F = big(0, 22, S)
        fd = yield from ffn_up(ins["ffn_wg_2"][0], ins["ffn_wu_2"][0], 0, 0, 22, F, hd)
        xnew.clear()
        yield from gemm(pairs(ins["ffn_wd_2"][0], 0, 1024), 22, lambda k: F[:, k, :], fd, lambda n, ps, tok: add_x(n, ps, tok, 1.0))
        xdep[:] = list(xnew)

    def block2_moe():
        P.barrier()
        RT = big(0, 8, 8)
        BI = big(64, 8)
        LG = big(72, 2, 8)
        GT = big(88, 2, 8)
        M8 = big(104, 2, 8)
        IX = big(120, 2, 8)
        IXF = big(136, 2, 8)
        E2 = big(152, 2, 8)
        DGm = big(256, 2, 128)
        GB = big(512, 8, S)
        Fs = [big(2560, 11, S), big(5376, 11, S)]
        t_r = [P.dma("rt", RT, ins["moe_router_2"][0].rearrange("(k p) n -> p k n", p=128), P.now()),
               P.dma("rb", BI, ins["moe_bias_2"][0].partition_broadcast(128), P.now())]
        hd = rmsnorm(x3, 8, "nffn", 1, h3, xdep)
        bi, ps, free = Ab.take()
        t = mms([(ps[:, 8 * b:8 * b + 8], h3[:, k, b * 128:(b + 1) * 128], RT[:, k, :], k == 0, k == 7) for b in range(2) for k in range(8)],
                hd, t_r, free)
        a = tt("dve", LG, ps[:, 0:16].rearrange("p (b n) -> p b n", b=2), bc(BI, 2), ADD, t, t_r)
        Ab.give(bi, a)
        gts = []
        for b in range(2):
            m = P.put("dve", lambda e, b=b: e.max(M8[:, b, :], LG[:, b, :]), a)
            i = P.put("dve", lambda e, b=b: e.max_index(IX[:, b, :].bitcast(U32), M8[:, b, :], LG[:, b, :]), m)
            i = cp("dve", IXF[:, b, :], IX[:, b, :].bitcast(U32), i)
            d = tt("dve", E2[:, b, 0:1], M8[:, b, 1:2], M8[:, b, 0:1], SUB, m)
            d = act(E2[:, b, 0:1], E2[:, b, 0:1], ACT.Exp, d)
            s = ts("dve", E2[:, b, 1:2], E2[:, b, 0:1], 1.0, None, ADD, None, d)
            s = P.put("dve", lambda e, b=b: e.reciprocal(E2[:, b, 2:3], E2[:, b, 1:2]), s)
            s = tt("dve", E2[:, b, 3:4], E2[:, b, 0:1], E2[:, b, 2:3], MUL, s)
            g1 = ts("dve", GT[:, b, :], IOTA8, IXF[:, b, 0:1], E2[:, b, 2:3], ALU.is_equal, MUL, s, i)
            g2 = ts("dve", M8[:, b, :], IOTA8, IXF[:, b, 1:2], E2[:, b, 3:4], ALU.is_equal, MUL, g1)
            gts.append(tt("dve", GT[:, b, :], GT[:, b, :], M8[:, b, :], ADD, g2))
        gb, dfree = [], None
        for e8 in range(8):
            dg = [ts("dve", DGm[:, b, :], IDENT, GT[:, b, e8:e8 + 1], None, MUL, None, gts, dfree) for b in range(2)]
            bi, ps, free = Ab.take()
            t = mms([(ps[:, b * 128:(b + 1) * 128], ONES, DGm[:, b, :], True, True) for b in range(2)], dg, free)
            dfree = t
            gb.append(cp("act", GB[:, e8, :], ps[:, 0:S], t))
            Ab.give(bi, gb[-1])
        yield
        xnew.clear()
        xl = {}
        ff = [None, None]

        def up(e8):
            z = e8 % 2
            fd = yield from ffn_up(ins["moe_wg_2"][0][e8], ins["moe_wu_2"][0][e8], 0, 0, 11, Fs[z], [hd, gb, ff[z]], gate=GB[:, e8, :])
            return fd

        def down(e8, fd):
            z = e8 % 2

            def put_x(n, ps, tok):
                v = x3[:, 2 * n:2 * n + 2, :].rearrange("p t s -> p (t s)")
                xl[n] = tt("dve", v, ps[:, :], v, ADD, tok, xl.get(n), hd)
                ff[z] = tok
                return xl[n]
            yield from gemm(pairs(ins["moe_wd_2"][0][e8], 0, 1024), 11, lambda k: Fs[z][:, k, :], fd, put_x)
        for e8 in range(8):
            fd = yield from up(e8)
            yield from down(e8, fd)
        xdep[:] = list(xl.values())

    YA3 = big(20480, 4, S)
    Stat8 = Ring([S8[:, i * 8:(i + 1) * 8] for i in range(4)])

    phases = [lambda: block1_mix(0), lambda: block1_ffn(0), lambda: block1_mix(1), lambda: block1_ffn(1),
              lambda: block2_mix(0), lambda: block2_mem(0), block2_ffn, lambda: block2_mix(1), lambda: block2_mem(1), block2_moe]
    for ph in phases[ins.get("first", 0):ins.get("last", len(phases))]:
        run(ph())
    t_out = P.dma("out", out, X[:, :], xdep)

    with nc.Block() as block:
        @block.tensor
        def _(e):
            P.replay("pe", e)

        @block.scalar
        def _(e):
            P.replay("act", e)

        @block.vector
        def _(e):
            P.replay("dve", e)

        @block.gpsimd
        def _(e):
            P.replay("pool", e)

        @block.sync
        def _(e):
            P.replay("sp", e)
            e.wait_ge(P.sem[t_out[0]], t_out[1])


def constants():
    c = np.zeros((128, NCST), np.float32)
    i = np.arange(128)
    c[:, 0:128] = np.eye(128)
    c[:, 128:256] = 1.0
    c[:, 256:384] = (i[:, None] // 64) == (i[None, :] // 64)
    for m in range(64, 96):
        if m < 80:
            c[m + 16, 384 + m] = -1.0
        else:
            c[m - 16, 384 + m] = 1.0
    for m in range(128):
        if m % 64 < 32:
            c[m + 32, 512 + m] = -1.0
        else:
            c[m - 32, 512 + m] = 1.0
    t, j = i[:, None], i[None, :]
    low = t > j
    c[:, 640:768] = low & (t // 16 == j // 16)
    c[:, 768:896] = (low & (t // 16 == j // 16)).T
    c[:, 896:1024] = low & (t // 32 == j // 32) & (t // 16 != j // 16)
    c[:, 1024:1152] = low & (t // 64 == j // 64) & (t // 32 != j // 32)
    c[:, 1152:1280] = low & (t // 64 == j // 64)
    strict = ((t < j) & (t // 64 == j // 64)).astype(np.float32)
    incl = ((t <= j) & (t // 64 == j // 64)).astype(np.float32)
    c[:, 1280:1792] = np.concatenate([strict, incl, strict, incl], 1)
    c[:, 1792:2048] = (np.arange(256) % 64 != 0)[None, :]
    c[:, 2048:2112] = np.tile(np.eye(64), (2, 1))
    c[:, 2112:2120] = np.arange(8)[None, :]
    f1 = np.array(INV1, np.uint32).view(np.float32)
    f2 = np.array(INV2, np.uint32).view(np.float32)
    c[:, 2120] = f1[i % 16]
    c[:, 2121] = f2[i % 32]
    return c


INV1 = [0x3f800000, 0x3f0ff59a, 0x3ea1e89b, 0x3e361887, 0x3dcccccd, 0x3d6655c3, 0x3d0186e2, 0x3c91ad39, 0x3c23d70a, 0x3bb8449c,
        0x3b4f3e37, 0x3ae91528, 0x3a83126f, 0x3a136a16, 0x39a5cb5f, 0x393a7753]
INV2 = [0x3f800000, 0x3f3ff911, 0x3f0ff59a, 0x3ed7e89b, 0x3ea1e89b, 0x3e72d423, 0x3e361887, 0x3e088d77, 0x3dcccccd, 0x3d99940d,
        0x3d6655c2, 0x3d2cba15, 0x3d0186e3, 0x3cc2434f, 0x3c91ad39, 0x3c5a7bf2, 0x3c23d70a, 0x3bf5b9b0, 0x3bb8449c, 0x3b8a2e77,
        0x3b4f3e38, 0x3b1b690d, 0x3ae91528, 0x3aaec98e, 0x3a83126f, 0x3a44948c, 0x3a136a16, 0x39dd1725, 0x39a5cb60, 0x3978a815,
        0x393a7753, 0x390bd472]


def pack_vectors(inputs):
    cols = []
    for l in range(2):
        for key, name, n in VECS1 + VECS2:
            a = np.asarray(inputs[name])
            if key == "v0":
                a = a[0]
            else:
                a = a[l]
            a = a.reshape(-1)
            if a.size == 64:
                a = np.concatenate([a, a])
            if key == "mu":
                z = np.zeros(64, a.dtype)
                a = np.concatenate([a[0:1536], a[1536:1600], z, a[1600:1664], z, a[1664:1792]])
            assert a.size == 128 * n, name
            cols.append(a.reshape(n, 128).T)
    return np.ascontiguousarray(np.concatenate(cols, 1))


_WHOLE = ["positions", "positions_2", "w_in", "w_uq", "w_ukv", "w_o_mla", "w_o_sc", "w_o_cf", "gm_ln_g", "gm_ln_b", "gm_bs",
          "w_o_gm", "w_out", "w_ffn_in", "w_ffn_out", "w_in_2", "rwkv_w2_2", "rwkv_a2_2", "rwkv_g2_2", "rwkv_v1_2",
          "rwkv_v2_2", "w_branch_a_2", "w_branch_b_2", "w_out_2", "mem_wq_2", "mem_wkv_2", "mem_wo_2", "ffn_wg_2", "ffn_wu_2",
          "ffn_wd_2", "moe_router_2", "moe_bias_2", "moe_wg_2", "moe_wu_2", "moe_wd_2"]


def by_features(a):
    return np.ascontiguousarray(a.T.reshape(8, 128, 256).transpose(1, 0, 2).reshape(128, 2048))


def lay_out(inputs):
    arrays = {k: np.ascontiguousarray(inputs[k]) for k in _WHOLE}
    for k in ("positions", "positions_2"):
        arrays[k] = arrays[k].reshape(256)
    arrays["xT"] = by_features(np.asarray(inputs["x"])[0])
    arrays["memT"] = by_features(np.asarray(inputs["mem_2"])[0])
    arrays["gm_wsT"] = np.ascontiguousarray(np.asarray(inputs["gm_ws"]).transpose(0, 3, 1, 2).reshape(2, 128, 512))
    arrays["vecs"] = pack_vectors(inputs)
    arrays["cst"] = constants()
    return arrays


def kernel(**inputs):
    import concourse.bacc as bacc
    from concourse.bass_utils import run_bass_kernel_spmd

    nc = bacc.Bacc("TRN2", target_bir_lowering=False, num_devices=1, dynamic_dma_scratch_size=1024)
    arrays = lay_out(inputs)
    ins = {k: nc.dram_tensor("in_" + k, a.shape, mybir.dt.from_np(a.dtype), kind="ExternalInput").ap() for k, a in arrays.items()}
    out = nc.dram_tensor("out_x", (128, 2048), F32, kind="ExternalOutput").ap()
    build_program(nc, ins, out)
    r = run_bass_kernel_spmd(nc, [{"in_" + k: a for k, a in arrays.items()}], core_ids=[0])
    y = r.results[0]["out_x"].reshape(128, 8, 256)
    return np.ascontiguousarray(y.transpose(2, 1, 0).reshape(1, 256, 1024))
```

```python
import numpy as np
from contextlib import ExitStack
import concourse.bass as bass
from concourse import mybir

S = 256
F32 = mybir.dt.float32
F32R = mybir.dt.float32r
I32 = mybir.dt.int32
U32 = mybir.dt.uint32
ALU = mybir.AluOpType
ACT = mybir.ActivationFunctionType
AXX = mybir.AxisListType.X

VECS1 = [("nmp", "norm_mix_pre", 8), ("qn", "mla_q_norm", 2), ("kvn", "mla_kv_norm", 2), ("scw", "sc_conv_w", 12),
         ("cfw", "cf_conv_w", 124), ("cfb", "cf_conv_b", 4), ("clg", "cf_ln_g", 4), ("clb", "cf_ln_b", 4),
         ("gb", "gate_b", 32), ("npo", "norm_mix_post", 8), ("nfp", "norm_ffn_pre", 8), ("nfo", "norm_ffn_post", 8)]
VECS2 = [("nmix", "norm_mix_2", 8), ("mu", "rwkv_mu_2", 15), ("w0", "rwkv_w0_2", 4), ("a0", "rwkv_a0_2", 4),
         ("kk", "rwkv_kk_2", 4), ("ka", "rwkv_ka_2", 4), ("rk", "rwkv_rk_2", 4), ("lxg", "rwkv_lnx_g_2", 4),
         ("lxb", "rwkv_lnx_b_2", 4), ("dq", "dsa_q_norm_2", 1), ("dk", "dsa_k_norm_2", 1), ("di", "idx_k_norm_2", 1),
         ("nmem", "norm_mem_2", 8), ("mtok", "mem_tok_norm_2", 8), ("mq", "mem_q_norm_2", 1), ("mk", "mem_k_norm_2", 1),
         ("nffn", "norm_ffn_2", 8), ("v0", "rwkv_v0_2", 4)]
NVEC = 2 * (sum(n for _, _, n in VECS1) + sum(n for _, _, n in VECS2))
NCST = 10 * 128 + 256 + 256 + 64 + 8 + 4


def vec_offsets():
    off, at = {}, 0
    for l in range(2):
        for key, _, n in VECS1 + VECS2:
            off[key, l] = at
            at += n
    return off


def build_program(nc, ins, out):
    ctx = ExitStack()
    with ctx:
        build(nc, ctx, ins, out)


class Prog:

    def __init__(self, nc, ctx):
        self.nc, self.ctx = nc, ctx
        self.q = {e: [] for e in ("pe", "act", "dve", "pool", "sp")}
        self.n = {e: 0 for e in ("pe", "act", "dve", "pool")}
        self.sem = {e: ctx.enter_context(nc.semaphore("s_" + e)) for e in self.n}
        self.dn = {}
        self.bar = {e: [] for e in self.q}

    def put(self, eng, fn, *after):
        self.q[eng].append((self.bar[eng] + flat(after), fn, self.sem[eng], 1))
        self.bar[eng] = []
        self.n[eng] += 1
        return (eng, self.n[eng])

    def dma(self, slot, dst, src, *after, eng="sp"):
        key = "d_" + slot
        if key not in self.sem:
            self.sem[key] = self.ctx.enter_context(self.nc.semaphore(key))
            self.dn[key] = 0
        self.q[eng].append((flat(after), lambda e: e.dma_start(dst, src), self.sem[key], 16))
        self.dn[key] += 16
        return (key, self.dn[key])

    def reserve(self, eng):
        self.q[eng].append(None)
        self.n[eng] += 1
        return eng, len(self.q[eng]) - 1, (eng, self.n[eng])

    def fill(self, place, fn, *after):
        eng, at, _ = place
        self.q[eng][at] = (flat(after), fn, self.sem[eng], 1)

    def now(self):
        return [(e, n) for e, n in self.n.items() if n]

    def barrier(self):
        for e in self.n:
            self.bar[e] = self.now()

    def replay(self, eng, e):
        seen = {}
        for after, fn, sem, inc in self.q[eng]:
            for key, val in after:
                if seen.get(key, 0) < val:
                    e.wait_ge(self.sem[key], val)
                    seen[key] = val
            fn(e).then_inc(sem, inc)


def flat(ts):
    r = []
    for t in ts:
        if t is None:
            continue
        if isinstance(t, list):
            r += flat(t)
        else:
            r.append(t)
    return r


class Ring:

    def __init__(self, bufs):
        self.bufs, self.free, self.i = bufs, [None] * len(bufs), 0

    def take(self):
        n = len(self.bufs)
        i = next((j % n for j in range(self.i, self.i + n) if self.free[j % n] != "taken"), None)
        assert i is not None, "ring overrun"
        self.i = (i + 1) % n
        tok, self.free[i] = self.free[i], "taken"
        return i, self.bufs[i], tok

    def give(self, i, *tok):
        self.free[i] = flat(tok)


def build(nc, ctx, ins, out):
    P = Prog(nc, ctx)
    VO = vec_offsets()

    def sb(name, n, dt=F32):
        return nc.alloc_sbuf_tensor(name, [128, n], dt)

    def tt(eng, o, a, b, op, *dep):
        return P.put(eng, lambda e: e.tensor_tensor(o, a, b, op), *dep)

    def ts(eng, o, a, s1, s2, op0, op1, *dep):
        if s2 is None:
            return P.put(eng, lambda e: e.tensor_scalar(o, a, s1, None, op0), *dep)
        return P.put(eng, lambda e: e.tensor_scalar(o, a, s1, s2, op0, op1), *dep)

    def stt(eng, o, a, s, b, op0, op1, *dep):
        return P.put(eng, lambda e: e.scalar_tensor_tensor(out=o, in0=a, scalar=s, in1=b, op0=op0, op1=op1), *dep)

    def cp(eng, o, a, *dep):
        if eng == "act":
            return P.put("act", lambda e: e.activation(o, a, ACT.Copy), *dep)
        return P.put(eng, lambda e: e.tensor_copy(o, a), *dep)

    def act(o, a, f, *dep, bias=None, scale=1.0, acc=None):
        kw = {}
        if bias is not None:
            kw["bias"] = bias
        if acc is not None:
            kw["accum_out"] = acc
        return P.put("act", lambda e: e.activation(o, a, f, scale=scale, **kw), *dep)

    def mms(items, *dep):
        def fn(e):
            for o, l, r, st, sp in items:
                if r is None:
                    last = e.transpose(o, l, IDENT[0:l.shape[0], 0:l.shape[0]])
                else:
                    last = e.matmul(o, l, r, start=st, stop=sp)
            return last
        return P.put("pe", fn, *dep)

    MUL, ADD, SUB, MAX, MIN = ALU.mult, ALU.add, ALU.subtract, ALU.max, ALU.min

    SLOT, NRAW, NSPL, AHEAD = 1024, 3, 4, 2
    WF = Ring([sb(f"wf{i}", SLOT) for i in range(NRAW)])
    WH = [sb(f"wh{i}", SLOT, F32R) for i in range(NSPL)]
    WL = [sb(f"wl{i}", SLOT, F32R) for i in range(NSPL)]
    X = sb("X", 2048)
    HH = sb("HH", 2048, F32R)
    HL = sb("HL", 2048, F32R)
    VEC = sb("VEC", NVEC)
    CST = sb("CST", NCST)
    ROPE = sb("ROPE", 512)
    SC = sb("SC", 8 * 512)
    ST = sb("ST", 64)
    S8 = sb("S8", 32)
    IDLE = sb("IDLE", 8)
    RS = sb("RS", 4 * 48)
    ARENA = 31924
    arena = sb("arena", ARENA)
    arena_at = nc.sbuf_base - 4 * ARENA
    PS = [ctx.enter_context(nc.psum_tensor(f"ps{i}", [128, 512], F32)) for i in range(8)]
    Gb = Ring(PS[0:4])
    Ab = Ring(PS[4:8])
    Scr = Ring([SC[:, i * 512:(i + 1) * 512] for i in range(8)])
    Stat = Ring([ST[:, i * 4:(i + 1) * 4] for i in range(16)])

    def cst(i, n=128):
        return CST[:, i:i + n]

    IDENT, ONES, BONES = cst(0), cst(128), cst(256)
    ROT96, ROT64 = cst(384), cst(512)
    D16, D16T, C16, C32, CST64 = cst(640), cst(768), cst(896), cst(1024), cst(1152)
    MASKT = cst(1280, 256)
    SCM = cst(1536, 256)
    ID64 = cst(1792, 64)
    IOTA8 = cst(1856, 8)
    IF1, IF2 = cst(1864, 1), cst(1865, 1)

    x3 = X[:, :].rearrange("p (t s) -> p t s", s=S)
    h2 = [t[:, :].rearrange("p (t s) -> p t s", s=S) for t in (HH, HL)]

    def vec(key, l, i=0, n=1):
        o = VO[key, l] + i
        return VEC[:, o:o + n]

    placed = [0]

    def big(off, *shape, dt=F32):
        n = int(np.prod(shape))
        assert off + n <= ARENA, (off, shape)
        placed[0] += 1
        v = nc.alloc_sbuf_tensor_at(f"b{placed[0]}_{off}", [128, n], dt, offset=arena_at + 4 * off)[:, :]
        if len(shape) == 1:
            return v
        if len(shape) == 2:
            return v.rearrange("p (a b) -> p a b", b=shape[1])
        if len(shape) == 3:
            return v.rearrange("p (a b c) -> p a b c", b=shape[1], c=shape[2])
        return v.rearrange("p (a b c d) -> p a b c d", b=shape[1], c=shape[2], d=shape[3])

    def big2(off, *shape):
        n = int(np.prod(shape))
        return [big(off, *shape, dt=F32R), big(off + n, *shape, dt=F32R)]

    def bc(ap, n):
        return ap.unsqueeze(1).broadcast_to([ap.shape[0], n, ap.shape[-1]])

    t_vec = P.dma("vec", VEC[:, :], ins["vecs"])
    t_cst = P.dma("cst", CST[:, :], ins["cst"])
    t_x = P.dma("x", X[:, :], ins["xT"])
    t_c = [t_vec, t_cst]

    loaded = [0]
    places = []
    gave = [None] * NSPL

    def reserve_split():
        i = len(places)
        places.append((P.reserve("act"), P.reserve("pool" if i % 3 == 2 else "dve")))

    for _ in range(AHEAD):
        reserve_split()

    def take_w(src, m, n):
        i = loaded[0]
        loaded[0] += 1
        reserve_split()
        fi, buf, free = WF.take()
        v = buf[:, 0:m * n]
        tok = P.dma(f"w{fi}", v.rearrange("p (m n) -> p m n", n=n), src, free)
        z = i % NSPL
        hi, lo = WH[z][:, 0:m * n], WL[z][:, 0:m * n]
        (ph, pl) = places[i]
        P.fill(ph, lambda e: e.activation(hi, v, ACT.Copy), tok, gave[z])
        P.fill(pl, lambda e: e.tensor_tensor(lo, v, hi.bitcast(F32), ALU.subtract), tok, gave[z], ph[2])
        WF.give(fi, ph[2], pl[2])
        gave[z] = "taken"
        return z, hi, lo, [ph[2], pl[2]]

    def give_w(z, *tok):
        gave[z] = flat(tok)

    def products(out, stat, mov, first, last):
        return [(out, stat[0], mov[0], first, False), (out, stat[0], mov[1], False, False), (out, stat[1], mov[0], False, last)]

    def unit(arr, b0, m, k0, k1):
        return arr[b0:b0 + m, :, k0 * 128:k1 * 128].rearrange("b p n -> p b n"), m, (k1 - k0) * 128

    def chunks(kt):
        c = -(-kt // 8)
        cuts = [round(kt * i / c) for i in range(c + 1)]
        return list(zip(cuts, cuts[1:]))

    def gemm(banks, kt, rhs, dep, consume, ring=None):
        ring = ring or Gb
        byk = isinstance(dep, dict)
        wide = SLOT // (kt * 128) if kt <= 4 else 1
        for n, bank in enumerate(banks):
            bi, ps, free = ring.take()
            held = None
            for t, (arr, b) in enumerate(bank):
                for a0, a1 in chunks(kt):
                    b0 = b - b % wide
                    key = (id(arr), b0, a0)
                    if held is None or held[0] != key:
                        if held is not None:
                            give_w(held[1][0], tok)
                        held = (key, take_w(*unit(arr, b0, wide, a0, a1)))
                    z, hi, lo, wt = held[1]
                    o = (b - b0) * kt * 128
                    for g in ([(k, k + 1) for k in range(a0, a1)] if byk and n == 0 and t == 0 else [(a0, a1)]):
                        items = []
                        for k in range(*g):
                            c = slice(o + (k - a0) * 128, o + (k - a0 + 1) * 128)
                            items += products(ps[:, t * S:(t + 1) * S], (hi[:, c], lo[:, c]), rhs(k), k == 0, k == kt - 1)
                        tok = mms(items, wt, free, dep[g[0]] if byk else dep)
            give_w(held[1][0], tok)
            ring.give(bi, consume(n, ps, tok))
            yield

    def pairs(arr, b0, nb):
        return [[(arr, b) for b in range(i, min(i + 2, b0 + nb))] for i in range(b0, b0 + nb, 2)]

    def split(dst, src, dep, n=None, eng="pool"):
        a = P.put("act", lambda e: e.activation(dst[0], src, ACT.Copy), dep)
        b = P.put(eng, lambda e: e.tensor_tensor(dst[1], src, dst[0].bitcast(F32), ALU.subtract), dep, a)
        return [a, b]

    rs_last = [None]

    def rsqrt(dst, src, scale, eps, dep, w, final=1.0, floor=None):
        pp = src.shape[0]
        v, t = RS[0:pp, 0:w], RS[0:pp, 48:48 + w]
        y = RS[0:pp, 96:96 + w]
        if floor is None:
            k = ts("dve", v, src, float(scale), float(eps), MUL, ADD, dep, rs_last[0])
        else:
            k = ts("dve", v, src, float(floor), None, MAX, None, dep, rs_last[0])
        k = ts("dve", y.bitcast(I32), v.bitcast(I32), -0.5, float(0x5f3759df), MUL, ADD, k)
        for c in (3.0, 12.0):
            k = tt("dve", t, y, y, MUL, k)
            k = tt("dve", t, t, v, MUL, k)
            k = stt("dve", y, t, c, y, SUB, MUL, k)
        k = tt("dve", t, y, y, MUL, k)
        k = tt("dve", t, t, v, MUL, k)
        k = ts("dve", t, t, float(-final / 8192.0), float(final * 0.09375), MUL, ADD, k)
        k = tt("dve", dst, t, y, MUL, k)
        rs_last[0] = k
        return k

    def mean_rs(src, nt, scale, eps, dep, final=1.0):
        ai, pa, fa = Ab.take()
        bi, pb, fb = Ab.take()
        for t0 in range(0, nt, 2):
            si, sq, sfree = Scr.take()
            sqv = sq.rearrange("p (t s) -> p t s", s=S)
            a = act(sqv, src[:, t0:t0 + 2, :], ACT.Square, dep[t0:t0 + 2] if isinstance(dep, tuple) else dep, sfree)
            k = mms([(p[:, 0:1], sqv[:, u, b * 128:(b + 1) * 128], ONES[:, 0:1], t0 + u == 0, t0 + u == nt - 1)
                     for u in range(2) for b, p in enumerate((pa, pb))], a, fa, fb, t_c)
            Scr.give(si, k)
        si, r, sfree = Scr.take()
        c0 = cp("dve", r[:, 0:1], pa[:, 0:1], k, sfree)
        c1 = cp("dve", r[:, 1:2], pb[:, 0:1], k)
        Ab.give(ai, c0)
        Ab.give(bi, c1)
        k = rsqrt(r[:, 2:4], r[:, 0:2], scale, eps, [c0, c1], 2, final=final)
        ci, pc, fc = Ab.take()
        k = mms([(pc[:, b * 128:(b + 1) * 128], r[:, 2 + b:3 + b].broadcast_to([128, 128]), IDENT, True, True) for b in range(2)], k, fc)
        Scr.give(si, k)
        return ci, pc, k

    def head_rs(src, nt, scale, eps, dep, use, heads=2, floor=None):
        ai, pa, fa = Ab.take()
        w = heads
        ind = BONES[:, 63:65] if heads == 2 else ONES[:, 0:1]
        for t0 in range(0, nt, 2):
            m = min(2, nt - t0)
            si, sq, sfree = Scr.take()
            sqv = sq[:, 0:m * S].rearrange("p (t s) -> p t s", s=S)
            a = act(sqv, src[:, t0:t0 + m, :], ACT.Square, dep, sfree)
            k = mms([(pa[:, ((t0 + u) * 2 + b) * w:((t0 + u) * 2 + b + 1) * w], sqv[:, u, b * 128:(b + 1) * 128], ind, True, True)
                     for u in range(m) for b in range(2)], a, fa, t_c)
            Scr.give(si, k)
        si, r, sfree = Scr.take()
        n = nt * 2 * w
        k = rsqrt(r[:, 0:n], pa[:, 0:n], scale, eps, [k, sfree], n, floor=floor)
        Ab.give(ai, k)
        toks, last = [], None
        for t0 in range(0, nt, 2):
            m = min(2, nt - t0)
            bi, ps, free = Ab.take()
            items = []
            for u in range(m):
                for b in range(2):
                    c = ((t0 + u) * 2 + b) * w
                    g = 128 // w
                    items += [(ps[e * g:(e + 1) * g, u * S + b * 128:u * S + (b + 1) * 128], r[:, c + e:c + e + 1].broadcast_to([128, g]), IDENT, True, True)
                              for e in range(w)]
            last = mms(items, k, free)
            x = use(t0, m, ps[:, 0:m * S].rearrange("p (t s) -> p t s", s=S), last)
            Ab.give(bi, x)
            toks.append(x)
        Scr.give(si, last)
        return toks

    def rmsnorm(src, nt, gkey, l, dst, dep):
        ci, pc, k = mean_rs(src, nt, 1.0 / (128 * nt), 1e-6, dep)
        toks, last = {}, []
        for t in range(0, nt, 2):
            si, s, sfree = Scr.take()
            s3 = s.rearrange("p (t s) -> p t s", s=S)
            a = [stt("dve", s3[:, u, :], src[:, t + u, :], vec(gkey, l, t + u), pc[:, 0:S], MUL, MUL, k, dep, sfree, t_c) for u in range(2)]
            last += a
            x = split([d[:, t:t + 2, :] for d in dst], s3, a, eng="dve" if t % 4 == 0 else "pool")
            Scr.give(si, x)
            toks[t] = toks[t + 1] = x
        Ab.give(ci, last)
        return toks

    def residual_rms(m, gkey, l, dep, fac):
        ci, pc, k = mean_rs(m, 8, fac * fac / 1024, 1e-6, dep, final=fac)
        toks, last = [], []
        for t in range(8):
            a = stt("dve", m[:, t, :], m[:, t, :], vec(gkey, l, t), pc[:, 0:S], MUL, MUL, k, dep)
            last.append(a)
            toks.append(tt("pool" if t % 2 else "dve", x3[:, t, :], x3[:, t, :], m[:, t, :], ADD, a))
        Ab.give(ci, last)
        return toks

    def sigmoid_in(o, a, *dep, bias=None, eng="dve"):
        k = act(o, a, ACT.Tanh, *dep, bias=bias, scale=0.5)
        return ts(eng, o, o, 0.5, 0.5, MUL, ADD, k), k

    def attention(nh, q, kk, scale, v, dst, dv, dep, nks=(256, 256), pen=None, K=128, base=lambda h: 0, done=None):
        kept = {}
        for h in range(nh + 1):
            if h < nh:
                bi, ps, free = Ab.take()
                s3 = ps[:, :].rearrange("p (b s) -> p b s", s=S)
                t = mms([(s3[:, b, 0:nks[b]], q(h)[:, b * 128:(b + 1) * 128], kk(h)[:, 0:nks[b]], True, True) for b in range(2)],
                        dep, free)
                si, pr, sfree = Scr.take()
                p3 = pr.rearrange("p (b s) -> p b s", s=S)
                ti, st, tfree = Stat.take()
                ui, su, ufree = Stat.take()
                if pen is None:
                    m = P.put("dve", lambda e, o=st[:, 0:2], i=s3: e.reduce_max(o, i, AXX), t, tfree)
                    m = ts("dve", st[:, 2:4], st[:, 0:2], -float(scale), None, MUL, None, m)
                    ex = []
                    for b in range(2):
                        ex.append(act(p3[:, b, :], s3[:, b, :], ACT.Exp, m, sfree, ufree, bias=st[:, 2 + b:3 + b], scale=float(scale),
                                      acc=su[:, b:b + 1]))
                    Ab.give(bi, ex)
                else:
                    ms = [stt("dve", p3[:, b, 0:nks[b]], s3[:, b, 0:nks[b]], float(scale), pen(b), MUL, ADD, t, sfree, dep)
                          for b in range(2)]
                    Ab.give(bi, ms)
                    m = [P.put("dve", lambda e, o=st[:, b:b + 1], i=p3[:, b, 0:nks[b]]: e.reduce_max(o, i, AXX), ms[b], tfree)
                         for b in range(2)]
                    m = ts("dve", st[:, 2:4], st[:, 0:2], -1.0, None, MUL, None, m)
                    ex = []
                    for b in range(2):
                        ex.append(act(p3[:, b, 0:nks[b]], p3[:, b, 0:nks[b]], ACT.Exp, m, ufree, bias=st[:, 2 + b:3 + b],
                                      acc=su[:, b:b + 1]))
                rc = P.put("dve", lambda e, o=su[:, 2:4], i=su[:, 0:2]: e.reciprocal(o, i), ex)
                sc = [ts("dve", p3[:, b, 0:nks[b]], p3[:, b, 0:nks[b]], su[:, 2 + b:3 + b], None, MUL, None, rc) for b in range(2)]
                Stat.give(ti, ex)
                Stat.give(ui, sc)
                kept[h] = (si, p3, sc)
                yield
            if h > 0:
                g = h - 1
                si, p3, sc = kept.pop(g)
                bi, ps, free = Ab.take()
                tp = ps[:, :].rearrange("p (k s) -> p k s", s=S)
                todo = [(tp[:, kt, b * 128:(b + 1) * 128], p3[:, b, kt * 128:(kt + 1) * 128], None, True, True)
                        for b in range(2) for kt in range(nks[b] // 128)]
                t = mms(todo, sc, free, t_c)
                Scr.give(si, t)
                pi, pt, pfree = Scr.take()
                pt3 = pt.rearrange("p (k s) -> p k s", s=S)
                if nks[0] == 256:
                    c = [cp("act", pt, ps[:, :], t, pfree)]
                else:
                    c = [cp("act", pt3[:, 0, :], tp[:, 0, :], t, pfree), cp("act", pt3[:, 1, 128:256], tp[:, 1, 128:256], t, pfree)]
                Ab.give(bi, c)
                bi, ps, free = Ab.take()
                items = []
                if nks[0] == 256:
                    items = [(ps[0:dv, 0:S], v(g, kt), pt3[:, kt, :], kt == 0, kt == 1) for kt in range(2)]
                else:
                    items = [(ps[0:dv, 0:128], v(g, 0), pt3[:, 0, 0:128], True, True),
                             (ps[0:dv, 128:256], v(g, 0), pt3[:, 0, 128:256], True, False),
                             (ps[0:dv, 128:256], v(g, 1), pt3[:, 1, 128:256], False, True)]
                t = mms(items, c, free, dep)
                Scr.give(pi, t)
                c = cp("dve", dst(g), ps[0:dv, 0:S], t)
                Ab.give(bi, c)
                done.append(c)
                yield

    def run(g):
        for _ in g:
            pass

    def interleave(gens, weights):
        gens = [[g, w, 0.0] for g, w in zip(gens, weights)]
        while gens:
            gens.sort(key=lambda a: a[2])
            a = gens[0]
            try:
                next(a[0])
                a[2] += a[1]
            except StopIteration:
                gens.pop(0)

    TWO_PI = 2 * np.pi
    C1 = 6.28125
    C2 = float(np.float32(np.round((TWO_PI - C1) * 2**20) / 2**20))
    C3 = float(TWO_PI - C1 - C2)
    MAGIC = 12582912.0

    def rope_tables(key, pos, freq):
        si, sc, sf = Scr.take()
        ki, kk2, kf = Scr.take()
        pi = sc[:, 0:S].bitcast(I32)
        t = P.dma("pos", pi, pos.partition_broadcast(128), sf, kf, P.now(), eng="act")
        ang, kx = sc[:, 256:512], kk2[:, 0:S]
        a = ts("dve", ang, pi, freq, None, MUL, None, t, t_c)
        r = []
        for j, (shift, add) in enumerate(((0.25, np.pi / 2), (0.0, 0.0))):
            o = ROPE[:, j * S:(j + 1) * S]
            k = ts("dve", kx, ang, float(1 / TWO_PI), float(shift), MUL, ADD, a)
            k = ts("dve", kx, kx, MAGIC, None, ADD, None, k)
            k = ts("dve", kx, kx, -MAGIC, None, ADD, None, k)
            k = stt("dve", o, kx, -C1, ang, MUL, ADD, k)
            k = stt("dve", o, kx, -C2, o, MUL, ADD, k)
            a = k = stt("dve", o, kx, -C3, o, MUL, ADD, k)
            k = ts("dve", o, o, float(add), None, ADD, None, k)
            k = ts("dve", o, o, 3.1415925, -3.1415925, MIN, MAX, k)
            r.append(act(o, o, ACT.Sin, k))
        Scr.give(si, a)
        Scr.give(ki, a)
        return r

    t_rope = [rope_tables(0, ins["positions"], IF1)]
    xdep = [t_x]


    def block1_mix(l):
        P.barrier()
        wa, wb, wkr, w_uq, w_ukv = ins["w_in_a"][l], ins["w_in_b"][l], ins["w_kr"][l], ins["w_uq"][l], ins["w_ukv"][l]
        G = big(0, 32, S)
        CP2 = big2(8192, 4, S)
        C = big(10240, 4, S)
        QT = big(11264, 8, S)
        KT = big(13312, 8, S)
        V = big(15360, 2, 512)
        O = big(16384, 4, S)
        Bc = big(17408, 4, S)
        CA = big(18432, 4, 288)
        ZS = big(19584, 4, 258)
        CY = big(20616, 4, S)
        GU = big(21640, 4, S)
        GV = big(22664, 2, 512)
        GR = big(23688, 1536)
        WS = big(25224, 512)
        BcS, GUS, CYS = big2(25736, 4, S), big2(27784, 4, S), big2(29832, 4, S)
        now = P.now()
        t_gr = [P.dma("gr0", GR[:, 0:512], ins["gm_ln_g"][l].partition_broadcast(128), now, eng="act"),
                P.dma("gr1", GR[:, 512:1024], ins["gm_ln_b"][l].partition_broadcast(128), now, eng="act"),
                P.dma("gr2", GR[:, 1024:1536], ins["gm_bs"][l].rearrange("g t -> (g t)").partition_broadcast(128), now, eng="act")]
        t_ws = P.dma("ws", WS[:, :], ins["gm_wsT"][l], now, eng="act")
        cos1, sin1 = ROPE[:, 0:S], ROPE[:, S:2 * S]

        hd = rmsnorm(x3, 8, "nmp", l, h2, xdep)
        rhs = lambda k: (h2[0][:, k, :], h2[1][:, k, :])
        hall = list(hd.values())
        yield
        cdone = []

        def put_c(dst, t0):
            def f(n, ps, tok):
                c = cp("act", dst[:, t0 + 2 * n:t0 + 2 * n + 2, :], ps[:, :].rearrange("p (t s) -> p t s", s=S), tok)
                cdone.append(c)
                return c
            return f
        yield from gemm(pairs(wa, 0, 4), 8, rhs, hd, put_c(C, 0))
        cq = rmsnorm(C[:, 0:2, :], 2, "qn", l, [x[:, 0:2, :] for x in CP2], cdone)[0]
        ck = rmsnorm(C[:, 2:4, :], 2, "kvn", l, [x[:, 2:4, :] for x in CP2], cdone)[0]
        ki, kr, kfree = Scr.take()
        kk1 = []

        def put_kr(n, ps, tok):
            kk1.append(cp("act", kr[0:96, 0:S], ps[0:96, 0:S], tok, kfree))
            return kk1[-1]
        yield from gemm([[(wkr, 0)]], 8, rhs, hall, put_kr)
        bi, ps, free = Gb.take()
        t = mms([(ps[0:96, S:2 * S], ROT96[0:96, 0:96], kr[0:96, 0:S], True, True)], kk1, free)
        b1 = tt("dve", kr[64:96, 0:S], kr[64:96, 0:S], cos1[64:96, :], MUL, t, t_rope)
        b2 = tt("dve", kr[64:96, S:2 * S], ps[64:96, S:2 * S], sin1[64:96, :], MUL, t)
        Gb.give(bi, b2)
        kdone = [tt("dve", KT[64:96, :, :], bc(kr[64:96, 0:S], 8), bc(kr[64:96, S:2 * S], 8), ADD, b1, b2)]
        Scr.give(ki, kdone)
        yield

        zc = P.put("pool", lambda e: e.memset(CA[:, :, :], 0.0))
        zs = P.put("pool", lambda e: e.memset(ZS[:, :, :], 0.0))
        az = []

        def put_a(n, ps, tok):
            c = cp("act", CA[:, 2 * n:2 * n + 2, 15:271], ps[:, :].rearrange("p (t s) -> p t s", s=S), tok, zc)
            az.append(c)
            return c

        def put_g(n, ps, tok):
            si, s, sf = Scr.take()
            a = act(s, ps[:, :], ACT.Tanh, tok, sf, scale=0.5)
            b = ts("dve", s, s, 0.5, 0.5, MUL, ADD, a)
            c = tt("dve", CA[:, 2 * n:2 * n + 2, 15:271], CA[:, 2 * n:2 * n + 2, 15:271], s.rearrange("p (t s) -> p t s", s=S), MUL, b, az[n])
            az[n] = c
            Scr.give(si, c)
            return a
        yield from gemm(pairs(wb, 12, 4), 8, rhs, hall, put_a)
        yield from gemm(pairs(wb, 16, 4), 8, rhs, hall, put_g)

        last = {}

        def conv():
            for t in range(4):
                last[t] = ts("dve", CY[:, t, :], CA[:, t, 0:S], vec("cfw", l, t), vec("cfb", l, t), MUL, ADD, az)
            yield
            for k in range(1, 31):
                for t in range(4):
                    last[t] = stt("dve", CY[:, t, :], CA[:, t, k:k + S], vec("cfw", l, 4 * k + t), CY[:, t, :], MUL, ADD, last[t])
                yield
            toks = list(last.values())
            bi, ps, free = Ab.take()
            m = mms([(ps[:, 0:S], ONES, CY[:, t, :], t == 0, t == 3) for t in range(4)], toks, free)
            si, s, sf = Scr.take()
            mean = ts("dve", s[:, 0:S], ps[:, 0:S], 1.0 / 512, None, MUL, None, m, sf)
            Ab.give(bi, mean)
            cen = [tt("dve", CY[:, 2 * i:2 * i + 2, :], CY[:, 2 * i:2 * i + 2, :], bc(s[:, 0:S], 2), SUB, mean, toks) for i in range(2)]
            yield
            ci, pc, k = mean_rs(CY, 4, 1.0 / 512, 1e-6, cen)
            yield
            fin, nrm, out2 = [], [], []
            for p in range(2):
                a = tt("dve", CY[:, 2 * p:2 * p + 2, :], CY[:, 2 * p:2 * p + 2, :], bc(pc[:, 0:S], 2), MUL, k)
                nrm.append(a)
                ti, th, tf = Scr.take()
                z3 = CY[:, 2 * p:2 * p + 2, :]
                a = [ts("dve", CY[:, t, :], CY[:, t, :], vec("clg", l, t), vec("clb", l, t), MUL, ADD, a) for t in (2 * p, 2 * p + 1)]
                t3 = th.rearrange("p (t s) -> p t s", s=S)
                b = act(t3, z3, ACT.Tanh, a, tf, scale=0.5)
                b = stt("dve", z3, t3, 1.0, z3, ADD, MUL, b)
                b = ts("dve", z3, z3, 0.5, None, MUL, None, b)
                Scr.give(ti, b)
                fin.append(b)
                out2.append(split([x[:, 2 * p:2 * p + 2, :] for x in CYS], z3, b))
                yield
            Ab.give(ci, nrm)
            Scr.give(si, fin)
            last["y"] = out2

        def gelu(dst, src, w, tok, free):
            si, s, sf = Scr.take()
            a = act(s[:, 0:w], src, ACT.Square, tok, sf)
            a = ts("dve", s[:, 0:w], s[:, 0:w], 0.044715, 1.0, MUL, ADD, a)
            a = tt("dve", s[:, 0:w], s[:, 0:w], src, MUL, a)
            a = act(s[:, 0:w], s[:, 0:w], ACT.Tanh, a, scale=float(np.sqrt(2 / np.pi)))
            a = stt("dve", s[:, 0:w], s[:, 0:w], 1.0, src, ADD, MUL, a)
            b = ts("pool", dst, s[:, 0:w], 0.5, None, MUL, None, a, free)
            Scr.give(si, b)
            return a, b

        def main():
            qdone, vdone = [], []
            cqs = lambda k: (CP2[0][:, k, :], CP2[1][:, k, :])

            def put_q(p, ps, t):
                b2i, ps2, free2 = Ab.take()
                qv = QT[0:96, 2 * p:2 * p + 2, :]
                a = cp("act", qv, ps[0:96, :].rearrange("p (t s) -> p t s", s=S), t)
                m = mms([(ps2[0:96, :], ROT96[0:96, 0:96], qv, True, True)], a, free2)
                si, s, sf = Scr.take()
                qr = QT[64:96, 2 * p:2 * p + 2, :]
                s3 = s[64:96, :].rearrange("p (t s) -> p t s", s=S)
                b = tt("dve", qr, qr, bc(cos1[64:96, :], 2), MUL, m)
                c = tt("dve", s3, ps2[64:96, :].rearrange("p (t s) -> p t s", s=S), bc(sin1[64:96, :], 2), MUL, m, sf)
                Ab.give(b2i, c)
                d = tt("dve", qr, qr, s3, ADD, b, c)
                Scr.give(si, d)
                qdone.append(d)
                return a
            yield from gemm(pairs(w_uq, 0, 8), 2, cqs, cq, put_q)

            def put_k(p, ps, t):
                a = cp("act", KT[0:64, 2 * p:2 * p + 2, :], ps[0:64, :].rearrange("p (t s) -> p t s", s=S), t)
                kdone.append(a)
                return a
            yield from gemm(pairs(w_ukv, 0, 8), 2, lambda k: cqs(k + 2), ck, put_k)
            bks = [Gb.take() for _ in range(2)]
            for g in range(2):
                z, hi, lo, wt = take_w(*unit(w_ukv, 4 * g, 4, 0, 2))
                for tb in range(2):
                    items = []
                    for h in range(4):
                        for k in range(2):
                            c = slice(h * 256 + k * 128 + 64, h * 256 + k * 128 + 128)
                            items += products(bks[tb][1][:, (4 * g + h) * 64:(4 * g + h + 1) * 64],
                                              [x[:, tb * 128:(tb + 1) * 128] for x in cqs(k + 2)], (hi[:, c], lo[:, c]), k == 0, k == 1)
                    t = mms(items, ck, wt, bks[tb][2])
                    if g:
                        a = cp("act", V[:, tb, :], bks[tb][1][:, :], t)
                        Gb.give(bks[tb][0], a)
                        vdone.append(a)
                give_w(z, t)
            yield
            odone = []
            o = lambda h: O[(h % 2) * 64:(h % 2) * 64 + 64, h // 2, :]
            yield from attention(8, lambda h: QT[0:96, h, :], lambda h: KT[0:96, h, :], 96 ** -0.5,
                                 lambda h, kt: V[:, kt, h * 64:(h + 1) * 64], o, 64, [qdone, kdone, vdone], done=odone)
            last["o"] = split(CP2, O, [odone, vdone, qdone, kdone])

        def rest():
            bd, cd = [], []

            def put_b(n, ps, tok):
                c = cp("act", Bc[:, 2 * n:2 * n + 2, :], ps[:, :].rearrange("p (t s) -> p t s", s=S), tok)
                bd.append(c)
                return c

            def put_cc(n, ps, tok):
                c = cp("act", ZS[:, 2 * n:2 * n + 2, 1:257], ps[:, :].rearrange("p (t s) -> p t s", s=S), tok, zs)
                cd.append(c)
                return c

            def put_x(n, ps, tok):
                z = ZS[:, 2 * n:2 * n + 2, 1:257]
                c = tt("dve", z, ps[:, :].rearrange("p (t s) -> p t s", s=S), z, MUL, tok, cd[n])
                cd[n] = c
                return c
            yield from gemm(pairs(wb, 0, 4), 8, rhs, hall, put_b)
            yield from gemm(pairs(wb, 4, 4), 8, rhs, hall, put_cc)
            yield from gemm(pairs(wb, 8, 4), 8, rhs, hall, put_x)
            sd = []
            for t in range(4):
                si, s, sf = Scr.take()
                y = s[:, 0:S]
                a = ts("dve", y, ZS[:, t, 0:S], vec("scw", l, t), None, MUL, None, cd, sf)
                a = stt("dve", y, ZS[:, t, 1:257], vec("scw", l, 4 + t), y, MUL, ADD, a)
                a = stt("dve", y, ZS[:, t, 2:258], vec("scw", l, 8 + t), y, MUL, ADD, a)
                a = tt("pool", Bc[:, t, :], Bc[:, t, :], y, MUL, a, bd)
                Scr.give(si, a)
                sd.append(a)
            last["s"] = split(BcS, Bc, sd)
            yield
            ud, vd = [], []

            def put_u(n, ps, tok):
                a, b = gelu(GU[:, 2 * n:2 * n + 2, :].rearrange("p t s -> p (t s)"), ps[:, :], 512, tok, None)
                ud.append(b)
                return a
            yield from gemm(pairs(wb, 20, 4), 8, rhs, hall, put_u)
            bks = [Gb.take() for _ in range(2)]
            tks = [None, None]
            for g in range(4):
                z, hi, lo, wt = take_w(*unit(wb, 24 + g, 1, 0, 8))
                for tb in range(2):
                    items = []
                    for k in range(8):
                        c = slice(k * 128, (k + 1) * 128)
                        items += products(bks[tb][1][:, g * 128:(g + 1) * 128], [x[:, tb * 128:(tb + 1) * 128] for x in rhs(k)],
                                          (hi[:, c], lo[:, c]), k == 0, k == 7)
                    tks[tb] = mms(items, hall, wt, bks[tb][2])
                give_w(z, tks)
            for tb in range(2):
                bi, ps, t = bks[tb][0], bks[tb][1], tks[tb]
                gv = GV[:, tb, :]
                a, b = gelu(gv, ps[:, :], 512, t, None)
                Gb.give(bi, a)
                ti, st, tf = Stat.take()
                t2, st2, tf2 = Stat.take()
                si, s, sf = Scr.take()
                c = P.put("dve", lambda e, o=s[:, 0:6], i=gv: e.bn_stats(o, i), b, sf)
                c = P.put("dve", lambda e, o=st[:, 0:2], i=s[:, 0:6]: e.bn_aggr(o, i), c, tf)
                Scr.give(si, c)
                c = rsqrt(st2[:, 0:1], st[:, 1:2], 1.0, 1e-6, [c, tf2], w=1)
                d = ts("dve", gv, gv, st[:, 0:1], st2[:, 0:1], SUB, MUL, c)
                d = tt("dve", gv, gv, GR[:, 0:512], MUL, d, t_gr)
                d = tt("dve", gv, gv, GR[:, 512:1024], ADD, d)
                Stat.give(ti, d)
                Stat.give(t2, d)
                vd.append(d)
                yield
            gd = []
            for g in range(4):
                bi, ps, free = Ab.take()
                t = mms([(ps[:, n * 128:(n + 1) * 128], GV[:, n, g * 128:(g + 1) * 128], WS[:, g * 128:(g + 1) * 128], True, True)
                         for n in range(2)], vd, t_ws, free)
                si, s, sf = Scr.take()
                a = tt("dve", s[:, 0:S].rearrange("p (n t) -> p n t", n=2), ps[:, 0:S].rearrange("p (n t) -> p n t", n=2),
                       bc(GR[:, 1024 + g * 128:1024 + (g + 1) * 128], 2), ADD, t, sf, t_gr)
                Ab.give(bi, a)
                a = tt("pool", GU[:, g, :], GU[:, g, :], s[:, 0:S], MUL, a, ud)
                Scr.give(si, a)
                gd.append(a)
            last["g"] = split(GUS, GU, gd)
            yield

            gi, hb, gf = Scr.take()
            hbt = ts("dve", hb[:, 0:32], vec("gb", l, 0, 32), 0.5, None, MUL, None, gf, t_c)
            gates = []

            def put_gate(n, ps, tok):
                r = [act(G[:, 2 * n + u, :], ps[:, u * S:(u + 1) * S], ACT.Tanh, tok, hbt, bias=hb[:, 2 * n + u:2 * n + u + 1], scale=0.5)
                     for u in range(2)]
                gates.append(r)
                return r
            yield from gemm(pairs(wb, 28, 32), 8, rhs, hall, put_gate)
            Scr.give(gi, gates)
            last["gates"] = gates

        interleave([main(), rest(), conv()], [1.0, 1.0, 1.6])

        M = big(11264, 8, S)
        M2 = big2(13312, 8, S)
        mt = {}
        for b, (src, key, W) in enumerate(((BcS, "s", "w_o_sc"), (GUS, "g", "w_o_gm"), (CYS, "y", "w_o_cf"), (CP2, "o", "w_o_mla"))):
            gb = {"s": 1, "g": 3, "y": 2, "o": 0}[key]

            def put_m(n, ps, tok, b=b, gb=gb):
                mv = M[:, 2 * n:2 * n + 2, :].rearrange("p t s -> p (t s)")
                gv = G[:, 8 * gb + 2 * n:8 * gb + 2 * n + 2, :].rearrange("p t s -> p (t s)")
                if b == 0:
                    a = stt("dve", mv, gv, 1.0, ps[:, :], ADD, MUL, tok, last["gates"], last["o"])
                    mt[n] = a
                    return a
                si, s, sf = Scr.take()
                a = stt("dve", s, gv, 1.0, ps[:, :], ADD, MUL, tok, sf)
                mt[n] = tt("pool", mv, mv, s, ADD, a, mt[n])
                Scr.give(si, mt[n])
                if b == 3:
                    mt[n] = split([x[:, 2 * n:2 * n + 2, :] for x in M2], M[:, 2 * n:2 * n + 2, :], mt[n])
                return a
            yield from gemm(pairs(ins[W][l], 0, 8), 4, lambda k, src=src: (src[0][:, k, :], src[1][:, k, :]), last[key], put_m)
        Y = big(0, 8, S)
        yd = []

        def put_y(n, ps, tok):
            a = cp("act", Y[:, 2 * n:2 * n + 2, :].rearrange("p t s -> p (t s)"), ps[:, :], tok, gread)
            yd.append(a)
            return a
        gread = list(mt.values())
        md = {k: mt[k // 2] for k in range(8)}
        yield from gemm(pairs(ins["w_out"][l], 0, 8), 8, lambda k: (M2[0][:, k, :], M2[1][:, k, :]), md, put_y)
        xdep[:] = residual_rms(Y, "npo", l, yd, 0.5)

    def ffn_up(Wg, Wu, nt, F2, hd, rdy, gate=None):
        fd = {}

        def put_f(n, ps, tok):
            si, s, sf = Scr.take()
            t = act(s[:, 0:S], ps[:, 0:S], ACT.Tanh, tok, sf, scale=0.5)
            a = stt("dve", s[:, S:2 * S], s[:, 0:S], 1.0, ps[:, 0:S], ADD, MUL, t)
            if gate is not None:
                a = tt("pool", s[:, S:2 * S], s[:, S:2 * S], gate, MUL, a, rdy)
            b = stt("dve", s[:, 0:S], ps[:, S:2 * S], 0.5, s[:, S:2 * S], MUL, MUL, a)
            fd[n] = split([x[:, n, :] for x in F2], s[:, 0:S], [b, rdy])
            Scr.give(si, fd[n])
            return b
        yield from gemm([[(Wg, j), (Wu, j)] for j in range(nt)], 8, lambda k: (h2[0][:, k, :], h2[1][:, k, :]), hd, put_f)
        return fd

    def block1_ffn(l):
        P.barrier()
        hd = rmsnorm(x3, 8, "nfp", l, h2, xdep)
        F2 = big2(0, 22, S)
        fd = yield from ffn_up(ins["w_ffn_g"][l], ins["w_ffn_u"][l], 22, F2, hd, None)
        Y = big(11264, 8, S)
        yd = []

        def put_y(n, ps, tok):
            a = cp("act", Y[:, 2 * n:2 * n + 2, :].rearrange("p t s -> p (t s)"), ps[:, :], tok)
            yd.append(a)
            return a
        yield from gemm(pairs(ins["w_ffn_out"][l], 0, 8), 22, lambda k: (F2[0][:, k, :], F2[1][:, k, :]), fd, put_y)
        xdep[:] = residual_rms(Y, "nfo", l, yd, 1.0)

    def add_x(n, ps, tok, fac=1.0):
        v = x3[:, 2 * n:2 * n + 2, :].rearrange("p t s -> p (t s)")
        a = stt("dve", v, ps[:, :], fac, v, MUL, ADD, tok)
        xnew.append(a)
        return a

    xnew = []
    WT2 = [0.5, 1.0, 4.0]

    vf3 = big(21920, 4, S)

    def block2_mix(l):
        P.barrier()
        w_in = ins["w_in_2"][l]
        if l == 0:
            t_rope[0] = rope_tables(1, ins["positions_2"], IF2)
        SW = big(19744, 2176)
        now = P.now()
        ld = [P.dma("sw0", SW[0:64, 0:512], ins["rwkv_w2_2"][l], now, eng="act"),
              P.dma("sw1", SW[0:64, 512:1024], ins["rwkv_a2_2"][l], now, eng="act"),
              P.dma("sw2", SW[:, 1024:1536], ins["rwkv_g2_2"][l], now, eng="act")]
        if l:
            ld += [P.dma("sw3", SW[:, 1536:1664].rearrange("p (k n) -> p k n", n=32),
                         ins["rwkv_v1_2"][l - 1].rearrange("(k p) n -> p k n", p=128), now, eng="act"),
                   P.dma("sw4", SW[0:32, 1664:2176], ins["rwkv_v2_2"][l - 1], now, eng="act")]
        hd = rmsnorm(x3, 8, "nmix", l, h2, xdep)
        rhs = lambda k: (h2[0][:, k, :], h2[1][:, k, :])
        hall = list(hd.values())
        yield
        CS = big(0, 15, S)
        CP = big(3840, 15, 257)
        zc = P.put("pool", lambda e: e.memset(CP[:, :, 0:1], 0.0))
        cd = []

        def put_p(n, ps, tok):
            a = cp("act", CP[:, 2 * n:2 * n + 2, 1:257], ps[:, :].rearrange("p (t s) -> p t s", s=S), tok)
            cd.append(a)
            return a
        yield from gemm(pairs(w_in, 0, 12), 8, rhs, hd, put_p)

        def put_q(n, ps, tok):
            cd.append([cp("act", CP[0:64, 12 + u, 1:257], ps[64 * u:64 * u + 64, 0:S], tok) for u in range(2)])
            return cd[-1]

        def put_r(n, ps, tok):
            a = cp("act", CP[:, 14, 1:257], ps[:, 0:S], tok)
            cd.append(a)
            return a
        yield from gemm([[(w_in, 12)]], 8, rhs, hall, put_q)
        yield from gemm([[(w_in, 13)]], 8, rhs, hall, put_r)
        md = []
        for t0, t1, pp in ((0, 12, 128), (12, 14, 64), (14, 15, 128)):
            a = tt("dve", CS[0:pp, t0:t1, :], CP[0:pp, t0:t1, 0:S], CP[0:pp, t0:t1, 1:257], SUB, cd, zc)
            for t in range(t0, t1):
                md.append(stt("dve", CS[0:pp, t, :], CS[0:pp, t, :], vec("mu", l, t)[0:pp, :], CP[0:pp, t, 1:257], MUL, ADD, a))
        yield
        r3, k3, v3 = CS[:, 0:4, :], CS[:, 4:8, :], CS[:, 8:12, :]
        LW, CUM, AA, GG, KK, BB = (big(3840 + 1024 * i, 4, S) for i in range(6))
        AR = big(9984, 4, 2, 2, 128)
        BT, KTl, BH, KH, Y = (big(12032 + 1024 * i, 4, S) for i in range(5))
        RP = big(17152, 4, S)
        MN = big(18176, 4, 3, 128)
        PC = big(19712, 4, 4)
        DA = big(22944, 10, S)
        V2 = big(25504, 2, 64)
        IW = big(25632, 2, 8)
        SCO, WKX, PEN = (big(25648 + 384 * i, 384) for i in range(3))
        O = big(26800, 4, S)
        GT = big(27824, 16, S)
        YAs, Os = big2(12032, 4, S), big2(14080, 4, S)
        ya = []

        def rwkv():
            si, tw, sf = Scr.take()
            a = act(tw[0:64, 0:S], CS[0:64, 12, :], ACT.Tanh, md, sf)
            g1 = act(tw[:, S:2 * S], CS[:, 14, :], ACT.Tanh, md, scale=0.5)
            g1 = ts("dve", tw[:, S:2 * S], tw[:, S:2 * S], 0.5, 0.5, MUL, ADD, g1)
            hi, hbv, hf = Scr.take()
            hb = ts("dve", hbv[:, 0:4], vec("w0", l, 0, 4), 0.5, None, MUL, None, hf, t_c)
            hb = ts("dve", hbv[:, 4:8], vec("a0", l, 0, 4), 0.5, None, MUL, None, hb)
            if l:
                hb = ts("dve", hbv[:, 8:12], vec("v0", l, 0, 4), 0.5, None, MUL, None, hb)
            hb = ts("dve", hbv[:, 12:16], vec("ka", l, 0, 4), -1.0, 1.0, MUL, ADD, hb)
            cde = float(np.exp(-0.5) / 2)
            lw, aa, gg = [], [], []
            for p in range(2):
                bi, ps, free = Ab.take()
                t = mms([(ps[:, u * S:(u + 1) * S], SW[0:64, (2 * p + u) * 128:(2 * p + u + 1) * 128], tw[0:64, 0:S], True, True) for u in range(2)], a, ld, free)
                ac = [act(LW[:, 2 * p + u, :], ps[:, u * S:(u + 1) * S], ACT.Tanh, t, hb, md, bias=hbv[:, 2 * p + u:2 * p + u + 1], scale=0.5) for u in range(2)]
                Ab.give(bi, ac)
                lw.append(ts("dve", LW[:, 2 * p:2 * p + 2, :], LW[:, 2 * p:2 * p + 2, :], -cde, -cde, MUL, ADD, ac))
                bi, ps, free = Ab.take()
                t2 = mms([(ps[:, u * S:(u + 1) * S], SW[0:64, 512 + (2 * p + u) * 128:512 + (2 * p + u + 1) * 128], CS[0:64, 13, :], True, True) for u in range(2)], md, ld, free)
                ac = [act(AA[:, 2 * p + u, :], ps[:, u * S:(u + 1) * S], ACT.Tanh, t2, hb, bias=hbv[:, 4 + 2 * p + u:5 + 2 * p + u], scale=0.5) for u in range(2)]
                Ab.give(bi, ac)
                aa.append(ts("dve", AA[:, 2 * p:2 * p + 2, :], AA[:, 2 * p:2 * p + 2, :], 0.5, 0.5, MUL, ADD, ac))
                bi, ps, free = Ab.take()
                t3 = mms([(ps[:, u * S:(u + 1) * S], SW[:, 1024 + (2 * p + u) * 128:1024 + (2 * p + u + 1) * 128], tw[:, S:2 * S], True, True) for u in range(2)], g1, ld, free)
                gg.append(cp("act", GG[:, 2 * p:2 * p + 2, :].rearrange("p t s -> p (t s)"), ps[:, :], t3, md))
                Ab.give(bi, gg[-1])
                yield
            Scr.give(si, t2, t3)
            if l == 0:
                vdep = [cp("pool", vf3, v3, md)]
            else:
                bi, ps, free = Ab.take()
                t = mms([(ps[0:32, 0:S], SW[:, 1536 + 32 * k:1568 + 32 * k], v3[:, k, :], k == 0, k == 3) for k in range(4)], md, ld, free)
                si, s, sf = Scr.take()
                c = cp("act", s[0:32, 0:S], ps[0:32, 0:S], t, sf)
                Ab.give(bi, c)
                vdep = []
                df = tt("dve", vf3, vf3, v3, SUB, md)
                for p in range(2):
                    bi, ps, free = Ab.take()
                    t = mms([(ps[:, u * S:(u + 1) * S], SW[0:32, 1664 + (2 * p + u) * 128:1664 + (2 * p + u + 1) * 128], s[0:32, 0:S], True, True) for u in range(2)], c, ld, free)
                    di, d, df2 = Scr.take()
                    ac = [act(d[:, u * S:(u + 1) * S], ps[:, u * S:(u + 1) * S], ACT.Tanh, t, hb, df2, bias=hbv[:, 8 + 2 * p + u:9 + 2 * p + u], scale=0.5) for u in range(2)]
                    Ab.give(bi, ac)
                    x = ts("dve", d, d, 0.5, 0.5, MUL, ADD, ac)
                    x = tt("dve", d, d, vf3[:, 2 * p:2 * p + 2, :].rearrange("p t s -> p (t s)"), MUL, x, df)
                    vp = v3[:, 2 * p:2 * p + 2, :].rearrange("p t s -> p (t s)")
                    x = tt("dve", vp, vp, d, ADD, x)
                    Scr.give(di, x)
                    vdep.append(x)
                Scr.give(si, t)
                yield
            kt = [ts("dve", KK[:, t, :], k3[:, t, :], vec("kk", l, t), None, MUL, None, md) for t in range(4)]
            kn = head_rs(KK, 4, 1.0, 0.0, kt, lambda t0, m, ps3, tok: tt("dve", KK[:, t0:t0 + m, :], KK[:, t0:t0 + m, :], ps3, MUL, tok),
                         floor=1e-24)
            yield
            k2 = []
            for t in range(4):
                c = ts("dve", BT[:, t, :], AA[:, t, :], vec("ka", l, t), hbv[:, 12 + t:13 + t], MUL, ADD, aa, hb)
                k2.append(tt("dve", k3[:, t, :], k3[:, t, :], BT[:, t, :], MUL, c, kt))
            Scr.give(hi, k2, lw, aa)
            bb = tt("dve", BB[:, :, :], KK[:, :, :], AA[:, :, :], MUL, kn, aa)
            cu = []
            for t in range(4):
                cu.append(P.put("dve", lambda e, t=t: e.tensor_tensor_scan(CUM[:, t, :], SCM, LW[:, t, :], 0.0, MUL, ADD), lw, t_c))
            yield
            e1 = tt("dve", LW[:, :, :], CUM[:, :, :], LW[:, :, :], SUB, cu)
            e1 = act(LW[:, :, :], LW[:, :, :], ACT.Exp, e1)
            a1 = stt("dve", AR[:, :, :, 0, :], KK[:, :, :].rearrange("p t (b s) -> p t b s", s=128), -1.0,
                     LW[:, :, :].rearrange("p t (b s) -> p t b s", s=128), MUL, MUL, e1, kn)
            e2 = act(LW[:, :, :], CUM[:, :, :], ACT.Exp, a1, cu)
            a2 = tt("dve", AR[:, :, :, 1, :], r3.rearrange("p t (b s) -> p t b s", s=128), LW[:, :, :].rearrange("p t (b s) -> p t b s", s=128), MUL, e2, md)
            cl = CUM[:, :, :].rearrange("p t (c s) -> p t c s", s=64)
            pc = act(PC[:, :, :], cl[:, :, :, 63], ACT.Exp, cu, md)
            e3 = act(LW[:, :, :], CUM[:, :, :], ACT.Exp, a2, scale=-1.0)
            b1 = tt("dve", BT[:, :, :], BB[:, :, :], LW[:, :, :], MUL, e3, bb, k2)
            b2 = tt("dve", KTl[:, :, :], k3, LW[:, :, :], MUL, e3, k2)
            yield
            e4 = []
            for t in range(4):
                e4.append(tt("dve", LW[:, t, :].rearrange("p (c s) -> p c s", s=64),
                             cl[:, t, :, 63:64].broadcast_to([128, 4, 64]), cl[:, t, :, :], SUB, b1, b2))
            e4 = act(LW[:, :, :], LW[:, :, :], ACT.Exp, e4)
            b3 = tt("dve", BH[:, :, :], BB[:, :, :], LW[:, :, :], MUL, e4, bb)
            b4 = tt("dve", KH[:, :, :], k3, LW[:, :, :], MUL, e4, k2)
            bo = [stt("dve", BB[:, t, :], r3[:, t, :], vec("rk", l, t), k3[:, t, :], MUL, MUL, b1, b3) for t in range(4)]
            bon = []
            for p in range(2):
                bi, ps, free = Ab.take()
                bp = BB[:, 2 * p:2 * p + 2, :].rearrange("p t s -> p (t s)")
                t = mms([(ps[:, :], BONES, bp, True, True)], bo, free)
                bon.append(tt("dve", bp, ps[:, :], v3[:, 2 * p:2 * p + 2, :].rearrange("p t s -> p (t s)"), MUL, t, vdep))
                Ab.give(bi, bon[-1])
            ready = [a1, a2, b1, b2, b3, b4, vdep, pc, bon, bo, gg, lw, aa]
            yield
            WK = [big(3840, 1024), big(4864, 1024)]
            WK2 = [big(5888, 1024), big(7936, 1024)]
            WK3 = [big(0, 1024), big(1024, 1024)]
            WK4 = [SW[:, 0:512], SW[:, 512:1024]]
            gfree = [ready, ready]
            yd, rd, mn = [], [], []

            def group(j, blk, z):
                dep = [ready, gfree[z]]
                LT4 = WK[z].rearrange("p (e n) -> p e n", e=2)
                LL = WK2[z][:, 0:512].rearrange("p (e a n) -> p e a n", e=2, a=2)
                TT = WK2[z][:, 512:1024].rearrange("p (e a n) -> p e a n", e=2, a=2)
                TK = WK3[z][:, 0:512].rearrange("p (a n) -> p a n", a=4)
                Lf = WK3[z][:, 512:768].rearrange("p (e n) -> p e n", e=2)
                L16 = WK3[z][:, 768:1024].rearrange("p (e n) -> p e n", e=2)
                ZZ = WK4[z][:, 0:256].rearrange("p (e n) -> p e n", e=2)
                XU = WK4[z][:, 256:512].rearrange("p (e n) -> p e n", e=2)
                cols = slice(blk * 128, (blk + 1) * 128)
                bi, ps, free = Ab.take()
                t = mms([(ps[:, 0:128], AR[:, j, blk, 0, :], None, 1, 1), (ps[:, 128:256], v3[:, j, cols], None, 1, 1),
                         (ps[:, 256:384], BH[:, j, cols], None, 1, 1), (ps[:, 384:512], KH[:, j, cols], None, 1, 1)], dep, free)
                tk = cp("act", TK.rearrange("p a n -> p (a n)"), ps[:, :], t, dep)
                Ab.give(bi, tk)
                lt = []
                for e in range(2):
                    r = slice(64 * e, 64 * e + 64)
                    bi, ps, free = Ab.take()
                    ar = AR[r, j, blk, :, :].rearrange("p a n -> p (a n)")
                    t = mms([(ps[:, 0:256], BT[r, j, cols], ar, True, True), (ps[:, 256:512], KTl[r, j, cols], ar, True, True)], dep, free)
                    lt.append(tt("dve", LT4[:, e, :].rearrange("p (a n) -> p a n", a=2), ps[:, :].rearrange("p (a n) -> p a n", a=2), bc(MASKT, 2), MUL, t, dep))
                    Ab.give(bi, lt[-1])
                yield
                lf = []
                for e in range(2):
                    bi, ps, free = Ab.take()
                    r = slice(64 * e, 64 * e + 64)
                    t = mms([(ps[:, 0:128], AR[r, j, blk, 0, :], BT[r, j, cols], True, True)], dep, free)
                    lf.append(tt("dve", Lf[:, e, :], ps[:, 0:128], CST64, MUL, t, dep))
                    Ab.give(bi, lf[-1])
                d1 = tt("pool", LL[:, :, 0, :], Lf, bc(D16, 2), MUL, lf, dep)
                d2 = tt("pool", LL[:, :, 1, :], LT4[:, :, 0:128], bc(D16T, 2), MUL, lt, dep)
                i1 = tt("pool", TT[:, :, 0, :], LL[:, :, 0, :], bc(IDENT, 2), ADD, d1, dep)
                i2 = tt("pool", TT[:, :, 1, :], LL[:, :, 1, :], bc(IDENT, 2), ADD, d2, dep)
                l16 = tt("pool", L16, Lf, bc(C16, 2), MUL, lf, dep)
                l32 = tt("pool", Lf, Lf, bc(C32, 2), MUL, l16, d1)
                yield
                ll, tn = [d1, d2], [i1, i2]
                for m in range(3):
                    bi, ps, free = Ab.take()
                    v = ps[:, :].rearrange("p (e a n) -> p e a n", e=2, a=2)
                    t = mms([x for e in range(2) for x in ((v[:, e, 0, :], LL[:, e, 1, :], LL[:, e, 0, :], True, True),
                                                          (v[:, e, 1, :], LL[:, e, 0, :], LL[:, e, 1, :], True, True))], ll, free)
                    ll = cp("act", LL, v, t, tn)
                    Ab.give(bi, ll)
                    yield
                    bi, ps, free = Ab.take()
                    v = ps[:, :].rearrange("p (e a n) -> p e a n", e=2, a=2)
                    t = mms([x for e in range(2) for x in ((v[:, e, 0, :], TT[:, e, 1, :], LL[:, e, 0, :], True, True),
                                                          (v[:, e, 1, :], LL[:, e, 0, :], TT[:, e, 1, :], True, True))], ll, tn, free)
                    tn = tt("dve", TT, TT, v, ADD, t)
                    Ab.give(bi, tn)
                    yield
                for c, Lo in ((0, L16), (1, Lf)):
                    bi, ps, free = Ab.take()
                    t = mms([(ps[:, e * 128:(e + 1) * 128], Lo[:, e, :], TT[:, e, 1, :], True, True) for e in range(2)], tn, l16, l32, free)
                    zz = cp("act", ZZ, ps[:, 0:256].rearrange("p (e n) -> p e n", e=2), t, dep, tn)
                    Ab.give(bi, zz)
                    bi, ps, free = Ab.take()
                    v = ps[:, :].rearrange("p (e a n) -> p e a n", e=2, a=2)
                    if c == 0:
                        t = mms([x for e in range(2) for x in ((v[:, e, 0, :], ZZ[:, e, :], TT[:, e, 0, :], True, True),
                                                              (v[:, e, 1, :], TT[:, e, 0, :], ZZ[:, e, :], True, True))], zz, free)
                        tn = tt("dve", TT, TT, v, ADD, t)
                    else:
                        t = mms([(v[:, e, 1, :], TT[:, e, 0, :], ZZ[:, e, :], True, True) for e in range(2)], zz, free)
                        tn = tt("dve", TT[:, :, 1, :], TT[:, :, 1, :], v[:, :, 1, :], ADD, t)
                    Ab.give(bi, tn)
                    yield
                bi, ps, free = Ab.take()
                t = mms([(ps[:, e * 64:(e + 1) * 64], LT4[:, e, 256:384], TK[:, 1, e * 64:(e + 1) * 64], True, True) for e in range(2)], lt, tk, free)
                xc = cp("act", ZZ[:, 0, :], ps[:, 0:128], t, tn)
                Ab.give(bi, xc)
                bi, ps, free = Ab.take()
                v = ps[:, 0:256].rearrange("p (e n) -> p e n", e=2)
                t = mms([x for e in range(2) for x in ((v[:, e, 0:64], TT[:, e, 1, :], TK[:, 0, e * 64:(e + 1) * 64], True, True),
                                                      (v[:, e, 64:128], TT[:, e, 1, :], ZZ[:, 0, e * 64:(e + 1) * 64], True, True))], xc, tn, tk, free)
                xu = cp("act", XU, v, t, dep)
                Ab.give(bi, xu)
                yield
                bi, ps, free = Ab.take()
                q = [slice(64 * e, 64 * e + 64) for e in range(2)]
                t = mms([x for e in range(2) for x in (
                    (ps[q[e], 0:128], XU[:, e, 0:64], LT4[:, e, 128:256], True, True),
                    (ps[q[e], 128:256], XU[:, e, 64:128], LT4[:, e, 128:256], True, False),
                    (ps[q[e], 128:256], TK[:, 1, q[e]], LT4[:, e, 384:512], False, True))], xu, free)
                o = [tt("dve", RP[:, j, cols], ps[:, 0:128], AR[:, j, blk, 1, :], ADD, t, dep),
                     cp("dve", Y[:, j, cols], ps[:, 128:256], t, dep)]
                Ab.give(bi, o)
                rd.append(o)
                mm = []
                for c in range(2):
                    ch = 2 * blk + c
                    if ch == 3:
                        continue
                    r = slice(64 * c, 64 * c + 64)
                    bi, ps, free = Ab.take()
                    items = []
                    for e in range(2):
                        items += [(ps[q[e], 0:64], XU[r, e, 0:64], TK[r, 2, q[e]], True, True),
                                  (ps[q[e], 64:128], TK[r, 2, q[e]], XU[r, e, 64:128], True, False),
                                  (ps[q[e], 64:128], TK[r, 3, q[e]], TK[r, 1, q[e]], False, True)]
                    t = mms(items, xu, tk, free)
                    c2 = [cp("dve", MN[:, j, ch, 64:128], ps[:, 64:128], t, dep),
                          stt("dve", MN[:, j, ch, 0:64], ID64, PC[:, j, ch:ch + 1], ps[:, 0:64], MUL, ADD, t, dep)]
                    Ab.give(bi, c2)
                    mm.append(c2)
                mn.append(mm)
                gfree[z] = [o, mm, t]
                yield

            groups = [(j, b) for j in range(4) for b in range(2)]
            for i in range(0, 8, 2):
                interleave([group(*groups[i], 0), group(*groups[i + 1], 1)], [1.0, 1.0])
                yield
            SS = WK[0][:, 0:512].rearrange("p (c j n) -> p c j n", c=2, n=64)
            st = [MN[:, :, 0, 64:128], SS[:, 0, :, :], SS[:, 1, :, :]]
            sd = [mn, gfree[0], gfree[1]]
            q = [slice(64 * e, 64 * e + 64) for e in range(2)]
            for c in range(1, 3):
                new = []
                for e in range(2):
                    bi, ps, free = Ab.take()
                    t = mms([(ps[q[e], j * 64:(j + 1) * 64], MN[q[e], j, c, 0:64], st[c - 1][q[e], j, :], True, True) for j in range(4)], sd, free)
                    new.append(tt("dve", st[c][q[e], :, :], ps[q[e], 0:256].rearrange("p (j n) -> p j n", n=64), MN[q[e], :, c, 64:128], ADD, t, sd))
                    Ab.give(bi, new[-1])
                sd = [sd, new]
            yy = []
            for g in range(2):
                for e in range(2):
                    bi, ps, free = Ab.take()
                    v = ps[q[e], 0:384].rearrange("p (j n) -> p j n", n=192)
                    t = mms([(v[:, u, 64 * c:64 * c + 64], st[c][q[e], 2 * g + u, :], RP[q[e], 2 * g + u, 64 * c + 64:64 * c + 128], True, True)
                             for u in range(2) for c in range(3)], sd, rd, free)
                    yv = Y[q[e], 2 * g:2 * g + 2, 64:256]
                    yy.append(tt("dve", yv, v, yv, ADD, t, rd))
                    Ab.give(bi, yy[-1])
            yield
            cen = []
            for p in range(2):
                bi, ps, free = Ab.take()
                yp = Y[:, 2 * p:2 * p + 2, :].rearrange("p t s -> p (t s)")
                t = mms([(ps[:, :], BONES, yp, True, True)], yy, free)
                cen.append(stt("dve", yp, ps[:, :], -1.0 / 64, yp, MUL, ADD, t))
                Ab.give(bi, cen[-1])
            a = head_rs(Y, 4, 1.0 / 64, 1e-5 * 64, cen, lambda t0, m, ps3, tok: tt("dve", Y[:, t0:t0 + m, :], Y[:, t0:t0 + m, :], ps3, MUL, tok))
            fin = []
            for t in range(4):
                b = ts("dve", Y[:, t, :], Y[:, t, :], vec("lxg", l, t), vec("lxb", l, t), MUL, ADD, a)
                b = tt("pool", Y[:, t, :], Y[:, t, :], BB[:, t, :], ADD, b, bon)
                fin.append(tt("pool", Y[:, t, :], Y[:, t, :], GG[:, t, :], MUL, b, gg))
            ya.append(split(YAs, Y, fin))
            yield
        odone, gates = [], []

        def sparse():
            dd = []

            def put_d(t0):
                def f(n, ps, tok):
                    a = cp("act", DA[:, t0 + 2 * n:t0 + 2 * n + 2, :], ps[:, :].rearrange("p (t s) -> p t s", s=S), tok)
                    dd.append(a)
                    return a
                return f
            yield from gemm(pairs(w_in, 14, 4), 8, rhs, hall, put_d(0))
            for j, n in ((0, 64), (1, 8)):
                z, hi, lo, wt = take_w(*unit(w_in, 18 + 5 * j, 1, 0, 8))
                bi, ps, free = Gb.take()
                items = []
                for k in range(8):
                    c = slice(k * 128, (k + 1) * 128)
                    items += products(ps[:, 0:S], (hi[:, c], lo[:, c]), rhs(k), k == 0, k == 7)
                for tb in range(2):
                    for k in range(8):
                        c = slice(k * 128 + 64, k * 128 + 64 + n)
                        items += products(ps[:, S + 64 * tb:S + 64 * tb + n], [x[:, tb * 128:(tb + 1) * 128] for x in rhs(k)],
                                          (hi[:, c], lo[:, c]), k == 0, k == 7)
                t = mms(items, hall, wt, free)
                give_w(z, t)
                o = [cp("act", DA[0:64, 4 + j, :], ps[0:64, 0:S], t), cp("act", DA[64:128, 4 + j, :], ps[0:64, 0:S], t)]
                dst = V2 if j == 0 else IW
                o.append(cp("act", dst, ps[:, S:S + 128].rearrange("p (b n) -> p b n", b=2)[:, :, 0:n], t))
                Gb.give(bi, o)
                dd.append(o)
                yield
            yield from gemm(pairs(w_in, 19, 4), 8, rhs, hall, put_d(6))
            keys = ["dq"] * 4 + ["dk", "di"]
            nd = head_rs(DA, 6, 1.0 / 64, 1e-6, dd, lambda t0, m, ps3, tok: [
                stt("dve", DA[:, t, :], DA[:, t, :], vec(keys[t], l), ps3[:, t - t0, :], MUL, MUL, tok) for t in range(t0, t0 + m)])
            cos2, sin2 = ROPE[:, 0:S], ROPE[:, S:2 * S]
            rp = []
            yield
            for p in (2, 3, 4, 0, 1):
                bi, ps, free = Ab.take()
                dv = DA[:, 2 * p:2 * p + 2, :]
                t = mms([(ps[:, :], ROT64, dv.rearrange("p t s -> p (t s)"), True, True)], nd, dd, free)
                a = tt("pool", dv, dv, bc(cos2, 2), MUL, t, t_rope)
                si, s, sf = Scr.take()
                s3 = s.rearrange("p (t s) -> p t s", s=S)
                b = tt("dve", s3, ps[:, :].rearrange("p (t s) -> p t s", s=S), bc(sin2, 2), MUL, t, sf, t_rope)
                Ab.give(bi, b)
                rp.append(tt("pool", dv, dv, s3, ADD, a, b))
                Scr.give(si, rp[-1])
                yield
            nks = (128, 256)
            acc = [None, None]
            for b in range(2):
                nk, b0 = nks[b], 128 * b
                for p in range(4):
                    si, s, sf = Scr.take()
                    s3 = s[:, 0:2 * nk].rearrange("p (e s) -> p e s", e=2)
                    a = []
                    for e in range(2):
                        bi, ps, free = Ab.take()
                        r = slice(64 * e, 64 * e + 64)
                        t = mms([(ps[:, 0:nk], DA[r, 6 + p, b * 128:(b + 1) * 128], DA[r, 5, 0:nk], True, True)], rp, free)
                        a.append(act(s3[:, e, :], ps[:, 0:nk], ACT.Relu, t, sf, scale=0.125))
                        Ab.give(bi, a[-1])
                    for e in range(2):
                        w = IW[:, b, 2 * p + e:2 * p + e + 1]
                        if p == 0 and e == 0:
                            acc[b] = ts("dve", SCO[:, b0:b0 + nk], s3[:, e, :], w, None, MUL, None, a, dd)
                        else:
                            acc[b] = stt("dve", SCO[:, b0:b0 + nk], s3[:, e, :], w, SCO[:, b0:b0 + nk], MUL, ADD, a, acc[b])
                    Scr.give(si, acc[b])
                    yield
                a = ts("dve", SCO[:, b0:b0 + nk], SCO[:, b0:b0 + nk], float(8 ** -0.5), None, MUL, None, acc[b])
                m0 = 64 if b == 0 else 192
                a = P.put("dve", lambda e, b0=b0, m0=m0: e.memset(SCO[0:64, b0 + m0:b0 + m0 + 64], -1e30), a)
                for it in range(8):
                    src = SCO if it == 0 else WKX
                    xi, m8, mf = Stat8.take()
                    c = P.put("dve", lambda e, o=m8, i=src[:, b0:b0 + nk]: e.max(o, i), a, mf)
                    a = P.put("dve", lambda e, o=WKX[:, b0:b0 + nk], r=m8, i=src[:, b0:b0 + nk]: e.match_replace(o, r, i, -3e38), c)
                    Stat8.give(xi, a)
                    yield
                a = ts("dve", PEN[:, b0:b0 + nk], WKX[:, b0:b0 + nk], -3e38, -1e30, ALU.is_gt, MUL, a)
                a = P.put("dve", lambda e, b0=b0, m0=m0: e.memset(PEN[0:64, b0 + m0:b0 + m0 + 64], -1e30), a)
                acc[b] = a
            yield from attention(8, lambda h: DA[64 * (h % 2):64 * (h % 2) + 64, h // 2, :],
                                 lambda h: DA[64 * (h % 2):64 * (h % 2) + 64, 4, :], 0.125,
                                 lambda h, kt: V2[:, kt, :], lambda h: O[64 * (h % 2):64 * (h % 2) + 64, h // 2, :], 64,
                                 [rp, acc], nks=nks, pen=lambda b: PEN[:, 128 * b:128 * b + nks[b]], done=odone)

        def gate_gemm():
            def put_gate(n, ps, tok):
                a = act(GT[:, 2 * n:2 * n + 2, :].rearrange("p t s -> p (t s)"), ps[:, :], ACT.Tanh, tok, scale=0.5)
                gates.append(a)
                return a
            yield from gemm(pairs(w_in, 24, 16), 8, rhs, hall, put_gate)

        interleave([rwkv(), sparse(), gate_gemm()], WT2)
        os = split(Os, O, [odone, ya])
        M = big(0, 8, S)
        M2 = big2(2048, 8, S)
        mt = {}
        for b, (src, W, dep) in enumerate(((YAs, "w_branch_a_2", ya), (Os, "w_branch_b_2", os))):
            def put_m(n, ps, tok, b=b):
                mv = M[:, 2 * n:2 * n + 2, :].rearrange("p t s -> p (t s)")
                gv = GT[:, 8 * b + 2 * n:8 * b + 2 * n + 2, :].rearrange("p t s -> p (t s)")
                if b == 0:
                    mt[n] = stt("dve", mv, gv, 1.0, ps[:, :], ADD, MUL, tok, gates)
                    return mt[n]
                si, s, sf = Scr.take()
                a = stt("dve", s, gv, 1.0, ps[:, :], ADD, MUL, tok, sf)
                mt[n] = tt("pool", mv, mv, s, ADD, a, mt[n])
                Scr.give(si, mt[n])
                mt[n] = split([x[:, 2 * n:2 * n + 2, :] for x in M2], M[:, 2 * n:2 * n + 2, :], mt[n], eng="dve" if n % 2 else "pool")
                return a
            yield from gemm(pairs(ins[W][l], 0, 8), 4, lambda k, src=src: (src[0][:, k, :], src[1][:, k, :]), dep, put_m)
        xnew.clear()
        yield from gemm(pairs(ins["w_out_2"][l], 0, 8), 8, lambda k: (M2[0][:, k, :], M2[1][:, k, :]), {k: mt[k // 2] for k in range(8)},
                        lambda n, ps, tok: add_x(n, ps, tok, 0.5))
        xdep[:] = list(xnew)

    def block2_mem(l):
        P.barrier()
        MT = big(0, 8, S)
        MH = big2(2048, 8, S)
        Q, K = big(6144, 4, S), big(7168, 4, S)
        V = big(8192, 2, 512)
        O = big(9216, 4, S)
        Os = big2(10240, 4, S)
        W = ins["mem_wkv_2"][l]
        t_m = P.dma("mem", MT.rearrange("p t s -> p (t s)"), ins["memT"], P.now(), eng="act")
        mh = rmsnorm(MT, 8, "mtok", l, MH, [t_m])
        hd = rmsnorm(x3, 8, "nmem", l, h2, xdep)
        yield
        mem = lambda k: (MH[0][:, k, :], MH[1][:, k, :])
        mall = list(mh.values())
        qd, kd, vd = [], [], []

        def put_to(dst, lst):
            def f(n, ps, tok):
                a = cp("act", dst[:, 2 * n:2 * n + 2, :].rearrange("p t s -> p (t s)"), ps[:, :], tok)
                lst.append(a)
                return a
            return f

        def normed(src, key, dep):
            return head_rs(src, 4, 1.0 / 128, 1e-6, dep, lambda t0, m, ps3, tok: [
                stt("dve", src[:, t, :], src[:, t, :], vec(key, l), ps3[:, t - t0, :], MUL, MUL, tok) for t in range(t0, t0 + m)], heads=1)
        yield from gemm(pairs(W, 0, 4), 8, mem, mh, put_to(K, kd))
        yield from gemm(pairs(ins["mem_wq_2"][l], 0, 4), 8, lambda k: (h2[0][:, k, :], h2[1][:, k, :]), list(hd.values()), put_to(Q, qd))
        bks = [Gb.take() for _ in range(2)]
        tks = [None, None]
        for g in range(4):
            z, hi, lo, wt = take_w(*unit(W, 4 + g, 1, 0, 8))
            for tb in range(2):
                items = []
                for k in range(8):
                    c = slice(k * 128, (k + 1) * 128)
                    items += products(bks[tb][1][:, g * 128:(g + 1) * 128], [x[:, tb * 128:(tb + 1) * 128] for x in mem(k)],
                                      (hi[:, c], lo[:, c]), k == 0, k == 7)
                tks[tb] = mms(items, mall, wt, bks[tb][2])
            give_w(z, tks)
            if g == 0:
                nd = normed(K, "mk", kd)
            if g == 1:
                nd = nd + normed(Q, "mq", qd)
        for tb in range(2):
            a = cp("act", V[:, tb, :], bks[tb][1][:, :], tks[tb])
            Gb.give(bks[tb][0], a)
            vd.append(a)
        yield
        od = []
        yield from attention(4, lambda h: Q[:, h, :], lambda h: K[:, h, :], 128 ** -0.5, lambda h, kt: V[:, kt, h * 128:(h + 1) * 128],
                             lambda h: O[:, h, :], 128, [nd, vd], done=od)
        os = split(Os, O, od)
        xnew.clear()
        yield from gemm(pairs(ins["mem_wo_2"][l], 0, 8), 4, lambda k: (Os[0][:, k, :], Os[1][:, k, :]), os, add_x)
        xdep[:] = list(xnew)

    def block2_ffn():
        P.barrier()
        hd = rmsnorm(x3, 8, "nffn", 0, h2, xdep)
        F2 = big2(0, 22, S)
        fd = yield from ffn_up(ins["ffn_wg_2"][0], ins["ffn_wu_2"][0], 22, F2, hd, None)
        xnew.clear()
        yield from gemm(pairs(ins["ffn_wd_2"][0], 0, 8), 22, lambda k: (F2[0][:, k, :], F2[1][:, k, :]), fd, add_x)
        xdep[:] = list(xnew)

    def block2_moe():
        P.barrier()
        RT = big(0, 8, 8)
        BI = big(64, 8)
        LG = big(72, 2, 8)
        GT = big(88, 2, 8)
        M8 = big(104, 2, 8)
        IX = big(120, 2, 8)
        IXF = big(136, 2, 8)
        E2 = big(152, 2, 8)
        DGm = big(256, 2, 128)
        GB = big(512, 8, S)
        RTs = big2(13824, 8, 8)
        Fs = [big2(2560, 11, S), big2(8192, 11, S)]
        t_r = [P.dma("rt", RT, ins["moe_router_2"][0].rearrange("(k p) n -> p k n", p=128), P.now(), eng="act"),
               P.dma("rb", BI, ins["moe_bias_2"][0].partition_broadcast(128), P.now(), eng="act")]
        hd = rmsnorm(x3, 8, "nffn", 1, h2, xdep)
        rt = split(RTs, RT, t_r)
        hall = list(hd.values())
        bi, ps, free = Ab.take()
        items = []
        for b in range(2):
            for k in range(8):
                items += products(ps[:, 8 * b:8 * b + 8], [x[:, k, b * 128:(b + 1) * 128] for x in h2], [x[:, k, :] for x in RTs], k == 0, k == 7)
        t = mms(items, hall, rt, free)
        a = tt("dve", LG, ps[:, 0:16].rearrange("p (b n) -> p b n", b=2), bc(BI, 2), ADD, t, t_r)
        Ab.give(bi, a)
        gts = []
        for b in range(2):
            m = P.put("dve", lambda e, b=b: e.max(M8[:, b, :], LG[:, b, :]), a)
            i = P.put("dve", lambda e, b=b: e.max_index(IX[:, b, :].bitcast(U32), M8[:, b, :], LG[:, b, :]), m)
            i = cp("dve", IXF[:, b, :], IX[:, b, :].bitcast(U32), i)
            d = tt("dve", E2[:, b, 0:1], M8[:, b, 1:2], M8[:, b, 0:1], SUB, m)
            d = act(E2[:, b, 0:1], E2[:, b, 0:1], ACT.Exp, d)
            s = ts("dve", E2[:, b, 1:2], E2[:, b, 0:1], 1.0, None, ADD, None, d)
            s = P.put("dve", lambda e, b=b: e.reciprocal(E2[:, b, 2:3], E2[:, b, 1:2]), s)
            s = tt("dve", E2[:, b, 3:4], E2[:, b, 0:1], E2[:, b, 2:3], MUL, s)
            g1 = ts("dve", GT[:, b, :], IOTA8, IXF[:, b, 0:1], E2[:, b, 2:3], ALU.is_equal, MUL, s, i)
            g2 = ts("dve", M8[:, b, :], IOTA8, IXF[:, b, 1:2], E2[:, b, 3:4], ALU.is_equal, MUL, g1)
            gts.append(tt("dve", GT[:, b, :], GT[:, b, :], M8[:, b, :], ADD, g2))
        gb, dfree = [], None
        for e8 in range(8):
            dg = [ts("dve", DGm[:, b, :], IDENT, GT[:, b, e8:e8 + 1], None, MUL, None, gts, dfree) for b in range(2)]
            bi, ps, free = Ab.take()
            t = mms([(ps[:, b * 128:(b + 1) * 128], ONES, DGm[:, b, :], True, True) for b in range(2)], dg, free)
            dfree = t
            gb.append(cp("act", GB[:, e8, :], ps[:, 0:S], t))
            Ab.give(bi, gb[-1])
        yield
        xnew.clear()
        xl = {}
        ff = [None, None]

        def up(e8):
            z = e8 % 2
            fds[e8] = yield from ffn_up(ins["moe_wg_2"][0][e8], ins["moe_wu_2"][0][e8], 11, Fs[z], hd, [gb, ff[z]], gate=GB[:, e8, :])

        def down(e8):
            z = e8 % 2

            def put_x(n, ps, tok):
                v = x3[:, 2 * n:2 * n + 2, :].rearrange("p t s -> p (t s)")
                xl[n] = tt("dve", v, ps[:, :], v, ADD, tok, xl.get(n), hall)
                ff[z] = tok
                return xl[n]
            yield from gemm(pairs(ins["moe_wd_2"][0][e8], 0, 8), 11, lambda k: (Fs[z][0][:, k, :], Fs[z][1][:, k, :]), fds[e8], put_x)
        fds = {}
        ahead = up(0)
        for e8 in range(8):
            yield from ahead
            if e8 < 7:
                ahead = up(e8 + 1)
                next(ahead)
                yield
            yield from down(e8)
        xdep[:] = list(xl.values())

    Stat8 = Ring([S8[:, i * 8:(i + 1) * 8] for i in range(4)])

    phases = [lambda: block1_mix(0), lambda: block1_ffn(0), lambda: block1_mix(1), lambda: block1_ffn(1),
              lambda: block2_mix(0), lambda: block2_mem(0), block2_ffn, lambda: block2_mix(1), lambda: block2_mem(1), block2_moe]
    for ph in phases[ins.get("first", 0):ins.get("last", len(phases))]:
        run(ph())
    t_out = P.dma("out", out, X[:, :], xdep)
    for c, (ph, pl) in enumerate(places[loaded[0]:]):
        P.fill(ph, lambda e, c=c: e.activation(IDLE[:, 2 * c:2 * c + 1], CST[:, 0:1], ACT.Copy), t_cst)
        P.fill(pl, lambda e, c=c: e.memset(IDLE[:, 2 * c + 1:2 * c + 2], 0.0))

    with nc.Block() as block:
        @block.tensor
        def _(e):
            P.replay("pe", e)

        @block.scalar
        def _(e):
            P.replay("act", e)

        @block.vector
        def _(e):
            P.replay("dve", e)

        @block.gpsimd
        def _(e):
            P.replay("pool", e)

        @block.sync
        def _(e):
            P.replay("sp", e)
            e.wait_ge(P.sem[t_out[0]], t_out[1])


def constants():
    c = np.zeros((128, NCST), np.float32)
    i = np.arange(128)
    c[:, 0:128] = np.eye(128)
    c[:, 128:256] = 1.0
    c[:, 256:384] = (i[:, None] // 64) == (i[None, :] // 64)
    for m in range(64, 96):
        if m < 80:
            c[m + 16, 384 + m] = -1.0
        else:
            c[m - 16, 384 + m] = 1.0
    for m in range(128):
        if m % 64 < 32:
            c[m + 32, 512 + m] = -1.0
        else:
            c[m - 32, 512 + m] = 1.0
    t, j = i[:, None], i[None, :]
    low = t > j
    c[:, 640:768] = low & (t // 16 == j // 16)
    c[:, 768:896] = (low & (t // 16 == j // 16)).T
    c[:, 896:1024] = low & (t // 32 == j // 32) & (t // 16 != j // 16)
    c[:, 1024:1152] = low & (t // 64 == j // 64) & (t // 32 != j // 32)
    c[:, 1152:1280] = low & (t // 64 == j // 64)
    strict = ((t < j) & (t // 64 == j // 64)).astype(np.float32)
    incl = ((t <= j) & (t // 64 == j // 64)).astype(np.float32)
    c[:, 1280:1536] = np.concatenate([strict, incl], 1)
    c[:, 1536:1792] = (np.arange(256) % 64 != 0)[None, :]
    c[:, 1792:1856] = np.tile(np.eye(64), (2, 1))
    c[:, 1856:1864] = np.arange(8)[None, :]
    f1 = np.array(INV1, np.uint32).view(np.float32)
    f2 = np.array(INV2, np.uint32).view(np.float32)
    c[:, 1864] = f1[i % 16]
    c[:, 1865] = f2[i % 32]
    return c


INV1 = [0x3f800000, 0x3f0ff59a, 0x3ea1e89b, 0x3e361887, 0x3dcccccd, 0x3d6655c3, 0x3d0186e2, 0x3c91ad39, 0x3c23d70a, 0x3bb8449c,
        0x3b4f3e37, 0x3ae91528, 0x3a83126f, 0x3a136a16, 0x39a5cb5f, 0x393a7753]
INV2 = [0x3f800000, 0x3f3ff911, 0x3f0ff59a, 0x3ed7e89b, 0x3ea1e89b, 0x3e72d423, 0x3e361887, 0x3e088d77, 0x3dcccccd, 0x3d99940d,
        0x3d6655c2, 0x3d2cba15, 0x3d0186e3, 0x3cc2434f, 0x3c91ad39, 0x3c5a7bf2, 0x3c23d70a, 0x3bf5b9b0, 0x3bb8449c, 0x3b8a2e77,
        0x3b4f3e38, 0x3b1b690d, 0x3ae91528, 0x3aaec98e, 0x3a83126f, 0x3a44948c, 0x3a136a16, 0x39dd1725, 0x39a5cb60, 0x3978a815,
        0x393a7753, 0x390bd472]


def pack_vectors(inputs):
    cols = []
    for l in range(2):
        for key, name, n in VECS1 + VECS2:
            a = np.asarray(inputs[name])
            if key == "v0":
                a = a[0]
            else:
                a = a[l]
            a = a.reshape(-1)
            if a.size == 64:
                a = np.concatenate([a, a])
            if key == "mu":
                z = np.zeros(64, a.dtype)
                a = np.concatenate([a[0:1536], a[1536:1600], z, a[1600:1664], z, a[1664:1792]])
            assert a.size == 128 * n, name
            cols.append(a.reshape(n, 128).T)
    return np.ascontiguousarray(np.concatenate(cols, 1))


_WHOLE = ["positions", "positions_2", "gm_ln_g", "gm_ln_b", "gm_bs", "rwkv_w2_2", "rwkv_a2_2", "rwkv_g2_2", "rwkv_v1_2",
          "rwkv_v2_2", "moe_router_2", "moe_bias_2"]
_BLOCKED = ["w_o_mla", "w_o_sc", "w_o_cf", "w_o_gm", "w_out", "w_ffn_out", "w_branch_a_2", "w_branch_b_2", "w_out_2",
            "mem_wq_2", "mem_wkv_2", "mem_wo_2", "ffn_wg_2", "ffn_wu_2", "ffn_wd_2", "moe_wg_2", "moe_wu_2", "moe_wd_2"]


def blocks(a):
    lead, (k, n) = a.shape[:-2], a.shape[-2:]
    b = a.reshape(*lead, k // 128, 128, n // 128, 128)
    m = len(lead)
    return np.ascontiguousarray(b.transpose(*range(m), m + 2, m + 1, m, m + 3)).reshape(*lead, n // 128, 128, k)


def padded(a, left, width):
    r = np.zeros((*a.shape[:-1], width), a.dtype)
    r[..., left:left + a.shape[-1]] = a
    return r


def by_features(a):
    return np.ascontiguousarray(a.T.reshape(8, 128, 256).transpose(1, 0, 2).reshape(128, 2048))


def lay_out(inputs):
    arrays = {k: np.ascontiguousarray(inputs[k]) for k in _WHOLE}
    for k in ("positions", "positions_2"):
        arrays[k] = arrays[k].reshape(256)
    arrays["xT"] = by_features(np.asarray(inputs["x"])[0])
    arrays["memT"] = by_features(np.asarray(inputs["mem_2"])[0])
    arrays["gm_wsT"] = np.ascontiguousarray(np.asarray(inputs["gm_ws"]).transpose(0, 3, 1, 2).reshape(2, 128, 512))
    for k in _BLOCKED:
        arrays[k] = blocks(np.asarray(inputs[k]))
    w = np.asarray(inputs["w_in"])
    arrays["w_in_a"] = blocks(w[:, :, 0:512])
    arrays["w_kr"] = blocks(padded(w[:, :, 512:544], 64, 128))
    arrays["w_in_b"] = blocks(w[:, :, 544:8224])
    w = np.asarray(inputs["w_uq"]).reshape(2, 256, 8, 96)
    arrays["w_uq"] = blocks(padded(w, 0, 128).reshape(2, 256, 1024))
    arrays["w_ukv"] = blocks(np.asarray(inputs["w_ukv"]))
    w = np.asarray(inputs["w_ffn_in"])
    arrays["w_ffn_g"], arrays["w_ffn_u"] = blocks(w[:, :, 0:2816]), blocks(w[:, :, 2816:5632])
    w = np.asarray(inputs["w_in_2"])
    arrays["w_in_2"] = blocks(np.concatenate([w[:, :, 0:2944], padded(w[:, :, 2944:3016], 0, 128), w[:, :, 3016:5064]], 2))
    arrays["vecs"] = pack_vectors(inputs)
    arrays["cst"] = constants()
    return arrays


def kernel(**inputs):
    import concourse.bacc as bacc
    from concourse.bass_utils import run_bass_kernel_spmd

    nc = bacc.Bacc("TRN2", target_bir_lowering=False, num_devices=1, dynamic_dma_scratch_size=1024)
    arrays = lay_out(inputs)
    ins = {k: nc.dram_tensor("in_" + k, a.shape, mybir.dt.from_np(a.dtype), kind="ExternalInput").ap() for k, a in arrays.items()}
    out = nc.dram_tensor("out_x", (128, 2048), F32, kind="ExternalOutput").ap()
    build_program(nc, ins, out)
    r = run_bass_kernel_spmd(nc, [{"in_" + k: a for k, a in arrays.items()}], core_ids=[0])
    y = r.results[0]["out_x"].reshape(128, 8, 256)
    return np.ascontiguousarray(y.transpose(2, 1, 0).reshape(1, 256, 1024))
```

```python
import numpy as np
from contextlib import ExitStack
import concourse.bass as bass
from concourse import mybir

S = 256
F32 = mybir.dt.float32
F32R = mybir.dt.float32r
I32 = mybir.dt.int32
U32 = mybir.dt.uint32
ALU = mybir.AluOpType
ACT = mybir.ActivationFunctionType
AXX = mybir.AxisListType.X

VECS1 = [("nmp", "norm_mix_pre", 8), ("qn", "mla_q_norm", 2), ("kvn", "mla_kv_norm", 2), ("scw", "sc_conv_w", 12),
         ("cfw", "cf_conv_w", 124), ("cfb", "cf_conv_b", 4), ("clg", "cf_ln_g", 4), ("clb", "cf_ln_b", 4),
         ("gb", "gate_b", 32), ("npo", "norm_mix_post", 8), ("nfp", "norm_ffn_pre", 8), ("nfo", "norm_ffn_post", 8)]
VECS2 = [("nmix", "norm_mix_2", 8), ("mu", "rwkv_mu_2", 15), ("w0", "rwkv_w0_2", 4), ("a0", "rwkv_a0_2", 4),
         ("kk", "rwkv_kk_2", 4), ("ka", "rwkv_ka_2", 4), ("rk", "rwkv_rk_2", 4), ("lxg", "rwkv_lnx_g_2", 4),
         ("lxb", "rwkv_lnx_b_2", 4), ("dq", "dsa_q_norm_2", 1), ("dk", "dsa_k_norm_2", 1), ("di", "idx_k_norm_2", 1),
         ("nmem", "norm_mem_2", 8), ("mtok", "mem_tok_norm_2", 8), ("mq", "mem_q_norm_2", 1), ("mk", "mem_k_norm_2", 1),
         ("nffn", "norm_ffn_2", 8), ("v0", "rwkv_v0_2", 4)]
NVEC = 2 * (sum(n for _, _, n in VECS1) + sum(n for _, _, n in VECS2))
NCST = 10 * 128 + 256 + 256 + 64 + 8 + 4


def vec_offsets():
    off, at = {}, 0
    for l in range(2):
        for key, _, n in VECS1 + VECS2:
            off[key, l] = at
            at += n
    return off


def build_program(nc, ins, out):
    ctx = ExitStack()
    with ctx:
        build(nc, ctx, ins, out)


class Prog:

    def __init__(self, nc, ctx):
        self.nc, self.ctx = nc, ctx
        self.q = {e: [] for e in ("pe", "act", "dve", "pool", "sp")}
        self.n = {e: 0 for e in ("pe", "act", "dve", "pool")}
        self.sem = {e: ctx.enter_context(nc.semaphore("s_" + e)) for e in self.n}
        self.dn = {}
        self.bar = {e: [] for e in self.q}

    def put(self, eng, fn, *after):
        self.q[eng].append((self.bar[eng] + flat(after), fn, self.sem[eng], 1))
        self.bar[eng] = []
        self.n[eng] += 1
        return (eng, self.n[eng])

    def dma(self, slot, dst, src, *after, eng="sp"):
        key = "d_" + slot
        if key not in self.sem:
            self.sem[key] = self.ctx.enter_context(self.nc.semaphore(key))
            self.dn[key] = 0
        self.q[eng].append((flat(after), lambda e: e.dma_start(dst, src), self.sem[key], 16))
        self.dn[key] += 16
        return (key, self.dn[key])

    def reserve(self, eng):
        self.q[eng].append(None)
        self.n[eng] += 1
        return eng, len(self.q[eng]) - 1, (eng, self.n[eng])

    def fill(self, place, fn, *after):
        eng, at, _ = place
        self.q[eng][at] = (flat(after), fn, self.sem[eng], 1)

    def now(self):
        return [(e, n) for e, n in self.n.items() if n]

    def barrier(self, snap=None):
        for e in self.n:
            self.bar[e] = snap or self.now()

    def replay(self, eng, e):
        seen = {}
        for after, fn, sem, inc in self.q[eng]:
            for key, val in after:
                if seen.get(key, 0) < val:
                    e.wait_ge(self.sem[key], val)
                    seen[key] = val
            fn(e).then_inc(sem, inc)


def flat(ts):
    r = []
    for t in ts:
        if t is None:
            continue
        if isinstance(t, list):
            r += flat(t)
        else:
            r.append(t)
    return r


class Ring:

    def __init__(self, bufs):
        self.bufs, self.free, self.i = bufs, [None] * len(bufs), 0

    def take(self):
        n = len(self.bufs)
        i = next((j % n for j in range(self.i, self.i + n) if self.free[j % n] != "taken"), None)
        assert i is not None, "ring overrun"
        self.i = (i + 1) % n
        tok, self.free[i] = self.free[i], "taken"
        return i, self.bufs[i], tok

    def give(self, i, *tok):
        self.free[i] = flat(tok)


def build(nc, ctx, ins, out):
    P = Prog(nc, ctx)
    VO = vec_offsets()

    def sb(name, n, dt=F32):
        return nc.alloc_sbuf_tensor(name, [128, n], dt)

    def tt(eng, o, a, b, op, *dep):
        return P.put(eng, lambda e: e.tensor_tensor(o, a, b, op), *dep)

    def ts(eng, o, a, s1, s2, op0, op1, *dep):
        if s2 is None:
            return P.put(eng, lambda e: e.tensor_scalar(o, a, s1, None, op0), *dep)
        return P.put(eng, lambda e: e.tensor_scalar(o, a, s1, s2, op0, op1), *dep)

    def stt(eng, o, a, s, b, op0, op1, *dep):
        return P.put(eng, lambda e: e.scalar_tensor_tensor(out=o, in0=a, scalar=s, in1=b, op0=op0, op1=op1), *dep)

    def cp(eng, o, a, *dep):
        if eng == "act":
            return P.put("act", lambda e: e.activation(o, a, ACT.Copy), *dep)
        return P.put(eng, lambda e: e.tensor_copy(o, a), *dep)

    def act(o, a, f, *dep, bias=None, scale=1.0, acc=None):
        kw = {}
        if bias is not None:
            kw["bias"] = bias
        if acc is not None:
            kw["accum_out"] = acc
        return P.put("act", lambda e: e.activation(o, a, f, scale=scale, **kw), *dep)

    def mms(items, *dep):
        def fn(e):
            for o, l, r, st, sp in items:
                if r is None:
                    last = e.transpose(o, l, IDENT[0:l.shape[0], 0:l.shape[0]])
                else:
                    last = e.matmul(o, l, r, start=st, stop=sp)
            return last
        return P.put("pe", fn, *dep)

    MUL, ADD, SUB, MAX, MIN = ALU.mult, ALU.add, ALU.subtract, ALU.max, ALU.min

    SLOT, NRAW, NSPL, AHEAD = 1024, 4, 4, 2
    WF = Ring([sb(f"wf{i}", SLOT) for i in range(NRAW)])
    WH = [sb(f"wh{i}", SLOT, F32R) for i in range(NSPL)]
    WL = [sb(f"wl{i}", SLOT, F32R) for i in range(NSPL)]
    X = sb("X", 2048)
    HH = sb("HH", 2048, F32R)
    HL = sb("HL", 2048, F32R)
    VEC = sb("VEC", NVEC)
    CST = sb("CST", NCST)
    ROPE = sb("ROPE", 512)
    SC = sb("SC", 6 * 512)
    ST = sb("ST", 64)
    S8 = sb("S8", 32)
    IDLE = sb("IDLE", 8)
    RS = sb("RS", 4 * 48)
    ARENA = 31924
    arena = sb("arena", ARENA)
    arena_at = nc.sbuf_base - 4 * ARENA
    PS = [ctx.enter_context(nc.psum_tensor(f"ps{i}", [128, 512], F32)) for i in range(8)]
    Gb = Ring(PS[0:4])
    Ab = Ring(PS[4:8])
    Scr = Ring([SC[:, i * 512:(i + 1) * 512] for i in range(6)])
    Stat = Ring([ST[:, i * 4:(i + 1) * 4] for i in range(16)])

    def cst(i, n=128):
        return CST[:, i:i + n]

    IDENT, ONES, BONES = cst(0), cst(128), cst(256)
    ROT96, ROT64 = cst(384), cst(512)
    D16, D16T, C16, C32, CST64 = cst(640), cst(768), cst(896), cst(1024), cst(1152)
    MASKT = cst(1280, 256)
    SCM = cst(1536, 256)
    ID64 = cst(1792, 64)
    IOTA8 = cst(1856, 8)
    IF1, IF2 = cst(1864, 1), cst(1865, 1)

    x3 = X[:, :].rearrange("p (t s) -> p t s", s=S)
    h2 = [t[:, :].rearrange("p (t s) -> p t s", s=S) for t in (HH, HL)]

    def vec(key, l, i=0, n=1):
        o = VO[key, l] + i
        return VEC[:, o:o + n]

    placed = [0]

    def big(off, *shape, dt=F32):
        n = int(np.prod(shape))
        assert off + n <= ARENA, (off, shape)
        placed[0] += 1
        v = nc.alloc_sbuf_tensor_at(f"b{placed[0]}_{off}", [128, n], dt, offset=arena_at + 4 * off)[:, :]
        if len(shape) == 1:
            return v
        if len(shape) == 2:
            return v.rearrange("p (a b) -> p a b", b=shape[1])
        if len(shape) == 3:
            return v.rearrange("p (a b c) -> p a b c", b=shape[1], c=shape[2])
        return v.rearrange("p (a b c d) -> p a b c d", b=shape[1], c=shape[2], d=shape[3])

    def big2(off, *shape):
        n = int(np.prod(shape))
        return [big(off, *shape, dt=F32R), big(off + n, *shape, dt=F32R)]

    def bc(ap, n):
        return ap.unsqueeze(1).broadcast_to([ap.shape[0], n, ap.shape[-1]])

    t_vec = P.dma("vec", VEC[:, :], ins["vecs"])
    t_cst = P.dma("cst", CST[:, :], ins["cst"])
    t_x = [P.dma(f"x{i}", X[:, i * 512:(i + 1) * 512], ins["xT"][:, i * 512:(i + 1) * 512], eng="act") for i in range(4)]
    t_c = [t_vec, t_cst]

    loaded = [0]
    places = []
    gave = [None] * NSPL
    LOW_MIX, LOW_FFN = ["dve", "pool", "pool"] * 2, ["dve", "pool", "dve", "pool", "dve", "pool"]
    low = [LOW_MIX]

    def reserve_split():
        i = len(places)
        places.append((P.reserve("act"), P.reserve(low[0][i % 6])))

    for _ in range(AHEAD):
        reserve_split()

    def take_w(src, m, n):
        i = loaded[0]
        loaded[0] += 1
        reserve_split()
        fi, buf, free = WF.take()
        v = buf[:, 0:m * n]
        tok = P.dma(f"w{fi}", v.rearrange("p (m n) -> p m n", n=n), src, free)
        z = i % NSPL
        hi, lo = WH[z][:, 0:m * n], WL[z][:, 0:m * n]
        (ph, pl) = places[i]
        P.fill(ph, lambda e: e.activation(hi, v, ACT.Copy), tok, gave[z])
        P.fill(pl, lambda e: e.tensor_tensor(lo, v, hi.bitcast(F32), ALU.subtract), tok, gave[z], ph[2])
        WF.give(fi, ph[2], pl[2])
        gave[z] = "taken"
        return z, hi, lo, [ph[2], pl[2]]

    def give_w(z, *tok):
        gave[z] = flat(tok)

    def products(out, stat, mov, first, last):
        return [(out, stat[0], mov[0], first, False), (out, stat[0], mov[1], False, False), (out, stat[1], mov[0], False, last)]

    def unit(arr, b0, m, k0, k1):
        return arr[b0:b0 + m, :, k0 * 128:k1 * 128].rearrange("b p n -> p b n"), m, (k1 - k0) * 128

    def chunks(kt):
        c = -(-kt // 8)
        cuts = [round(kt * i / c) for i in range(c + 1)]
        return list(zip(cuts, cuts[1:]))

    def gemm(banks, kt, rhs, dep, consume, ring=None):
        ring = ring or Gb
        byk = isinstance(dep, dict)
        wide = SLOT // (kt * 128) if kt <= 4 else 1
        for n, bank in enumerate(banks):
            bi, ps, free = ring.take()
            held = None
            for t, (arr, b) in enumerate(bank):
                for a0, a1 in chunks(kt):
                    b0 = b - b % wide
                    key = (id(arr), b0, a0)
                    if held is None or held[0] != key:
                        if held is not None:
                            give_w(held[1][0], tok)
                        held = (key, take_w(*unit(arr, b0, wide, a0, a1)))
                    z, hi, lo, wt = held[1]
                    o = (b - b0) * kt * 128
                    for g in ([(k, k + 1) for k in range(a0, a1)] if byk and n == 0 and t == 0 else [(a0, a1)]):
                        items = []
                        for k in range(*g):
                            c = slice(o + (k - a0) * 128, o + (k - a0 + 1) * 128)
                            items += products(ps[:, t * S:(t + 1) * S], (hi[:, c], lo[:, c]), rhs(k), k == 0, k == kt - 1)
                        tok = mms(items, wt, free, dep[g[0]] if byk else dep)
            give_w(held[1][0], tok)
            ring.give(bi, consume(n, ps, tok))
            yield

    def pairs(arr, b0, nb):
        return [[(arr, b) for b in range(i, min(i + 2, b0 + nb))] for i in range(b0, b0 + nb, 2)]

    def split(dst, src, dep, n=None, eng="pool"):
        a = P.put("act", lambda e: e.activation(dst[0], src, ACT.Copy), dep)
        b = P.put(eng, lambda e: e.tensor_tensor(dst[1], src, dst[0].bitcast(F32), ALU.subtract), dep, a)
        return [a, b]

    rs_last = [None]

    def rsqrt(dst, src, scale, eps, dep, w, final=1.0, floor=None):
        pp = src.shape[0]
        v, t = RS[0:pp, 0:w], RS[0:pp, 48:48 + w]
        y = RS[0:pp, 96:96 + w]
        if floor is None:
            k = ts("dve", v, src, float(scale), float(eps), MUL, ADD, dep, rs_last[0])
        else:
            k = ts("dve", v, src, float(floor), None, MAX, None, dep, rs_last[0])
        k = ts("dve", y.bitcast(I32), v.bitcast(I32), -0.5, float(0x5f3759df), MUL, ADD, k)
        for c in (3.0, 12.0):
            k = tt("dve", t, y, y, MUL, k)
            k = tt("dve", t, t, v, MUL, k)
            k = stt("dve", y, t, c, y, SUB, MUL, k)
        k = tt("dve", t, y, y, MUL, k)
        k = tt("dve", t, t, v, MUL, k)
        k = ts("dve", t, t, float(-final / 8192.0), float(final * 0.09375), MUL, ADD, k)
        k = tt("dve", dst, t, y, MUL, k)
        rs_last[0] = k
        return k

    def squares(src, nt):
        ai, pa, fa = Ab.take()
        return dict(src=src, nt=nt, ai=ai, pa=pa, fa=fa, wait=[], k=None)

    def add_sums(o, keep=0):
        while len(o["wait"]) > keep:
            t0, si, sqv, a = o["wait"].pop(0)
            nt, pa = o["nt"], o["pa"]
            o["k"] = mms([(pa[:, b * nt + t0 + u:b * nt + t0 + u + 1], sqv[:, u, b * 128:(b + 1) * 128], ONES[:, 0:1], True, True)
                          for u in range(2) for b in range(2)], a, o["fa"], t_c)
            Scr.give(si, o["k"])

    def add_pair(o, t0, dep, keep=1):
        si, sq, sfree = Scr.take()
        sqv = sq.rearrange("p (t s) -> p t s", s=S)
        o["wait"].append((t0, si, sqv, act(sqv, o["src"][:, t0:t0 + 2, :], ACT.Square, dep, sfree)))
        add_sums(o, keep)

    def mean_rs(src, nt, scale, eps, dep, final=1.0):
        if isinstance(dep, dict):
            o = dep
        else:
            o = squares(src, nt)
            for t0 in range(0, nt, 2):
                add_pair(o, t0, dep[t0 // 2] if nt == 8 and len(dep) == 4 else dep, keep=2)
                if t0 % 4 == 2 or t0 + 2 >= nt:
                    yield
                    add_sums(o)
        add_sums(o)
        ai, pa, k = o["ai"], o["pa"], o["k"]
        si, r, sfree = Scr.take()
        k = P.put("dve", lambda e: e.reduce_sum(r[:, 0:2], pa[:, 0:2 * nt].rearrange("p (b t) -> p b t", b=2), AXX), k, sfree)
        Ab.give(ai, k)
        k = rsqrt(r[:, 2:4], r[:, 0:2], scale, eps, k, 2, final=final)
        yield
        ci, pc, fc = Ab.take()
        k = mms([(pc[:, b * 128:(b + 1) * 128], r[:, 2 + b:3 + b].broadcast_to([128, 128]), IDENT, True, True) for b in range(2)], k, fc)
        Scr.give(si, k)
        return ci, pc, k

    def head_rs(src, nt, scale, eps, dep, use, heads=2, floor=None):
        ai, pa, fa = Ab.take()
        w = heads
        ind = BONES[:, 63:65] if heads == 2 else ONES[:, 0:1]
        for t0 in range(0, nt, 2):
            m = min(2, nt - t0)
            si, sq, sfree = Scr.take()
            sqv = sq[:, 0:m * S].rearrange("p (t s) -> p t s", s=S)
            a = act(sqv, src[:, t0:t0 + m, :], ACT.Square, dep, sfree)
            k = mms([(pa[:, ((t0 + u) * 2 + b) * w:((t0 + u) * 2 + b + 1) * w], sqv[:, u, b * 128:(b + 1) * 128], ind, True, True)
                     for u in range(m) for b in range(2)], a, fa, t_c)
            Scr.give(si, k)
            yield
        si, r, sfree = Scr.take()
        n = nt * 2 * w
        k = rsqrt(r[:, 0:n], pa[:, 0:n], scale, eps, [k, sfree], n, floor=floor)
        Ab.give(ai, k)
        yield
        toks, last = [], None
        for t0 in range(0, nt, 2):
            m = min(2, nt - t0)
            bi, ps, free = Ab.take()
            items = []
            for u in range(m):
                for b in range(2):
                    c = ((t0 + u) * 2 + b) * w
                    g = 128 // w
                    items += [(ps[e * g:(e + 1) * g, u * S + b * 128:u * S + (b + 1) * 128], r[:, c + e:c + e + 1].broadcast_to([128, g]), IDENT, True, True)
                              for e in range(w)]
            last = mms(items, k, free)
            x = use(t0, m, ps[:, 0:m * S].rearrange("p (t s) -> p t s", s=S), last)
            Ab.give(bi, x)
            toks.append(x)
        Scr.give(si, last)
        return toks

    def rmsnorm(src, nt, gkey, l, dst, dep, wfree=None, sums=None):
        ci, pc, k = yield from mean_rs(src, nt, 1.0 / (128 * nt), 1e-6, sums or dep)
        toks, last = {}, []
        for t in range(0, nt, 2):
            si, s, sfree = Scr.take()
            s3 = s.rearrange("p (t s) -> p t s", s=S)
            a = [stt("dve", s3[:, u, :], src[:, t + u, :], vec(gkey, l, t + u), pc[:, 0:S], MUL, MUL, k, dep, sfree, t_c) for u in range(2)]
            last += a
            x = split([d[:, t:t + 2, :] for d in dst], s3, [a, wfree], eng="dve" if t % 4 == 0 else "pool")
            Scr.give(si, x)
            toks[t] = toks[t + 1] = x
        Ab.give(ci, last)
        return toks

    def residual_rms(m, gkey, l, dep, fac, sums):
        ci, pc, k = yield from mean_rs(m, 8, fac * fac / 1024, 1e-6, sums, final=fac)
        toks, last = [], []
        for t in range(8):
            a = stt("dve", m[:, t, :], m[:, t, :], vec(gkey, l, t), pc[:, 0:S], MUL, MUL, k, dep)
            last.append(a)
            toks.append(tt("pool" if t % 2 else "dve", x3[:, t, :], x3[:, t, :], m[:, t, :], ADD, a))
            if t == 1:
                xs[0] = squares(x3, 8)
            if t % 2:
                add_pair(xs[0], t - 1, toks[-2:], keep=0)
        Ab.give(ci, last)
        return [toks[2 * n:2 * n + 2] for n in range(4)]

    def sigmoid_in(o, a, *dep, bias=None, eng="dve"):
        k = act(o, a, ACT.Tanh, *dep, bias=bias, scale=0.5)
        return ts(eng, o, o, 0.5, 0.5, MUL, ADD, k), k

    def attention(nh, q, kk, scale, v, dst, dv, dep, nks=(256, 256), pen=None, done=None, lag=1, gap=0.5):
        kept = {}
        for h in range(nh + lag):
            if h < nh:
                bi, ps, free = Ab.take()
                s3 = ps[:, :].rearrange("p (b s) -> p b s", s=S)
                t = mms([(s3[:, b, 0:nks[b]], q(h)[:, b * 128:(b + 1) * 128], kk(h)[:, 0:nks[b]], True, True) for b in range(2)],
                        dep, free)
                si, pr, sfree = Scr.take()
                p3 = pr.rearrange("p (b s) -> p b s", s=S)
                ti, st, tfree = Stat.take()
                ui, su, ufree = Stat.take()
                if pen is None:
                    m = P.put("dve", lambda e, o=st[:, 0:2], i=s3: e.reduce_max(o, i, AXX), t, tfree)
                    m = ts("dve", st[:, 2:4], st[:, 0:2], -float(scale), None, MUL, None, m)
                    ex = []
                    for b in range(2):
                        ex.append(act(p3[:, b, :], s3[:, b, :], ACT.Exp, m, sfree, ufree, bias=st[:, 2 + b:3 + b], scale=float(scale),
                                      acc=su[:, b:b + 1]))
                    Ab.give(bi, ex)
                else:
                    ms = [stt("dve", p3[:, b, 0:nks[b]], s3[:, b, 0:nks[b]], float(scale), pen(b), MUL, ADD, t, sfree, dep)
                          for b in range(2)]
                    Ab.give(bi, ms)
                    m = [P.put("dve", lambda e, o=st[:, b:b + 1], i=p3[:, b, 0:nks[b]]: e.reduce_max(o, i, AXX), ms[b], tfree)
                         for b in range(2)]
                    m = ts("dve", st[:, 2:4], st[:, 0:2], -1.0, None, MUL, None, m)
                    ex = []
                    for b in range(2):
                        ex.append(act(p3[:, b, 0:nks[b]], p3[:, b, 0:nks[b]], ACT.Exp, m, ufree, bias=st[:, 2 + b:3 + b],
                                      acc=su[:, b:b + 1]))
                rc = P.put("dve", lambda e, o=su[:, 2:4], i=su[:, 0:2]: e.reciprocal(o, i), ex)
                sc = [ts("dve", p3[:, b, 0:nks[b]], p3[:, b, 0:nks[b]], su[:, 2 + b:3 + b], None, MUL, None, rc) for b in range(2)]
                Stat.give(ti, ex)
                Stat.give(ui, sc)
                kept[h] = (si, p3, sc)
                yield
            if h >= lag:
                g = h - lag
                si, p3, sc = kept.pop(g)
                bi, ps, free = Ab.take()
                tp = ps[:, :].rearrange("p (k s) -> p k s", s=S)
                todo = [(tp[:, kt, b * 128:(b + 1) * 128], p3[:, b, kt * 128:(kt + 1) * 128], None, True, True)
                        for b in range(2) for kt in range(nks[b] // 128)]
                t = mms(todo, sc, free, t_c)
                Scr.give(si, t)
                pi, pt, pfree = Scr.take()
                pt3 = pt.rearrange("p (k s) -> p k s", s=S)
                if nks[0] == 256:
                    c = [cp("act", pt, ps[:, :], t, pfree)]
                else:
                    c = [cp("act", pt3[:, 0, :], tp[:, 0, :], t, pfree), cp("act", pt3[:, 1, 128:256], tp[:, 1, 128:256], t, pfree)]
                Ab.give(bi, c)
                yield gap
                bi, ps, free = Ab.take()
                items = []
                if nks[0] == 256:
                    items = [(ps[0:dv, 0:S], v(g, kt), pt3[:, kt, :], kt == 0, kt == 1) for kt in range(2)]
                else:
                    items = [(ps[0:dv, 0:128], v(g, 0), pt3[:, 0, 0:128], True, True),
                             (ps[0:dv, 128:256], v(g, 0), pt3[:, 0, 128:256], True, False),
                             (ps[0:dv, 128:256], v(g, 1), pt3[:, 1, 128:256], False, True)]
                t = mms(items, c, free, dep)
                Scr.give(pi, t)
                c = cp("dve", dst(g), ps[0:dv, 0:S], t)
                Ab.give(bi, c)
                done.append(c)
                yield

    def run(g):
        for _ in g:
            pass

    def interleave(gens, weights):
        gens = [[g, w, 0.0] for g, w in zip(gens, weights)]
        while gens:
            gens.sort(key=lambda a: a[2])
            a = gens[0]
            try:
                a[2] += a[1] * (next(a[0]) or 1)
            except StopIteration:
                gens.pop(0)

    TWO_PI = 2 * np.pi
    C1 = 6.28125
    C2 = float(np.float32(np.round((TWO_PI - C1) * 2**20) / 2**20))
    C3 = float(TWO_PI - C1 - C2)
    MAGIC = 12582912.0

    def rope_tables(key, pos, freq):
        si, sc, sf = Scr.take()
        ki, kk2, kf = Scr.take()
        pi = sc[:, 0:S].bitcast(I32)
        t = P.dma("pos", pi, pos.partition_broadcast(128), sf, kf, eng="act")
        ang, kx = sc[:, 256:512], kk2[:, 0:S]
        a = ts("dve", ang, pi, freq, None, MUL, None, t, t_c)
        r = []
        for j, (shift, add) in enumerate(((0.25, np.pi / 2), (0.0, 0.0))):
            o = ROPE[:, j * S:(j + 1) * S]
            k = ts("dve", kx, ang, float(1 / TWO_PI), float(shift), MUL, ADD, a)
            k = ts("dve", kx, kx, MAGIC, None, ADD, None, k)
            k = ts("dve", kx, kx, -MAGIC, None, ADD, None, k)
            k = stt("dve", o, kx, -C1, ang, MUL, ADD, k)
            k = stt("dve", o, kx, -C2, o, MUL, ADD, k)
            a = k = stt("dve", o, kx, -C3, o, MUL, ADD, k)
            k = ts("dve", o, o, float(add), None, ADD, None, k)
            k = ts("dve", o, o, 3.1415925, -3.1415925, MIN, MAX, k)
            r.append(act(o, o, ACT.Sin, k))
        Scr.give(si, a)
        Scr.give(ki, a)
        return r

    t_rope = [None]
    xdep = list(t_x)
    xs = [None]

    def start(key, l):
        snap = P.now()
        hd = yield from rmsnorm(x3, 8, key, l, h2, list(xdep), wfree=snap[0], sums=xs[0])
        P.barrier(snap)
        P.snap = snap
        return hd


    def block1_mix(l):
        low[0] = LOW_MIX
        hd = yield from start("nmp", l)
        wa, wb, wkr, w_uq, w_ukv = ins["w_in_a"][l], ins["w_in_b"][l], ins["w_kr"][l], ins["w_uq"][l], ins["w_ukv"][l]
        G = big(0, 32, S)
        CP2 = big2(8192, 4, S)
        C = big(10240, 4, S)
        QT = big(11264, 8, S)
        KT = big(13312, 8, S)
        V = big(15360, 2, 512)
        O = big(16384, 4, S)
        Bc = big(17408, 4, S)
        CA = big(18432, 4, 288)
        ZS = big(19584, 4, 258)
        CY = big(20616, 4, S)
        GU = big(21640, 4, S)
        GV = big(22664, 2, 512)
        GR = big(23688, 1536)
        WS = big(25224, 512)
        BcS, GUS, CYS = big2(25736, 4, S), big2(27784, 4, S), big2(29832, 4, S)
        now = P.snap
        t_gr = [P.dma("gr0", GR[:, 0:512], ins["gm_ln_g"][l].partition_broadcast(128), now, eng="act"),
                P.dma("gr1", GR[:, 512:1024], ins["gm_ln_b"][l].partition_broadcast(128), now, eng="act"),
                P.dma("gr2", GR[:, 1024:1536], ins["gm_bs"][l].rearrange("g t -> (g t)").partition_broadcast(128), now, eng="act")]
        t_ws = P.dma("ws", WS[:, :], ins["gm_wsT"][l], now, eng="act")
        cos1, sin1 = ROPE[:, 0:S], ROPE[:, S:2 * S]

        rhs = lambda k: (h2[0][:, k, :], h2[1][:, k, :])
        hall = list(hd.values())
        yield
        cdone = []

        def put_c(dst, t0):
            def f(n, ps, tok):
                c = cp("act", dst[:, t0 + 2 * n:t0 + 2 * n + 2, :], ps[:, :].rearrange("p (t s) -> p t s", s=S), tok)
                cdone.append(c)
                return c
            return f
        yield from gemm(pairs(wa, 0, 4), 8, rhs, hd, put_c(C, 0))
        kdone = []
        latent = {}

        def norms():
            if t_rope[0] is None:
                t_rope[0] = rope_tables(0, ins["positions"], IF1)
            latent["q"] = (yield from rmsnorm(C[:, 0:2, :], 2, "qn", l, [x[:, 0:2, :] for x in CP2], cdone))[0]
            yield
            latent["k"] = (yield from rmsnorm(C[:, 2:4, :], 2, "kvn", l, [x[:, 2:4, :] for x in CP2], cdone))[0]
            yield
            ki, kr, kfree = Scr.take()
            kk1 = []

            def put_kr(n, ps, tok):
                kk1.append(cp("act", kr[0:96, 0:S], ps[0:96, 0:S], tok, kfree))
                return kk1[-1]
            yield from gemm([[(wkr, 0)]], 8, rhs, hall, put_kr)
            bi, ps, free = Gb.take()
            t = mms([(ps[0:96, S:2 * S], ROT96[0:96, 0:96], kr[0:96, 0:S], True, True)], kk1, free)
            b1 = tt("dve", kr[64:96, 0:S], kr[64:96, 0:S], cos1[64:96, :], MUL, t, t_rope)
            b2 = tt("dve", kr[64:96, S:2 * S], ps[64:96, S:2 * S], sin1[64:96, :], MUL, t)
            Gb.give(bi, b2)
            kdone.append(tt("dve", KT[64:96, :, :], bc(kr[64:96, 0:S], 8), bc(kr[64:96, S:2 * S], 8), ADD, b1, b2))
            Scr.give(ki, kdone)
            yield

        zc = P.put("pool", lambda e: e.memset(CA[:, :, :], 0.0))
        zs = P.put("pool", lambda e: e.memset(ZS[:, :, :], 0.0))
        az = []

        def put_a(n, ps, tok):
            c = cp("act", CA[:, 2 * n:2 * n + 2, 15:271], ps[:, :].rearrange("p (t s) -> p t s", s=S), tok, zc)
            az.append(c)
            return c

        def put_g(n, ps, tok):
            si, s, sf = Scr.take()
            a = act(s, ps[:, :], ACT.Tanh, tok, sf, scale=0.5)
            b = ts("dve", s, s, 0.5, 0.5, MUL, ADD, a)
            c = tt("dve", CA[:, 2 * n:2 * n + 2, 15:271], CA[:, 2 * n:2 * n + 2, 15:271], s.rearrange("p (t s) -> p t s", s=S), MUL, b, az[n])
            az[n] = c
            Scr.give(si, c)
            return a

        def products1():
            yield from gemm(pairs(wb, 12, 4), 8, rhs, hall, put_a)
            yield from gemm(pairs(wb, 16, 4), 8, rhs, hall, put_g)
        interleave([products1(), norms()], IW1)
        cq, ck = latent["q"], latent["k"]

        last = {}

        def conv():
            for t in range(4):
                last[t] = ts("dve", CY[:, t, :], CA[:, t, 0:S], vec("cfw", l, t), vec("cfb", l, t), MUL, ADD, az)
            yield
            for k in range(1, 31):
                for t in range(4):
                    last[t] = stt("dve", CY[:, t, :], CA[:, t, k:k + S], vec("cfw", l, 4 * k + t), CY[:, t, :], MUL, ADD, last[t])
                yield
            toks = list(last.values())
            bi, ps, free = Ab.take()
            m = mms([(ps[:, 0:S], ONES, CY[:, t, :], t == 0, t == 3) for t in range(4)], toks, free)
            si, s, sf = Scr.take()
            mean = ts("dve", s[:, 0:S], ps[:, 0:S], 1.0 / 512, None, MUL, None, m, sf)
            Ab.give(bi, mean)
            cen = [tt("dve", CY[:, 2 * i:2 * i + 2, :], CY[:, 2 * i:2 * i + 2, :], bc(s[:, 0:S], 2), SUB, mean, toks) for i in range(2)]
            yield
            ci, pc, k = yield from mean_rs(CY, 4, 1.0 / 512, 1e-6, cen)
            yield
            fin, nrm, out2 = [], [], []
            for p in range(2):
                a = tt("dve", CY[:, 2 * p:2 * p + 2, :], CY[:, 2 * p:2 * p + 2, :], bc(pc[:, 0:S], 2), MUL, k)
                nrm.append(a)
                ti, th, tf = Scr.take()
                z3 = CY[:, 2 * p:2 * p + 2, :]
                a = [ts("dve", CY[:, t, :], CY[:, t, :], vec("clg", l, t), vec("clb", l, t), MUL, ADD, a) for t in (2 * p, 2 * p + 1)]
                t3 = th.rearrange("p (t s) -> p t s", s=S)
                b = act(t3, z3, ACT.Tanh, a, tf, scale=0.5)
                b = stt("dve", z3, t3, 1.0, z3, ADD, MUL, b)
                b = ts("dve", z3, z3, 0.5, None, MUL, None, b)
                Scr.give(ti, b)
                fin.append(b)
                out2.append(split([x[:, 2 * p:2 * p + 2, :] for x in CYS], z3, b))
                yield
            Ab.give(ci, nrm)
            Scr.give(si, fin)
            last["y"] = out2

        def gelu(dst, src, w, tok, free):
            si, s, sf = Scr.take()
            a = act(s[:, 0:w], src, ACT.Square, tok, sf)
            a = ts("dve", s[:, 0:w], s[:, 0:w], 0.044715, 1.0, MUL, ADD, a)
            a = tt("dve", s[:, 0:w], s[:, 0:w], src, MUL, a)
            a = act(s[:, 0:w], s[:, 0:w], ACT.Tanh, a, scale=float(np.sqrt(2 / np.pi)))
            a = stt("dve", s[:, 0:w], s[:, 0:w], 1.0, src, ADD, MUL, a)
            b = ts("pool", dst, s[:, 0:w], 0.5, None, MUL, None, a, free)
            Scr.give(si, b)
            return a, b

        def main():
            qdone, vdone = [], []
            cqs = lambda k: (CP2[0][:, k, :], CP2[1][:, k, :])

            def put_q(p, ps, t):
                b2i, ps2, free2 = Ab.take()
                qv = QT[0:96, 2 * p:2 * p + 2, :]
                a = cp("act", qv, ps[0:96, :].rearrange("p (t s) -> p t s", s=S), t)
                m = mms([(ps2[0:96, :], ROT96[0:96, 0:96], qv, True, True)], a, free2)
                si, s, sf = Scr.take()
                qr = QT[64:96, 2 * p:2 * p + 2, :]
                s3 = s[64:96, :].rearrange("p (t s) -> p t s", s=S)
                b = tt("dve", qr, qr, bc(cos1[64:96, :], 2), MUL, m)
                c = tt("dve", s3, ps2[64:96, :].rearrange("p (t s) -> p t s", s=S), bc(sin1[64:96, :], 2), MUL, m, sf)
                Ab.give(b2i, c)
                d = tt("dve", qr, qr, s3, ADD, b, c)
                Scr.give(si, d)
                qdone.append(d)
                return a
            yield from gemm(pairs(w_uq, 0, 8), 2, cqs, cq, put_q)

            def put_k(p, ps, t):
                a = cp("act", KT[0:64, 2 * p:2 * p + 2, :], ps[0:64, :].rearrange("p (t s) -> p t s", s=S), t)
                kdone.append(a)
                return a
            yield from gemm(pairs(w_ukv, 0, 8), 2, lambda k: cqs(k + 2), ck, put_k)
            bks = [Gb.take() for _ in range(2)]
            for g in range(2):
                z, hi, lo, wt = take_w(*unit(w_ukv, 4 * g, 4, 0, 2))
                for tb in range(2):
                    items = []
                    for h in range(4):
                        for k in range(2):
                            c = slice(h * 256 + k * 128 + 64, h * 256 + k * 128 + 128)
                            items += products(bks[tb][1][:, (4 * g + h) * 64:(4 * g + h + 1) * 64],
                                              [x[:, tb * 128:(tb + 1) * 128] for x in cqs(k + 2)], (hi[:, c], lo[:, c]), k == 0, k == 1)
                    t = mms(items, ck, wt, bks[tb][2])
                    if g:
                        a = cp("act", V[:, tb, :], bks[tb][1][:, :], t)
                        Gb.give(bks[tb][0], a)
                        vdone.append(a)
                give_w(z, t)
            yield
            odone = []
            o = lambda h: O[(h % 2) * 64:(h % 2) * 64 + 64, h // 2, :]
            yield from attention(8, lambda h: QT[0:96, h, :], lambda h: KT[0:96, h, :], 96 ** -0.5,
                                 lambda h, kt: V[:, kt, h * 64:(h + 1) * 64], o, 64, [qdone, kdone, vdone], done=odone, gap=1)
            last["o"] = split(CP2, O, [odone, vdone, qdone, kdone])

        def rest():
            bd, cd = [], []

            def put_b(n, ps, tok):
                c = cp("act", Bc[:, 2 * n:2 * n + 2, :], ps[:, :].rearrange("p (t s) -> p t s", s=S), tok)
                bd.append(c)
                return c

            def put_cc(n, ps, tok):
                c = cp("act", ZS[:, 2 * n:2 * n + 2, 1:257], ps[:, :].rearrange("p (t s) -> p t s", s=S), tok, zs)
                cd.append(c)
                return c

            def put_x(n, ps, tok):
                z = ZS[:, 2 * n:2 * n + 2, 1:257]
                c = tt("dve", z, ps[:, :].rearrange("p (t s) -> p t s", s=S), z, MUL, tok, cd[n])
                cd[n] = c
                return c
            yield from gemm(pairs(wb, 0, 4), 8, rhs, hall, put_b)
            yield from gemm(pairs(wb, 4, 4), 8, rhs, hall, put_cc)
            yield from gemm(pairs(wb, 8, 4), 8, rhs, hall, put_x)
            sd = []
            for t in range(4):
                si, s, sf = Scr.take()
                y = s[:, 0:S]
                a = ts("dve", y, ZS[:, t, 0:S], vec("scw", l, t), None, MUL, None, cd, sf)
                a = stt("dve", y, ZS[:, t, 1:257], vec("scw", l, 4 + t), y, MUL, ADD, a)
                a = stt("dve", y, ZS[:, t, 2:258], vec("scw", l, 8 + t), y, MUL, ADD, a)
                a = tt("pool", Bc[:, t, :], Bc[:, t, :], y, MUL, a, bd)
                Scr.give(si, a)
                sd.append(a)
            last["s"] = split(BcS, Bc, sd)
            yield
            ud, vd = [], []

            def put_u(n, ps, tok):
                a, b = gelu(GU[:, 2 * n:2 * n + 2, :].rearrange("p t s -> p (t s)"), ps[:, :], 512, tok, None)
                ud.append(b)
                return a
            yield from gemm(pairs(wb, 20, 4), 8, rhs, hall, put_u)
            bks = [Gb.take() for _ in range(2)]
            tks = [None, None]
            for g in range(4):
                z, hi, lo, wt = take_w(*unit(wb, 24 + g, 1, 0, 8))
                for tb in range(2):
                    items = []
                    for k in range(8):
                        c = slice(k * 128, (k + 1) * 128)
                        items += products(bks[tb][1][:, g * 128:(g + 1) * 128], [x[:, tb * 128:(tb + 1) * 128] for x in rhs(k)],
                                          (hi[:, c], lo[:, c]), k == 0, k == 7)
                    tks[tb] = mms(items, hall, wt, bks[tb][2])
                give_w(z, tks)
            for tb in range(2):
                bi, ps, t = bks[tb][0], bks[tb][1], tks[tb]
                gv = GV[:, tb, :]
                a, b = gelu(gv, ps[:, :], 512, t, None)
                Gb.give(bi, a)
                ti, st, tf = Stat.take()
                t2, st2, tf2 = Stat.take()
                si, s, sf = Scr.take()
                c = P.put("dve", lambda e, o=s[:, 0:6], i=gv: e.bn_stats(o, i), b, sf)
                c = P.put("dve", lambda e, o=st[:, 0:2], i=s[:, 0:6]: e.bn_aggr(o, i), c, tf)
                Scr.give(si, c)
                c = rsqrt(st2[:, 0:1], st[:, 1:2], 1.0, 1e-6, [c, tf2], w=1)
                d = ts("dve", gv, gv, st[:, 0:1], st2[:, 0:1], SUB, MUL, c)
                d = tt("dve", gv, gv, GR[:, 0:512], MUL, d, t_gr)
                d = tt("dve", gv, gv, GR[:, 512:1024], ADD, d)
                Stat.give(ti, d)
                Stat.give(t2, d)
                vd.append(d)
                yield
            yield GW
            gd = []
            for g in range(4):
                bi, ps, free = Ab.take()
                t = mms([(ps[:, n * 128:(n + 1) * 128], GV[:, n, g * 128:(g + 1) * 128], WS[:, g * 128:(g + 1) * 128], True, True)
                         for n in range(2)], vd, t_ws, free)
                si, s, sf = Scr.take()
                a = tt("dve", s[:, 0:S].rearrange("p (n t) -> p n t", n=2), ps[:, 0:S].rearrange("p (n t) -> p n t", n=2),
                       bc(GR[:, 1024 + g * 128:1024 + (g + 1) * 128], 2), ADD, t, sf, t_gr)
                Ab.give(bi, a)
                a = tt("pool", GU[:, g, :], GU[:, g, :], s[:, 0:S], MUL, a, ud)
                Scr.give(si, a)
                gd.append(a)
            last["g"] = split(GUS, GU, gd)
            yield

        def gating():
            gi, hb, gf = Scr.take()
            hbt = ts("dve", hb[:, 0:32], vec("gb", l, 0, 32), 0.5, None, MUL, None, gf, t_c)
            gates = []

            def put_gate(n, ps, tok):
                r = [act(G[:, 2 * n + u, :], ps[:, u * S:(u + 1) * S], ACT.Tanh, tok, hbt, bias=hb[:, 2 * n + u:2 * n + u + 1], scale=0.5)
                     for u in range(2)]
                gates.append(r)
                return r
            yield from gemm(pairs(wb, 28, 32), 8, rhs, hall, put_gate)
            Scr.give(gi, gates)
            last["gates"] = gates

        interleave([main(), rest(), conv(), gating()], WT1)

        M = big(11264, 8, S)
        M2 = big2(13312, 8, S)
        mt = {}
        for b, (src, key, W) in enumerate(((BcS, "s", "w_o_sc"), (GUS, "g", "w_o_gm"), (CYS, "y", "w_o_cf"), (CP2, "o", "w_o_mla"))):
            gb = {"s": 1, "g": 3, "y": 2, "o": 0}[key]

            def put_m(n, ps, tok, b=b, gb=gb):
                mv = M[:, 2 * n:2 * n + 2, :].rearrange("p t s -> p (t s)")
                gv = G[:, 8 * gb + 2 * n:8 * gb + 2 * n + 2, :].rearrange("p t s -> p (t s)")
                if b == 0:
                    a = stt("dve", mv, gv, 1.0, ps[:, :], ADD, MUL, tok, last["gates"], last["o"])
                    mt[n] = a
                    return a
                si, s, sf = Scr.take()
                a = stt("dve", s, gv, 1.0, ps[:, :], ADD, MUL, tok, sf)
                mt[n] = tt("dve" if b == 3 else "pool", mv, mv, s, ADD, a, mt[n])
                Scr.give(si, mt[n])
                if b == 3:
                    mt[n] = split([x[:, 2 * n:2 * n + 2, :] for x in M2], M[:, 2 * n:2 * n + 2, :], mt[n], eng="dve" if n % 2 else "pool")
                return a
            yield from gemm(pairs(ins[W][l], 0, 8), 4, lambda k, src=src: (src[0][:, k, :], src[1][:, k, :]), last[key], put_m)
        Y = big(0, 8, S)
        yd, ys = [], squares(Y, 8)

        def put_y(n, ps, tok):
            a = cp("act", Y[:, 2 * n:2 * n + 2, :].rearrange("p t s -> p (t s)"), ps[:, :], tok, gread)
            yd.append(a)
            add_pair(ys, 2 * n, a)
            return a
        gread = list(mt.values())
        md = {k: mt[k // 2] for k in range(8)}
        yield from gemm(pairs(ins["w_out"][l], 0, 8), 8, lambda k: (M2[0][:, k, :], M2[1][:, k, :]), md, put_y)
        xdep[:] = yield from residual_rms(Y, "npo", l, yd, 0.5, ys)

    def ffn_up(Wg, Wu, nt, F2, hd, rdy, gate=None):
        low[0] = LOW_FFN
        fd = {}

        def put_f(n, ps, tok):
            si, s, sf = Scr.take()
            t = act(s[:, 0:S], ps[:, 0:S], ACT.Tanh, tok, sf, scale=0.5)
            a = stt("dve", s[:, S:2 * S], s[:, 0:S], 1.0, ps[:, 0:S], ADD, MUL, t)
            b = c = stt("dve", s[:, 0:S], ps[:, S:2 * S], 0.5, s[:, S:2 * S], MUL, MUL, a)
            if gate is not None:
                c = tt("pool", s[:, 0:S], s[:, 0:S], gate, MUL, b, rdy)
            fd[n] = split([x[:, n, :] for x in F2], s[:, 0:S], [c, rdy], eng="dve")
            Scr.give(si, fd[n])
            return b
        yield from gemm([[(Wg, j), (Wu, j)] for j in range(nt)], 8, lambda k: (h2[0][:, k, :], h2[1][:, k, :]), hd, put_f)
        return fd

    def block1_ffn(l):
        hd = yield from start("nfp", l)
        F2 = big2(0, 22, S)
        fd = yield from ffn_up(ins["w_ffn_g"][l], ins["w_ffn_u"][l], 22, F2, hd, None)
        Y = big(11264, 8, S)
        yd, ys = [], squares(Y, 8)

        def put_y(n, ps, tok):
            a = cp("act", Y[:, 2 * n:2 * n + 2, :].rearrange("p t s -> p (t s)"), ps[:, :], tok)
            yd.append(a)
            add_pair(ys, 2 * n, a)
            return a
        yield from gemm(pairs(ins["w_ffn_out"][l], 0, 8), 22, lambda k: (F2[0][:, k, :], F2[1][:, k, :]), fd, put_y)
        xdep[:] = yield from residual_rms(Y, "nfo", l, yd, 1.0, ys)

    def add_x(n, ps, tok, fac=1.0):
        v = x3[:, 2 * n:2 * n + 2, :].rearrange("p t s -> p (t s)")
        a = stt("dve", v, ps[:, :], fac, v, MUL, ADD, tok)
        xnew.append(a)
        if n == 0:
            xs[0] = squares(x3, 8)
        add_pair(xs[0], 2 * n, a)
        return a

    xnew = []
    WT1, IW1, GW = [0.77, 0.96, 0.72, 1.58], [1.17, 1.18], 7
    IWM, RW = [1.0, 1.0], 2.0
    WT2, PJ, PREP, WT3 = [0.27, 0.5], 1, 1, [0.99, 0.98, 2.35]

    vf3 = big(21920, 4, S)
    MH = big2(22944, 8, S)
    mh = {}

    def block2_mix(l):
        low[0] = LOW_MIX
        hd = yield from start("nmix", l)
        w_in = ins["w_in_2"][l]
        SW = big(19744, 2176)
        now = P.snap
        ld = [P.dma("sw0", SW[0:64, 0:512], ins["rwkv_w2_2"][l], now, eng="act"),
              P.dma("sw1", SW[0:64, 512:1024], ins["rwkv_a2_2"][l], now, eng="act"),
              P.dma("sw2", SW[:, 1024:1536], ins["rwkv_g2_2"][l], now, eng="act")]
        if l:
            ld += [P.dma("sw3", SW[:, 1536:1664].rearrange("p (k n) -> p k n", n=32),
                         ins["rwkv_v1_2"][l - 1].rearrange("(k p) n -> p k n", p=128), now, eng="act"),
                   P.dma("sw4", SW[0:32, 1664:2176], ins["rwkv_v2_2"][l - 1], now, eng="act")]
        rhs = lambda k: (h2[0][:, k, :], h2[1][:, k, :])
        hall = list(hd.values())
        yield
        CS = big(0, 15, S)
        CP = big(12032, 15, 257)
        zc = P.put("pool", lambda e: e.memset(CP[:, :, 0:1], 0.0))
        md = []

        def mix(t0, m, pp, tok):
            a = tt("dve", CS[0:pp, t0:t0 + m, :], CP[0:pp, t0:t0 + m, 0:S], CP[0:pp, t0:t0 + m, 1:257], SUB, tok, zc)
            for t in range(t0, t0 + m):
                md.append(stt("dve", CS[0:pp, t, :], CS[0:pp, t, :], vec("mu", l, t)[0:pp, :], CP[0:pp, t, 1:257], MUL, ADD, a))

        def put_p(n, ps, tok):
            t0 = (4, 6, 8, 10, 0, 2)[n]
            a = cp("act", CP[:, t0:t0 + 2, 1:257], ps[:, :].rearrange("p (t s) -> p t s", s=S), tok)
            mix(t0, 2, 128, a)
            return a

        def put_q(n, ps, tok):
            a = [cp("act", CP[0:64, 12 + u, 1:257], ps[64 * u:64 * u + 64, 0:S], tok) for u in range(2)]
            mix(12, 2, 64, a)
            return a

        def put_r(n, ps, tok):
            a = cp("act", CP[:, 14, 1:257], ps[:, 0:S], tok)
            mix(14, 1, 128, a)
            return a
        yield from gemm([[(w_in, 12)]], 8, rhs, hd, put_q)
        yield from gemm([[(w_in, 13)]], 8, rhs, hall, put_r)
        r3, k3, v3 = CS[:, 0:4, :], CS[:, 4:8, :], CS[:, 8:12, :]
        LW, CUM, AA, GG, KK, BB = (big(3840 + 1024 * i, 4, S) for i in range(6))
        AR = big(9984, 4, 2, 2, 128)
        BT, KTl, BH, KH, Y = (big(12032 + 1024 * i, 4, S) for i in range(5))
        RP = big(17152, 4, S)
        MN = big(18176, 4, 3, 128)
        PC = big(19712, 4, 4)
        DA = big(22944, 10, S)
        V2 = big(25504, 2, 64)
        IW = big(25632, 2, 8)
        SCO, WKX, PEN = (big(25648 + 384 * i, 384) for i in range(3))
        O = big(26800, 4, S)
        GT = big(27824, 16, S)
        YAs, Os = big2(12032, 4, S), big2(14080, 4, S)
        ya = []

        kept = {}

        def rwkv():
            si, tw, sf = Scr.take()
            a = act(tw[0:64, 0:S], CS[0:64, 12, :], ACT.Tanh, md, sf)
            g1 = act(tw[:, S:2 * S], CS[:, 14, :], ACT.Tanh, md, scale=0.5)
            g1 = ts("dve", tw[:, S:2 * S], tw[:, S:2 * S], 0.5, 0.5, MUL, ADD, g1)
            hi, hbv, hf = Scr.take()
            hb = ts("dve", hbv[:, 0:4], vec("w0", l, 0, 4), 0.5, None, MUL, None, hf, t_c)
            hb = ts("dve", hbv[:, 4:8], vec("a0", l, 0, 4), 0.5, None, MUL, None, hb)
            if l:
                hb = ts("dve", hbv[:, 8:12], vec("v0", l, 0, 4), 0.5, None, MUL, None, hb)
            hb = ts("dve", hbv[:, 12:16], vec("ka", l, 0, 4), -1.0, 1.0, MUL, ADD, hb)
            cde = float(np.exp(-0.5) / 2)
            lw, aa, gg, cu = [], [], [], []

            def decays():
                for p in range(2):
                    bi, ps, free = Ab.take()
                    t = mms([(ps[:, u * S:(u + 1) * S], SW[0:64, (2 * p + u) * 128:(2 * p + u + 1) * 128], tw[0:64, 0:S], True, True) for u in range(2)], a, ld, free)
                    ac = [act(LW[:, 2 * p + u, :], ps[:, u * S:(u + 1) * S], ACT.Tanh, t, hb, md, bias=hbv[:, 2 * p + u:2 * p + u + 1], scale=0.5) for u in range(2)]
                    Ab.give(bi, ac)
                    lw.append(ts("dve", LW[:, 2 * p:2 * p + 2, :], LW[:, 2 * p:2 * p + 2, :], -cde, -cde, MUL, ADD, ac))
                    bi, ps, free = Ab.take()
                    t2 = mms([(ps[:, u * S:(u + 1) * S], SW[0:64, 512 + (2 * p + u) * 128:512 + (2 * p + u + 1) * 128], CS[0:64, 13, :], True, True) for u in range(2)], md, ld, free)
                    ac = [act(AA[:, 2 * p + u, :], ps[:, u * S:(u + 1) * S], ACT.Tanh, t2, hb, bias=hbv[:, 4 + 2 * p + u:5 + 2 * p + u], scale=0.5) for u in range(2)]
                    Ab.give(bi, ac)
                    aa.append(ts("dve", AA[:, 2 * p:2 * p + 2, :], AA[:, 2 * p:2 * p + 2, :], 0.5, 0.5, MUL, ADD, ac))
                    bi, ps, free = Ab.take()
                    t3 = mms([(ps[:, u * S:(u + 1) * S], SW[:, 1024 + (2 * p + u) * 128:1024 + (2 * p + u + 1) * 128], tw[:, S:2 * S], True, True) for u in range(2)], g1, ld, free)
                    gg.append(cp("act", GG[:, 2 * p:2 * p + 2, :].rearrange("p t s -> p (t s)"), ps[:, :], t3, md))
                    Ab.give(bi, gg[-1])
                    yield
                Scr.give(si, t2, t3)
                for t in range(4):
                    cu.append(P.put("dve", lambda e, t=t: e.tensor_tensor_scan(CUM[:, t, :], SCM, LW[:, t, :], 0.0, MUL, ADD), lw, t_c))
                yield
            side = decays()
            for _ in gemm([[(w_in, t), (w_in, t + 1)] for t in (4, 6, 8, 10, 0, 2)], 8, rhs, hall, put_p):
                yield PJ
                next(side, None)
            if l == 0:
                vdep = [cp("pool", vf3, v3, md)]
            else:
                bi, ps, free = Ab.take()
                t = mms([(ps[0:32, 0:S], SW[:, 1536 + 32 * k:1568 + 32 * k], v3[:, k, :], k == 0, k == 3) for k in range(4)], md, ld, free)
                si, s, sf = Scr.take()
                c = cp("act", s[0:32, 0:S], ps[0:32, 0:S], t, sf)
                Ab.give(bi, c)
                vdep = []
                df = tt("dve", vf3, vf3, v3, SUB, md)
                for p in range(2):
                    bi, ps, free = Ab.take()
                    t = mms([(ps[:, u * S:(u + 1) * S], SW[0:32, 1664 + (2 * p + u) * 128:1664 + (2 * p + u + 1) * 128], s[0:32, 0:S], True, True) for u in range(2)], c, ld, free)
                    di, d, df2 = Scr.take()
                    ac = [act(d[:, u * S:(u + 1) * S], ps[:, u * S:(u + 1) * S], ACT.Tanh, t, hb, df2, bias=hbv[:, 8 + 2 * p + u:9 + 2 * p + u], scale=0.5) for u in range(2)]
                    Ab.give(bi, ac)
                    x = ts("dve", d, d, 0.5, 0.5, MUL, ADD, ac)
                    x = tt("dve", d, d, vf3[:, 2 * p:2 * p + 2, :].rearrange("p t s -> p (t s)"), MUL, x, df)
                    vp = v3[:, 2 * p:2 * p + 2, :].rearrange("p t s -> p (t s)")
                    x = tt("dve", vp, vp, d, ADD, x)
                    Scr.give(di, x)
                    vdep.append(x)
                Scr.give(si, t)
                yield from fill(PREP)
            kt = [ts("dve", KK[:, t, :], k3[:, t, :], vec("kk", l, t), None, MUL, None, md) for t in range(4)]
            kn = yield from head_rs(KK, 4, 1.0, 0.0, kt, lambda t0, m, ps3, tok: tt("dve", KK[:, t0:t0 + m, :], KK[:, t0:t0 + m, :], ps3, MUL, tok),
                         floor=1e-24)
            yield from fill(PREP)
            k2 = []
            for t in range(4):
                c = ts("dve", BT[:, t, :], AA[:, t, :], vec("ka", l, t), hbv[:, 12 + t:13 + t], MUL, ADD, aa, hb, md)
                k2.append(tt("dve", k3[:, t, :], k3[:, t, :], BT[:, t, :], MUL, c, kt))
            Scr.give(hi, k2, lw, aa)
            bb = tt("dve", BB[:, :, :], KK[:, :, :], AA[:, :, :], MUL, kn, aa)
            e1 = tt("dve", LW[:, :, :], CUM[:, :, :], LW[:, :, :], SUB, cu)
            e1 = act(LW[:, :, :], LW[:, :, :], ACT.Exp, e1)
            a1 = stt("dve", AR[:, :, :, 0, :], KK[:, :, :].rearrange("p t (b s) -> p t b s", s=128), -1.0,
                     LW[:, :, :].rearrange("p t (b s) -> p t b s", s=128), MUL, MUL, e1, kn)
            e2 = act(LW[:, :, :], CUM[:, :, :], ACT.Exp, a1, cu)
            a2 = tt("dve", AR[:, :, :, 1, :], r3.rearrange("p t (b s) -> p t b s", s=128), LW[:, :, :].rearrange("p t (b s) -> p t b s", s=128), MUL, e2, md)
            cl = CUM[:, :, :].rearrange("p t (c s) -> p t c s", s=64)
            pc = act(PC[:, :, :], cl[:, :, :, 63], ACT.Exp, cu, md)
            e3 = act(LW[:, :, :], CUM[:, :, :], ACT.Exp, a2, scale=-1.0)
            b1 = tt("dve", BT[:, :, :], BB[:, :, :], LW[:, :, :], MUL, e3, bb, k2)
            b2 = tt("dve", KTl[:, :, :], k3, LW[:, :, :], MUL, e3, k2)
            yield from fill(PREP)
            e4 = []
            for t in range(4):
                e4.append(tt("dve", LW[:, t, :].rearrange("p (c s) -> p c s", s=64),
                             cl[:, t, :, 63:64].broadcast_to([128, 4, 64]), cl[:, t, :, :], SUB, b1, b2))
            e4 = act(LW[:, :, :], LW[:, :, :], ACT.Exp, e4)
            b3 = tt("dve", BH[:, :, :], BB[:, :, :], LW[:, :, :], MUL, e4, bb)
            b4 = tt("dve", KH[:, :, :], k3, LW[:, :, :], MUL, e4, k2)
            bo = [stt("dve", BB[:, t, :], r3[:, t, :], vec("rk", l, t), k3[:, t, :], MUL, MUL, b1, b3) for t in range(4)]
            bon = []
            for p in range(2):
                bi, ps, free = Ab.take()
                bp = BB[:, 2 * p:2 * p + 2, :].rearrange("p t s -> p (t s)")
                t = mms([(ps[:, :], BONES, bp, True, True)], bo, free)
                bon.append(tt("dve", bp, ps[:, :], v3[:, 2 * p:2 * p + 2, :].rearrange("p t s -> p (t s)"), MUL, t, vdep))
                Ab.give(bi, bon[-1])
            ready = [a1, a2, b1, b2, b3, b4, vdep, pc, bon, bo, gg, lw, aa]
            yield from fill(PREP)
            li, lent, lfree = Scr.take()
            WK = [big(3840, 1024), big(4864, 1024), SW[:, 0:1024]]
            WK2 = [big(5888, 1024), big(7936, 1024), SW[:, 1024:2048]]
            WK3 = [big(0, 768), big(1024, 768), big(3072, 768)]
            WK4 = [big(768, 256), big(1792, 256), lent[:, 0:256]]
            gfree = [ready, ready, [ready, lfree]]
            yd, rd, mn = [], [], []

            def group(j, blk, z):
                dep = [ready, gfree[z]]
                LT4 = WK[z].rearrange("p (e n) -> p e n", e=2)
                LL = WK2[z][:, 0:512].rearrange("p (e a n) -> p e a n", e=2, a=2)
                TT = WK2[z][:, 512:1024].rearrange("p (e a n) -> p e a n", e=2, a=2)
                TK = WK3[z][:, 0:512].rearrange("p (a n) -> p a n", a=4)
                Lf = WK3[z][:, 512:768].rearrange("p (e n) -> p e n", e=2)
                L16 = WK4[z].rearrange("p (e n) -> p e n", e=2)
                ZZ = WK2[z][:, 0:256].rearrange("p (e n) -> p e n", e=2)
                XU = WK2[z][:, 256:512].rearrange("p (e n) -> p e n", e=2)
                cols = slice(blk * 128, (blk + 1) * 128)
                bi, ps, free = Ab.take()
                t = mms([(ps[:, 0:128], AR[:, j, blk, 0, :], None, 1, 1), (ps[:, 128:256], v3[:, j, cols], None, 1, 1),
                         (ps[:, 256:384], BH[:, j, cols], None, 1, 1), (ps[:, 384:512], KH[:, j, cols], None, 1, 1)], dep, free)
                tk = cp("act", TK.rearrange("p a n -> p (a n)"), ps[:, :], t, dep)
                Ab.give(bi, tk)
                lt = []
                for e in range(2):
                    r = slice(64 * e, 64 * e + 64)
                    bi, ps, free = Ab.take()
                    ar = AR[r, j, blk, :, :].rearrange("p a n -> p (a n)")
                    t = mms([(ps[:, 0:256], BT[r, j, cols], ar, True, True), (ps[:, 256:512], KTl[r, j, cols], ar, True, True)], dep, free)
                    lt.append(tt("dve", LT4[:, e, :].rearrange("p (a n) -> p a n", a=2), ps[:, :].rearrange("p (a n) -> p a n", a=2), bc(MASKT, 2), MUL, t, dep))
                    Ab.give(bi, lt[-1])
                yield
                lf = []
                for e in range(2):
                    bi, ps, free = Ab.take()
                    r = slice(64 * e, 64 * e + 64)
                    t = mms([(ps[:, 0:128], AR[r, j, blk, 0, :], BT[r, j, cols], True, True)], dep, free)
                    lf.append(tt("dve", Lf[:, e, :], ps[:, 0:128], CST64, MUL, t, dep))
                    Ab.give(bi, lf[-1])
                d1 = tt("dve", LL[:, :, 0, :], Lf, bc(D16, 2), MUL, lf, dep)
                d2 = tt("pool", LL[:, :, 1, :], LT4[:, :, 0:128], bc(D16T, 2), MUL, lt, dep)
                i1 = tt("dve", TT[:, :, 0, :], LL[:, :, 0, :], bc(IDENT, 2), ADD, d1, dep)
                i2 = tt("pool", TT[:, :, 1, :], LL[:, :, 1, :], bc(IDENT, 2), ADD, d2, dep)
                yield
                ll, tn = [d1, d2], [i1, i2]
                l16 = tt("pool", L16, Lf, bc(C16, 2), MUL, lf, dep)
                l32 = tt("pool", Lf, Lf, bc(C32, 2), MUL, l16, d1)
                for m in range(4):
                    if m < 3:
                        bi, ps, free = Ab.take()
                        v = ps[:, :].rearrange("p (e a n) -> p e a n", e=2, a=2)
                        tl = mms([x for e in range(2) for x in ((v[:, e, 0, :], LL[:, e, 1, :], LL[:, e, 0, :], True, True),
                                                               (v[:, e, 1, :], LL[:, e, 0, :], LL[:, e, 1, :], True, True))], ll, free)
                    if m:
                        ci, pt, free = Ab.take()
                        w = pt[:, :].rearrange("p (e a n) -> p e a n", e=2, a=2)
                        t = mms([x for e in range(2) for x in ((w[:, e, 0, :], TT[:, e, 1, :], LL[:, e, 0, :], True, True),
                                                              (w[:, e, 1, :], LL[:, e, 0, :], TT[:, e, 1, :], True, True))], ll, tn, free)
                        tn = tt("dve", TT, TT, w, ADD, t)
                        Ab.give(ci, tn)
                    if m < 3:
                        ll = cp("act", LL, v, tl, [i1, i2] if m == 0 else t)
                        Ab.give(bi, ll)
                    yield
                for c, Lo in ((0, L16), (1, Lf)):
                    bi, ps, free = Ab.take()
                    t = mms([(ps[:, e * 128:(e + 1) * 128], Lo[:, e, :], TT[:, e, 1, :], True, True) for e in range(2)], tn, l16, l32, free)
                    zz = cp("act", ZZ, ps[:, 0:256].rearrange("p (e n) -> p e n", e=2), t, dep, tn)
                    Ab.give(bi, zz)
                    bi, ps, free = Ab.take()
                    v = ps[:, :].rearrange("p (e a n) -> p e a n", e=2, a=2)
                    if c == 0:
                        t = mms([x for e in range(2) for x in ((v[:, e, 0, :], ZZ[:, e, :], TT[:, e, 0, :], True, True),
                                                              (v[:, e, 1, :], TT[:, e, 0, :], ZZ[:, e, :], True, True))], zz, free)
                        tn = tt("dve", TT, TT, v, ADD, t)
                    else:
                        t = mms([(v[:, e, 1, :], TT[:, e, 0, :], ZZ[:, e, :], True, True) for e in range(2)], zz, free)
                        tn = tt("dve", TT[:, :, 1, :], TT[:, :, 1, :], v[:, :, 1, :], ADD, t)
                    Ab.give(bi, tn)
                    yield
                bi, ps, free = Ab.take()
                t = mms([(ps[:, e * 64:(e + 1) * 64], LT4[:, e, 256:384], TK[:, 1, e * 64:(e + 1) * 64], True, True) for e in range(2)], lt, tk, free)
                xc = cp("act", ZZ[:, 0, :], ps[:, 0:128], t, tn)
                Ab.give(bi, xc)
                bi, ps, free = Ab.take()
                v = ps[:, 0:256].rearrange("p (e n) -> p e n", e=2)
                t = mms([x for e in range(2) for x in ((v[:, e, 0:64], TT[:, e, 1, :], TK[:, 0, e * 64:(e + 1) * 64], True, True),
                                                      (v[:, e, 64:128], TT[:, e, 1, :], ZZ[:, 0, e * 64:(e + 1) * 64], True, True))], xc, tn, tk, free)
                xu = cp("act", XU, v, t, dep)
                Ab.give(bi, xu)
                yield
                bi, ps, free = Ab.take()
                q = [slice(64 * e, 64 * e + 64) for e in range(2)]
                t = mms([x for e in range(2) for x in (
                    (ps[q[e], 0:128], XU[:, e, 0:64], LT4[:, e, 128:256], True, True),
                    (ps[q[e], 128:256], XU[:, e, 64:128], LT4[:, e, 128:256], True, False),
                    (ps[q[e], 128:256], TK[:, 1, q[e]], LT4[:, e, 384:512], False, True))], xu, free)
                o = [tt("dve", RP[:, j, cols], ps[:, 0:128], AR[:, j, blk, 1, :], ADD, t, dep),
                     cp("dve", Y[:, j, cols], ps[:, 128:256], t, dep)]
                Ab.give(bi, o)
                rd.append(o)
                mm = []
                for c in range(2):
                    ch = 2 * blk + c
                    if ch == 3:
                        continue
                    r = slice(64 * c, 64 * c + 64)
                    bi, ps, free = Ab.take()
                    items = []
                    for e in range(2):
                        items += [(ps[q[e], 0:64], XU[r, e, 0:64], TK[r, 2, q[e]], True, True),
                                  (ps[q[e], 64:128], TK[r, 2, q[e]], XU[r, e, 64:128], True, False),
                                  (ps[q[e], 64:128], TK[r, 3, q[e]], TK[r, 1, q[e]], False, True)]
                    t = mms(items, xu, tk, free)
                    c2 = [cp("dve", MN[:, j, ch, 64:128], ps[:, 64:128], t, dep),
                          stt("dve", MN[:, j, ch, 0:64], ID64, PC[:, j, ch:ch + 1], ps[:, 0:64], MUL, ADD, t, dep)]
                    Ab.give(bi, c2)
                    mm.append(c2)
                mn.append(mm)
                gfree[z] = [o, mm, t]
                yield

            groups = [(j, b) for j in range(4) for b in range(2)]

            def worker(z):
                while groups:
                    yield from group(*groups.pop(0), z)
            busy = [worker(z) for z in range(3)]
            while busy:
                for w in list(busy):
                    if next(w, "end") == "end":
                        busy.remove(w)
                    yield
            Scr.give(li, gfree[2])
            kept.update(mn=mn, gfree=gfree, rd=rd, gg=gg, bon=bon)

        def tail():
            mn, gfree, rd, gg, bon = (kept[k] for k in ("mn", "gfree", "rd", "gg", "bon"))
            SS = LW.rearrange("p t s -> p (t s)")[:, 0:512].rearrange("p (c j n) -> p c j n", c=2, n=64)
            st = [MN[:, :, 0, 64:128], SS[:, 0, :, :], SS[:, 1, :, :]]
            sd = [mn, gfree]
            q = [slice(64 * e, 64 * e + 64) for e in range(2)]
            for c in range(1, 3):
                new = []
                for e in range(2):
                    bi, ps, free = Ab.take()
                    t = mms([(ps[q[e], j * 64:(j + 1) * 64], MN[q[e], j, c, 0:64], st[c - 1][q[e], j, :], True, True) for j in range(4)], sd, free)
                    new.append(tt("dve", st[c][q[e], :, :], ps[q[e], 0:256].rearrange("p (j n) -> p j n", n=64), MN[q[e], :, c, 64:128], ADD, t, sd))
                    Ab.give(bi, new[-1])
                sd = [sd, new]
            yy = []
            for g in range(2):
                for e in range(2):
                    bi, ps, free = Ab.take()
                    v = ps[q[e], 0:384].rearrange("p (j n) -> p j n", n=192)
                    t = mms([(v[:, u, 64 * c:64 * c + 64], st[c][q[e], 2 * g + u, :], RP[q[e], 2 * g + u, 64 * c + 64:64 * c + 128], True, True)
                             for u in range(2) for c in range(3)], sd, rd, free)
                    yv = Y[q[e], 2 * g:2 * g + 2, 64:256]
                    yy.append(tt("dve", yv, v, yv, ADD, t, rd))
                    Ab.give(bi, yy[-1])
            yield
            cen = []
            for p in range(2):
                bi, ps, free = Ab.take()
                yp = Y[:, 2 * p:2 * p + 2, :].rearrange("p t s -> p (t s)")
                t = mms([(ps[:, :], BONES, yp, True, True)], yy, free)
                cen.append(stt("dve", yp, ps[:, :], -1.0 / 64, yp, MUL, ADD, t))
                Ab.give(bi, cen[-1])
            a = yield from head_rs(Y, 4, 1.0 / 64, 1e-5 * 64, cen, lambda t0, m, ps3, tok: tt("dve", Y[:, t0:t0 + m, :], Y[:, t0:t0 + m, :], ps3, MUL, tok))
            fin = []
            for t in range(4):
                b = ts("dve", Y[:, t, :], Y[:, t, :], vec("lxg", l, t), vec("lxb", l, t), MUL, ADD, a)
                b = tt("pool", Y[:, t, :], Y[:, t, :], BB[:, t, :], ADD, b, bon)
                fin.append(tt("pool", Y[:, t, :], Y[:, t, :], GG[:, t, :], MUL, b, gg))
            ya.append(split(YAs, Y, fin))
            yield
        odone, gates = [], []

        def sparse():
            dd = []
            if l == 0:
                t_rope[0] = rope_tables(1, ins["positions_2"], IF2)

            def put_d(t0):
                def f(n, ps, tok):
                    a = cp("act", DA[:, t0 + 2 * n:t0 + 2 * n + 2, :], ps[:, :].rearrange("p (t s) -> p t s", s=S), tok)
                    dd.append(a)
                    return a
                return f
            yield from gemm(pairs(w_in, 14, 4), 8, rhs, hall, put_d(0))
            for j, n in ((0, 64), (1, 8)):
                z, hi, lo, wt = take_w(*unit(w_in, 18 + 5 * j, 1, 0, 8))
                bi, ps, free = Gb.take()
                items = []
                for k in range(8):
                    c = slice(k * 128, (k + 1) * 128)
                    items += products(ps[:, 0:S], (hi[:, c], lo[:, c]), rhs(k), k == 0, k == 7)
                for tb in range(2):
                    for k in range(8):
                        c = slice(k * 128 + 64, k * 128 + 64 + n)
                        items += products(ps[:, S + 64 * tb:S + 64 * tb + n], [x[:, tb * 128:(tb + 1) * 128] for x in rhs(k)],
                                          (hi[:, c], lo[:, c]), k == 0, k == 7)
                t = mms(items, hall, wt, free)
                give_w(z, t)
                o = [cp("act", DA[0:64, 4 + j, :], ps[0:64, 0:S], t), cp("act", DA[64:128, 4 + j, :], ps[0:64, 0:S], t)]
                dst = V2 if j == 0 else IW
                o.append(cp("act", dst, ps[:, S:S + 128].rearrange("p (b n) -> p b n", b=2)[:, :, 0:n], t))
                Gb.give(bi, o)
                dd.append(o)
                yield
            yield from gemm(pairs(w_in, 19, 4), 8, rhs, hall, put_d(6))
            keys = ["dq"] * 4 + ["dk", "di"]
            nd = yield from head_rs(DA, 6, 1.0 / 64, 1e-6, dd, lambda t0, m, ps3, tok: [
                stt("dve", DA[:, t, :], DA[:, t, :], vec(keys[t], l), ps3[:, t - t0, :], MUL, MUL, tok) for t in range(t0, t0 + m)])
            cos2, sin2 = ROPE[:, 0:S], ROPE[:, S:2 * S]
            rp = []
            yield
            for p in (2, 3, 4, 0, 1):
                bi, ps, free = Ab.take()
                dv = DA[:, 2 * p:2 * p + 2, :]
                t = mms([(ps[:, :], ROT64, dv.rearrange("p t s -> p (t s)"), True, True)], nd, dd, free)
                a = tt("pool", dv, dv, bc(cos2, 2), MUL, t, t_rope)
                si, s, sf = Scr.take()
                s3 = s.rearrange("p (t s) -> p t s", s=S)
                b = tt("dve", s3, ps[:, :].rearrange("p (t s) -> p t s", s=S), bc(sin2, 2), MUL, t, sf, t_rope)
                Ab.give(bi, b)
                rp.append(tt("pool", dv, dv, s3, ADD, a, b))
                Scr.give(si, rp[-1])
                yield
            nks = (128, 256)
            acc = [None, None]
            for b in range(2):
                nk, b0 = nks[b], 128 * b
                for p in range(4):
                    si, s, sf = Scr.take()
                    s3 = s[:, 0:2 * nk].rearrange("p (e s) -> p e s", e=2)
                    a = []
                    for e in range(2):
                        bi, ps, free = Ab.take()
                        r = slice(64 * e, 64 * e + 64)
                        t = mms([(ps[:, 0:nk], DA[r, 6 + p, b * 128:(b + 1) * 128], DA[r, 5, 0:nk], True, True)], rp, free)
                        a.append(act(s3[:, e, :], ps[:, 0:nk], ACT.Relu, t, sf, scale=0.125))
                        Ab.give(bi, a[-1])
                    for e in range(2):
                        w = IW[:, b, 2 * p + e:2 * p + e + 1]
                        if p == 0 and e == 0:
                            acc[b] = ts("dve", SCO[:, b0:b0 + nk], s3[:, e, :], w, None, MUL, None, a, dd)
                        else:
                            acc[b] = stt("dve", SCO[:, b0:b0 + nk], s3[:, e, :], w, SCO[:, b0:b0 + nk], MUL, ADD, a, acc[b])
                    Scr.give(si, acc[b])
                    yield
                a = ts("dve", SCO[:, b0:b0 + nk], SCO[:, b0:b0 + nk], float(8 ** -0.5), None, MUL, None, acc[b])
                m0 = 64 if b == 0 else 192
                a = P.put("dve", lambda e, b0=b0, m0=m0: e.memset(SCO[0:64, b0 + m0:b0 + m0 + 64], -1e30), a)
                for it in range(8):
                    src = SCO if it == 0 else WKX
                    xi, m8, mf = Stat8.take()
                    c = P.put("dve", lambda e, o=m8, i=src[:, b0:b0 + nk]: e.max(o, i), a, mf)
                    a = P.put("dve", lambda e, o=WKX[:, b0:b0 + nk], r=m8, i=src[:, b0:b0 + nk]: e.match_replace(o, r, i, -3e38), c)
                    Stat8.give(xi, a)
                    yield
                a = ts("dve", PEN[:, b0:b0 + nk], WKX[:, b0:b0 + nk], -3e38, -1e30, ALU.is_gt, MUL, a)
                a = P.put("dve", lambda e, b0=b0, m0=m0: e.memset(PEN[0:64, b0 + m0:b0 + m0 + 64], -1e30), a)
                acc[b] = a
            yield from attention(8, lambda h: DA[64 * (h % 2):64 * (h % 2) + 64, h // 2, :],
                                 lambda h: DA[64 * (h % 2):64 * (h % 2) + 64, 4, :], 0.125,
                                 lambda h, kt: V2[:, kt, :], lambda h: O[64 * (h % 2):64 * (h % 2) + 64, h // 2, :], 64,
                                 [rp, acc], nks=nks, pen=lambda b: PEN[:, 128 * b:128 * b + nks[b]], done=odone)

        def gate_gemm():
            def put_gate(n, ps, tok):
                a = act(GT[:, 2 * n:2 * n + 2, :].rearrange("p t s -> p (t s)"), ps[:, :], ACT.Tanh, tok, scale=0.5)
                gates.append(a)
                return a
            yield from gemm(pairs(w_in, 24, 16), 8, rhs, hall, put_gate)

        gate = gate_gemm()

        def fill(n):
            for _ in range(n):
                if next(gate, "end") == "end":
                    break
                yield
            yield
        interleave([rwkv(), sparse()], WT2)
        kept["os"] = split(Os, O, [odone, kept["gfree"]])
        M = big(0, 8, S)
        M2 = big2(2048, 8, S)
        mt = {}

        def branch(first, b, src, W, dep, free):
            def put_m(n, ps, tok):
                mv = M[:, 2 * n:2 * n + 2, :].rearrange("p t s -> p (t s)")
                gv = GT[:, 8 * b + 2 * n:8 * b + 2 * n + 2, :].rearrange("p t s -> p (t s)")
                if first:
                    mt[n] = stt("dve", mv, gv, 1.0, ps[:, :], ADD, MUL, tok, gates, free)
                    return mt[n]
                si, s, sf = Scr.take()
                a = stt("dve", s, gv, 1.0, ps[:, :], ADD, MUL, tok, gates, sf)
                c = tt("dve", mv, mv, s, ADD, a, mt[n])
                Scr.give(si, c)
                mt[n] = split([x[:, 2 * n:2 * n + 2, :] for x in M2], M[:, 2 * n:2 * n + 2, :], [c, free], eng="dve" if n % 2 else "pool")
                return a
            yield from gemm(pairs(ins[W][l], 0, 8), 4, lambda k: (src[0][:, k, :], src[1][:, k, :]), dep, put_m)

        def filler():
            yield from gate
            yield from branch(True, 1, Os, "w_branch_b_2", kept["os"], kept["gfree"])
        MT = big(9984, 8, S)
        t_m = P.dma("mem", MT.rearrange("p t s -> p (t s)"), ins["memT"], kept["gfree"], eng="act")

        def memory():
            mh.clear()
            mh.update((yield from rmsnorm(MT, 8, "mtok", l, MH, [t_m], wfree=[odone, kept["gfree"], kept["os"]])))
        interleave([tail(), filler(), memory()], WT3)
        yield from branch(False, 0, YAs, "w_branch_a_2", ya, ya)
        xnew.clear()
        yield from gemm(pairs(ins["w_out_2"][l], 0, 8), 8, lambda k: (M2[0][:, k, :], M2[1][:, k, :]), {k: mt[k // 2] for k in range(8)},
                        lambda n, ps, tok: add_x(n, ps, tok, 0.5))
        xdep[:] = list(xnew)

    def block2_mem(l):
        Q, K = big(6144, 4, S), big(7168, 4, S)
        V = big(8192, 2, 512)
        O = big(9216, 4, S)
        Os = big2(10240, 4, S)
        W = ins["mem_wkv_2"][l]
        snap = P.now()
        mem = lambda k: (MH[0][:, k, :], MH[1][:, k, :])
        mall = list(mh.values())
        got = {}
        qd, kd, vd = [], [], []

        def put_to(dst, lst):
            def f(n, ps, tok):
                a = cp("act", dst[:, 2 * n:2 * n + 2, :].rearrange("p t s -> p (t s)"), ps[:, :], tok)
                lst.append(a)
                return a
            return f

        def normed(src, key, dep):
            return (yield from head_rs(src, 4, 1.0 / 128, 1e-6, dep, lambda t0, m, ps3, tok: [
                stt("dve", src[:, t, :], src[:, t, :], vec(key, l), ps3[:, t - t0, :], MUL, MUL, tok) for t in range(t0, t0 + m)], heads=1))
        bks = [Gb.take() for _ in range(2)]
        tks = [None, None]
        nd = []

        def values(g0, g1):
            for g in range(g0, g1):
                z, hi, lo, wt = take_w(*unit(W, 4 + g, 1, 0, 8))
                for tb in range(2):
                    items = []
                    for k in range(8):
                        c = slice(k * 128, (k + 1) * 128)
                        items += products(bks[tb][1][:, g * 128:(g + 1) * 128], [x[:, tb * 128:(tb + 1) * 128] for x in mem(k)],
                                          (hi[:, c], lo[:, c]), k == 0, k == 7)
                    tks[tb] = mms(items, mall, wt, bks[tb][2])
                give_w(z, tks)
                yield

        def first():
            yield from gemm(pairs(W, 0, 4), 8, mem, mall, put_to(K, kd))
            yield from values(0, 3)

        def norm():
            got["h"] = yield from rmsnorm(x3, 8, "nmem", l, h2, list(xdep), wfree=snap, sums=xs[0])
        P.barrier(snap)
        interleave([first(), norm()], IWM)
        hd = got["h"]
        yield from gemm(pairs(ins["mem_wq_2"][l], 0, 4), 8, lambda k: (h2[0][:, k, :], h2[1][:, k, :]), hd, put_to(Q, qd))

        def both():
            nd.append((yield from normed(K, "mk", kd)))
            nd.append((yield from normed(Q, "mq", qd)))
        interleave([both(), values(3, 4)], [1.0, 4.0])
        for tb in range(2):
            a = cp("act", V[:, tb, :], bks[tb][1][:, :], tks[tb])
            Gb.give(bks[tb][0], a)
            vd.append(a)
        yield
        od = []
        yield from attention(4, lambda h: Q[:, h, :], lambda h: K[:, h, :], 128 ** -0.5, lambda h, kt: V[:, kt, h * 128:(h + 1) * 128],
                             lambda h: O[:, h, :], 128, [nd, vd], done=od)
        os = [split([x[:, 2 * n:2 * n + 2, :] for x in Os], O[:, 2 * n:2 * n + 2, :], od[2 * n:2 * n + 2], eng="dve") for n in range(2)]
        xnew.clear()
        yield from gemm(pairs(ins["mem_wo_2"][l], 0, 8), 4, lambda k: (Os[0][:, k, :], Os[1][:, k, :]), {k: os[k // 2] for k in range(4)}, add_x)
        xdep[:] = list(xnew)

    def block2_ffn():
        hd = yield from start("nffn", 0)
        F2 = big2(0, 22, S)
        fd = yield from ffn_up(ins["ffn_wg_2"][0], ins["ffn_wu_2"][0], 22, F2, hd, None)
        xnew.clear()
        yield from gemm(pairs(ins["ffn_wd_2"][0], 0, 8), 22, lambda k: (F2[0][:, k, :], F2[1][:, k, :]), fd, add_x)
        xdep[:] = list(xnew)

    def block2_moe():
        hd = yield from start("nffn", 1)
        RT = big(0, 8, 8)
        BI = big(64, 8)
        LG = big(72, 2, 8)
        GT = big(88, 2, 8)
        M8 = big(104, 2, 8)
        IX = big(120, 2, 8)
        IXF = big(136, 2, 8)
        E2 = big(152, 2, 8)
        DGm = big(256, 2, 128)
        GB = big(512, 8, S)
        RTs = big2(13824, 8, 8)
        Fs = [big2(2560, 11, S), big2(8192, 11, S)]
        t_r = [P.dma("rt", RT, ins["moe_router_2"][0].rearrange("(k p) n -> p k n", p=128), P.snap, eng="act"),
               P.dma("rb", BI, ins["moe_bias_2"][0].partition_broadcast(128), P.snap, eng="act")]
        rt = split(RTs, RT, t_r)
        hall = list(hd.values())
        gb = []

        def routing():
            bi, ps, free = Ab.take()
            items = []
            for b in range(2):
                for k in range(8):
                    items += products(ps[:, 8 * b:8 * b + 8], [x[:, k, b * 128:(b + 1) * 128] for x in h2], [x[:, k, :] for x in RTs], k == 0, k == 7)
            t = mms(items, hall, rt, free)
            a = tt("dve", LG, ps[:, 0:16].rearrange("p (b n) -> p b n", b=2), bc(BI, 2), ADD, t, t_r)
            Ab.give(bi, a)
            gts = []
            yield
            for b in range(2):
                m = P.put("dve", lambda e, b=b: e.max(M8[:, b, :], LG[:, b, :]), a)
                i = P.put("dve", lambda e, b=b: e.max_index(IX[:, b, :].bitcast(U32), M8[:, b, :], LG[:, b, :]), m)
                i = cp("dve", IXF[:, b, :], IX[:, b, :].bitcast(U32), i)
                d = tt("dve", E2[:, b, 0:1], M8[:, b, 1:2], M8[:, b, 0:1], SUB, m)
                d = act(E2[:, b, 0:1], E2[:, b, 0:1], ACT.Exp, d)
                s = ts("dve", E2[:, b, 1:2], E2[:, b, 0:1], 1.0, None, ADD, None, d)
                s = P.put("dve", lambda e, b=b: e.reciprocal(E2[:, b, 2:3], E2[:, b, 1:2]), s)
                s = tt("dve", E2[:, b, 3:4], E2[:, b, 0:1], E2[:, b, 2:3], MUL, s)
                g1 = ts("dve", GT[:, b, :], IOTA8, IXF[:, b, 0:1], E2[:, b, 2:3], ALU.is_equal, MUL, s, i)
                g2 = ts("dve", M8[:, b, :], IOTA8, IXF[:, b, 1:2], E2[:, b, 3:4], ALU.is_equal, MUL, g1)
                gts.append(tt("dve", GT[:, b, :], GT[:, b, :], M8[:, b, :], ADD, g2))
            yield 3
            dfree = None
            for e8 in range(8):
                dg = [ts("dve", DGm[:, b, :], IDENT, GT[:, b, e8:e8 + 1], None, MUL, None, gts, dfree) for b in range(2)]
                bi, ps, free = Ab.take()
                t = mms([(ps[:, b * 128:(b + 1) * 128], ONES, DGm[:, b, :], True, True) for b in range(2)], dg, free)
                dfree = t
                gb.append(cp("act", GB[:, e8, :], ps[:, 0:S], t))
                Ab.give(bi, gb[-1])
                yield 0.5

        xnew.clear()
        xl = {}
        ff = [None, None]

        def up(e8):
            z = e8 % 2
            fds[e8] = yield from ffn_up(ins["moe_wg_2"][0][e8], ins["moe_wu_2"][0][e8], 11, Fs[z], hd, [gb, ff[z]] if e8 else None,
                                        gate=GB[:, e8, :] if e8 else None)

        def down(e8):
            z = e8 % 2

            def put_x(n, ps, tok):
                v = x3[:, 2 * n:2 * n + 2, :].rearrange("p t s -> p (t s)")
                ff[z] = tok
                if e8:
                    xl[n] = tt("dve", v, ps[:, :], v, ADD, tok, xl.get(n), hall)
                    return xl[n]
                si, s, sf = Scr.take()
                a = tt("dve", s.rearrange("p (t s) -> p t s", s=S), ps[:, :].rearrange("p (t s) -> p t s", s=S), bc(GB[:, 0, :], 2), MUL, tok, gb, sf)
                xl[n] = tt("pool", v, s, v, ADD, a, hall)
                Scr.give(si, xl[n])
                return a
            yield from gemm(pairs(ins["moe_wd_2"][0][e8], 0, 8), 11, lambda k: (Fs[z][0][:, k, :], Fs[z][1][:, k, :]), fds[e8], put_x)
        fds = {}
        ahead = up(0)
        interleave([ahead, routing()], [1.0, RW])
        for e8 in range(8):
            yield from ahead
            if e8 < 7:
                ahead = up(e8 + 1)
                next(ahead)
                yield
            yield from down(e8)
        xdep[:] = list(xl.values())

    Stat8 = Ring([S8[:, i * 8:(i + 1) * 8] for i in range(4)])

    phases = [lambda: block1_mix(0), lambda: block1_ffn(0), lambda: block1_mix(1), lambda: block1_ffn(1),
              lambda: block2_mix(0), lambda: block2_mem(0), block2_ffn, lambda: block2_mix(1), lambda: block2_mem(1), block2_moe]
    for ph in phases[ins.get("first", 0):ins.get("last", len(phases))]:
        run(ph())
    t_out = [P.dma(f"out{i}", out[:, i * 512:(i + 1) * 512], X[:, i * 512:(i + 1) * 512], xdep[i]) for i in range(4)]
    for c, (ph, pl) in enumerate(places[loaded[0]:]):
        P.fill(ph, lambda e, c=c: e.activation(IDLE[:, 2 * c:2 * c + 1], CST[:, 0:1], ACT.Copy), t_cst)
        P.fill(pl, lambda e, c=c: e.memset(IDLE[:, 2 * c + 1:2 * c + 2], 0.0))

    with nc.Block() as block:
        @block.tensor
        def _(e):
            P.replay("pe", e)

        @block.scalar
        def _(e):
            P.replay("act", e)

        @block.vector
        def _(e):
            P.replay("dve", e)

        @block.gpsimd
        def _(e):
            P.replay("pool", e)

        @block.sync
        def _(e):
            P.replay("sp", e)
            for sem, val in t_out:
                e.wait_ge(P.sem[sem], val)


def constants():
    c = np.zeros((128, NCST), np.float32)
    i = np.arange(128)
    c[:, 0:128] = np.eye(128)
    c[:, 128:256] = 1.0
    c[:, 256:384] = (i[:, None] // 64) == (i[None, :] // 64)
    for m in range(64, 96):
        if m < 80:
            c[m + 16, 384 + m] = -1.0
        else:
            c[m - 16, 384 + m] = 1.0
    for m in range(128):
        if m % 64 < 32:
            c[m + 32, 512 + m] = -1.0
        else:
            c[m - 32, 512 + m] = 1.0
    t, j = i[:, None], i[None, :]
    low = t > j
    c[:, 640:768] = low & (t // 16 == j // 16)
    c[:, 768:896] = (low & (t // 16 == j // 16)).T
    c[:, 896:1024] = low & (t // 32 == j // 32) & (t // 16 != j // 16)
    c[:, 1024:1152] = low & (t // 64 == j // 64) & (t // 32 != j // 32)
    c[:, 1152:1280] = low & (t // 64 == j // 64)
    strict = ((t < j) & (t // 64 == j // 64)).astype(np.float32)
    incl = ((t <= j) & (t // 64 == j // 64)).astype(np.float32)
    c[:, 1280:1536] = np.concatenate([strict, incl], 1)
    c[:, 1536:1792] = (np.arange(256) % 64 != 0)[None, :]
    c[:, 1792:1856] = np.tile(np.eye(64), (2, 1))
    c[:, 1856:1864] = np.arange(8)[None, :]
    f1 = np.array(INV1, np.uint32).view(np.float32)
    f2 = np.array(INV2, np.uint32).view(np.float32)
    c[:, 1864] = f1[i % 16]
    c[:, 1865] = f2[i % 32]
    return c


INV1 = [0x3f800000, 0x3f0ff59a, 0x3ea1e89b, 0x3e361887, 0x3dcccccd, 0x3d6655c3, 0x3d0186e2, 0x3c91ad39, 0x3c23d70a, 0x3bb8449c,
        0x3b4f3e37, 0x3ae91528, 0x3a83126f, 0x3a136a16, 0x39a5cb5f, 0x393a7753]
INV2 = [0x3f800000, 0x3f3ff911, 0x3f0ff59a, 0x3ed7e89b, 0x3ea1e89b, 0x3e72d423, 0x3e361887, 0x3e088d77, 0x3dcccccd, 0x3d99940d,
        0x3d6655c2, 0x3d2cba15, 0x3d0186e3, 0x3cc2434f, 0x3c91ad39, 0x3c5a7bf2, 0x3c23d70a, 0x3bf5b9b0, 0x3bb8449c, 0x3b8a2e77,
        0x3b4f3e38, 0x3b1b690d, 0x3ae91528, 0x3aaec98e, 0x3a83126f, 0x3a44948c, 0x3a136a16, 0x39dd1725, 0x39a5cb60, 0x3978a815,
        0x393a7753, 0x390bd472]


def pack_vectors(inputs):
    cols = []
    for l in range(2):
        for key, name, n in VECS1 + VECS2:
            a = np.asarray(inputs[name])
            if key == "v0":
                a = a[0]
            else:
                a = a[l]
            a = a.reshape(-1)
            if a.size == 64:
                a = np.concatenate([a, a])
            if key == "mu":
                z = np.zeros(64, a.dtype)
                a = np.concatenate([a[0:1536], a[1536:1600], z, a[1600:1664], z, a[1664:1792]])
            assert a.size == 128 * n, name
            cols.append(a.reshape(n, 128).T)
    return np.ascontiguousarray(np.concatenate(cols, 1))


_WHOLE = ["positions", "positions_2", "gm_ln_g", "gm_ln_b", "gm_bs", "rwkv_w2_2", "rwkv_a2_2", "rwkv_g2_2", "rwkv_v1_2",
          "rwkv_v2_2", "moe_router_2", "moe_bias_2"]
_BLOCKED = ["w_o_mla", "w_o_sc", "w_o_cf", "w_o_gm", "w_out", "w_ffn_out", "w_branch_a_2", "w_branch_b_2", "w_out_2",
            "mem_wq_2", "mem_wkv_2", "mem_wo_2", "ffn_wg_2", "ffn_wu_2", "ffn_wd_2", "moe_wg_2", "moe_wu_2", "moe_wd_2"]


def blocks(a):
    lead, (k, n) = a.shape[:-2], a.shape[-2:]
    b = a.reshape(*lead, k // 128, 128, n // 128, 128)
    m = len(lead)
    return np.ascontiguousarray(b.transpose(*range(m), m + 2, m + 1, m, m + 3)).reshape(*lead, n // 128, 128, k)


def padded(a, left, width):
    r = np.zeros((*a.shape[:-1], width), a.dtype)
    r[..., left:left + a.shape[-1]] = a
    return r


def by_features(a):
    return np.ascontiguousarray(a.T.reshape(8, 128, 256).transpose(1, 0, 2).reshape(128, 2048))


def lay_out(inputs):
    arrays = {k: np.ascontiguousarray(inputs[k]) for k in _WHOLE}
    for k in ("positions", "positions_2"):
        arrays[k] = arrays[k].reshape(256)
    arrays["xT"] = by_features(np.asarray(inputs["x"])[0])
    arrays["memT"] = by_features(np.asarray(inputs["mem_2"])[0])
    arrays["gm_wsT"] = np.ascontiguousarray(np.asarray(inputs["gm_ws"]).transpose(0, 3, 1, 2).reshape(2, 128, 512))
    for k in _BLOCKED:
        arrays[k] = blocks(np.asarray(inputs[k]))
    w = np.asarray(inputs["w_in"])
    arrays["w_in_a"] = blocks(w[:, :, 0:512])
    arrays["w_kr"] = blocks(padded(w[:, :, 512:544], 64, 128))
    arrays["w_in_b"] = blocks(w[:, :, 544:8224])
    w = np.asarray(inputs["w_uq"]).reshape(2, 256, 8, 96)
    arrays["w_uq"] = blocks(padded(w, 0, 128).reshape(2, 256, 1024))
    arrays["w_ukv"] = blocks(np.asarray(inputs["w_ukv"]))
    w = np.asarray(inputs["w_ffn_in"])
    arrays["w_ffn_g"], arrays["w_ffn_u"] = blocks(w[:, :, 0:2816]), blocks(w[:, :, 2816:5632])
    w = np.asarray(inputs["w_in_2"])
    arrays["w_in_2"] = blocks(np.concatenate([w[:, :, 0:2944], padded(w[:, :, 2944:3016], 0, 128), w[:, :, 3016:5064]], 2))
    arrays["vecs"] = pack_vectors(inputs)
    arrays["cst"] = constants()
    return arrays


def kernel(**inputs):
    import concourse.bacc as bacc
    from concourse.bass_utils import run_bass_kernel_spmd

    nc = bacc.Bacc("TRN2", target_bir_lowering=False, num_devices=1, dynamic_dma_scratch_size=1024)
    arrays = lay_out(inputs)
    ins = {k: nc.dram_tensor("in_" + k, a.shape, mybir.dt.from_np(a.dtype), kind="ExternalInput").ap() for k, a in arrays.items()}
    out = nc.dram_tensor("out_x", (128, 2048), F32, kind="ExternalOutput").ap()
    build_program(nc, ins, out)
    r = run_bass_kernel_spmd(nc, [{"in_" + k: a for k, a in arrays.items()}], core_ids=[0])
    y = r.results[0]["out_x"].reshape(128, 8, 256)
    return np.ascontiguousarray(y.transpose(2, 1, 0).reshape(1, 256, 1024))
```
